# Optimizing a Trainium2 kernel written in Bass

```python
import jax, jax.numpy as jnp
from jax import lax
import numpy as np
import math

D_MODEL = 1024
BATCH = 1
SEQ = 256
DEPTH = 4

N_MIXERS = 3
GRID_W = 64
D_FF = 2816
NORM_EPS = 1e-6
HG_HEADS = 8
HG_DK = D_MODEL // HG_HEADS
HG_DV = D_MODEL // HG_HEADS
HG_CHUNK = 16
NA_HEADS = 16
NA_HEAD_DIM = D_MODEL // NA_HEADS
NA_WIN_R = 8
NA_WIN_C = 16
MLA_HEADS = 16
MLA_Q_LORA = 768
MLA_KV_LORA = 256
MLA_NOPE = 64
MLA_ROPE = 32
MLA_V = 64
ROPE_THETA = 10000.0
Q_BLOCK = 128
N_A = (DEPTH + 2) // 3
N_B = (DEPTH + 1) // 3
N_C = DEPTH // 3
NEG_INF = -1e30


def _rms_norm(x, g):
    xf = x.astype(jnp.float32)
    y = xf * lax.rsqrt(jnp.mean(xf * xf, axis=-1, keepdims=True) + NORM_EPS)
    return (y * g.astype(jnp.float32)).astype(x.dtype)

def _swiglu(x, w_gu, w_down):
    g, u = jnp.split(x @ w_gu, 2, axis=-1)
    return (jax.nn.silu(g) * u) @ w_down

def _rope(x, pos):
    half = x.shape[-1] // 2
    inv_freq = ROPE_THETA ** (-jnp.arange(half, dtype=jnp.float32) / half)
    ang = pos.astype(jnp.float32)[:, None] * inv_freq[None, :]
    cos = jnp.cos(ang)[:, None, :]
    sin = jnp.sin(ang)[:, None, :]
    xf = x.astype(jnp.float32)
    x1, x2 = xf[..., :half], xf[..., half:]
    return jnp.concatenate([x1 * cos - x2 * sin, x2 * cos + x1 * sin], axis=-1).astype(x.dtype)

def _gla_chunk_scan(q, k, v, logf):
    H, T, dk = q.shape
    dv = v.shape[-1]
    n = T // HG_CHUNK
    q = q.reshape(H, n, HG_CHUNK, dk)
    k = k.reshape(H, n, HG_CHUNK, dk)
    v = v.reshape(H, n, HG_CHUNK, dv)
    b = jnp.cumsum(logf.reshape(H, n, HG_CHUNK, dk), axis=2)
    tri = np.tril(np.ones((HG_CHUNK, HG_CHUNK), dtype=bool))[:, :, None]
    diff = b[:, :, :, None, :] - b[:, :, None, :, :]
    decay = jnp.where(tri, jnp.exp(jnp.where(tri, diff, 0.0)), 0.0)
    attn = jnp.einsum('hntd,hntsd,hnsd->hnts', q, decay, k)
    o_intra = jnp.einsum('hnts,hnsv->hntv', attn, v)
    b_last = b[:, :, -1, :]
    q_inter = q * jnp.exp(b)
    k_inter = k * jnp.exp(b_last[:, :, None, :] - b)
    chunk_kv = jnp.einsum('hncd,hncv->hndv', k_inter, v)

    def step(state, inp):
        q_c, dl, kv_c = inp
        o_c = jnp.einsum('hcd,hdv->hcv', q_c, state)
        state = jnp.exp(dl)[..., None] * state + kv_c
        return state, o_c

    s0 = jnp.zeros((H, dk, dv), q.dtype)
    _, o_inter = lax.scan(step, s0, (q_inter.transpose(1, 0, 2, 3), b_last.transpose(1, 0, 2), chunk_kv.transpose(1, 0, 2, 3)))
    o = o_intra + o_inter.transpose(1, 0, 2, 3)
    return o.reshape(H, T, dv)

def _hgrn2_mixer(h, w_in, g_norm, w_out, lb):
    B, T, _ = h.shape
    q, zf, zb, i, g = jnp.split(h @ w_in, 5, axis=-1)

    def to_heads(t, d):
        return t.reshape(B, T, HG_HEADS, d).transpose(0, 2, 1, 3).astype(jnp.float32)

    lbh = lb.astype(jnp.float32).reshape(HG_HEADS, 1, HG_DK)
    log_lb = jnp.log(lbh)
    log_1m_lb = jnp.log1p(-lbh)

    def forget(z):
        logf = jnp.logaddexp(log_lb, log_1m_lb + jax.nn.log_sigmoid(to_heads(z, HG_DK)))
        return 1.0 - jnp.exp(logf), logf

    k_f, logf_f = forget(zf)
    k_b, logf_b = forget(zb)
    qh = to_heads(q, HG_DK) * (HG_DK ** -0.5)
    vh = to_heads(i, HG_DV)

    def per_seq(a):
        q_s, kf_s, lf_s, kb_s, lbw_s, v_s = a
        fwd = _gla_chunk_scan(q_s, kf_s, v_s, lf_s)
        bwd = _gla_chunk_scan(q_s[:, ::-1], kb_s[:, ::-1], v_s[:, ::-1], lbw_s[:, ::-1])[:, ::-1]
        return fwd + bwd

    o = lax.map(per_seq, (qh, k_f, logf_f, k_b, logf_b, vh))
    o = o.transpose(0, 2, 1, 3)
    gh = g.reshape(B, T, HG_HEADS, HG_DV).astype(jnp.float32)
    o = _rms_norm(o, g_norm) * jax.nn.silu(gh)
    return o.reshape(B, T, D_MODEL).astype(h.dtype) @ w_out

def _na_mixer(h, w_in, q_norm, k_norm, rpb, w_out):
    B, T, _ = h.shape
    rows = T // GRID_W
    win_r = min(NA_WIN_R, rows)
    q, k, v = jnp.split(h @ w_in, 3, axis=-1)
    shp = (B, rows, GRID_W, NA_HEADS, NA_HEAD_DIM)
    q = _rms_norm(q.reshape(shp), q_norm)
    k = _rms_norm(k.reshape(shp), k_norm)
    v = v.reshape(shp)
    cols = np.arange(GRID_W)
    col_start = np.clip(cols - NA_WIN_C // 2, 0, GRID_W - NA_WIN_C)
    col_mask = (cols[None, :] >= col_start[:, None]) & (cols[None, :] < col_start[:, None] + NA_WIN_C)
    col_off = np.clip(cols[None, :] - cols[:, None] + NA_WIN_C - 1, 0, 2 * NA_WIN_C - 2)
    rpb_cols = rpb.astype(jnp.float32)[:, :, col_off]
    scale = NA_HEAD_DIM ** -0.5

    def attend_row(r):
        r0 = jnp.clip(r - win_r // 2, 0, rows - win_r)
        q_r = lax.dynamic_index_in_dim(q, r, axis=1, keepdims=False)
        k_blk = lax.dynamic_slice_in_dim(k, r0, win_r, axis=1)
        v_blk = lax.dynamic_slice_in_dim(v, r0, win_r, axis=1)
        s = jnp.einsum('bqhd,brkhd->bhqrk', q_r, k_blk).astype(jnp.float32) * scale
        row_off = r0 + jnp.arange(win_r) - r + NA_WIN_R - 1
        bias = jnp.take(rpb_cols, row_off, axis=1).transpose(0, 2, 1, 3)
        s = jnp.where(col_mask[:, None, :], s + bias, NEG_INF)
        p = jax.nn.softmax(s.reshape(B, NA_HEADS, GRID_W, win_r * GRID_W), axis=-1)
        p = p.reshape(B, NA_HEADS, GRID_W, win_r, GRID_W).astype(v.dtype)
        return jnp.einsum('bhqrk,brkhd->bqhd', p, v_blk)

    o = lax.map(attend_row, jnp.arange(rows))
    o = o.transpose(1, 0, 2, 3, 4).reshape(B, T, D_MODEL)
    return o @ w_out

def _dense_attention_blocks(q, k, v):
    B, T, H, dqk = q.shape
    n_blk = T // Q_BLOCK
    scale = dqk ** -0.5
    q_blocks = q.reshape(B, n_blk, Q_BLOCK, H, dqk).transpose(1, 0, 2, 3, 4)

    def attend(q_b):
        s = jnp.einsum('bqhd,bkhd->bhqk', q_b, k).astype(jnp.float32) * scale
        p = jax.nn.softmax(s, axis=-1).astype(v.dtype)
        return jnp.einsum('bhqk,bkhd->bqhd', p, v)

    o = lax.map(attend, q_blocks)
    return o.transpose(1, 0, 2, 3, 4).reshape(B, T, H * v.shape[-1])

def _mla_mixer(h, w_in, q_a_norm, w_uq, kv_a_norm, w_ukv, q_norm, k_norm, w_out):
    B, T, _ = h.shape
    c = h @ w_in
    c_q = c[..., :MLA_Q_LORA]
    c_kv = c[..., MLA_Q_LORA:MLA_Q_LORA + MLA_KV_LORA]
    k_rope = c[..., MLA_Q_LORA + MLA_KV_LORA:]
    q = (_rms_norm(c_q, q_a_norm) @ w_uq).reshape(B, T, MLA_HEADS, MLA_NOPE + MLA_ROPE)
    kv = (_rms_norm(c_kv, kv_a_norm) @ w_ukv).reshape(B, T, MLA_HEADS, MLA_NOPE + MLA_V)
    k_rope = jnp.broadcast_to(k_rope[:, :, None, :], (B, T, MLA_HEADS, MLA_ROPE))
    k = jnp.concatenate([kv[..., :MLA_NOPE], k_rope], axis=-1)
    v = kv[..., MLA_NOPE:]
    q = _rms_norm(q, q_norm)
    k = _rms_norm(k, k_norm)
    pos = jnp.arange(T)
    q = jnp.concatenate([q[..., :MLA_NOPE], _rope(q[..., MLA_NOPE:], pos)], axis=-1)
    k = jnp.concatenate([k[..., :MLA_NOPE], _rope(k[..., MLA_NOPE:], pos)], axis=-1)
    return _dense_attention_blocks(q, k, v) @ w_out

def first_inputs(seed: int = 0) -> dict:
    key = jax.random.key(seed)
    ks = iter(jax.random.split(key, 32))

    def nrm(shape, scale):
        return jax.random.normal(next(ks), shape, jnp.float32) * scale

    def gain(shape):
        return 1.0 + nrm(shape, 0.02)

    D = D_MODEL
    qk_dim = MLA_NOPE + MLA_ROPE
    return {
        'x': nrm((BATCH, SEQ, D), 1.0),
        'ffn1_norm': gain((DEPTH, D)),
        'ffn1_w_gu': nrm((DEPTH, D, 2 * D_FF), D ** -0.5),
        'ffn1_w_down': nrm((DEPTH, D_FF, D), D_FF ** -0.5),
        'mix_norm': gain((DEPTH, D)),
        'ffn2_norm': gain((DEPTH, D)),
        'ffn2_w_gu': nrm((DEPTH, D, 2 * D_FF), D ** -0.5),
        'ffn2_w_down': nrm((DEPTH, D_FF, D), D_FF ** -0.5),
        'hg_lb_logits': nrm((DEPTH, HG_HEADS * HG_DK), 0.5),
        'hg_w_in': nrm((N_A, D, 5 * D), D ** -0.5),
        'hg_g_norm': gain((N_A, HG_DV)),
        'hg_w_out': nrm((N_A, D, D), D ** -0.5),
        'na_w_in': nrm((N_B, D, 3 * D), D ** -0.5),
        'na_q_norm': gain((N_B, NA_HEAD_DIM)),
        'na_k_norm': gain((N_B, NA_HEAD_DIM)),
        'na_rpb': nrm((N_B, NA_HEADS, 2 * NA_WIN_R - 1, 2 * NA_WIN_C - 1), 0.2),
        'na_w_out': nrm((N_B, D, D), D ** -0.5),
        'mla_w_in': nrm((N_C, D, MLA_Q_LORA + MLA_KV_LORA + MLA_ROPE), D ** -0.5),
        'mla_q_a_norm': gain((N_C, MLA_Q_LORA)),
        'mla_w_uq': nrm((N_C, MLA_Q_LORA, MLA_HEADS * qk_dim), MLA_Q_LORA ** -0.5),
        'mla_kv_a_norm': gain((N_C, MLA_KV_LORA)),
        'mla_w_ukv': nrm((N_C, MLA_KV_LORA, MLA_HEADS * (MLA_NOPE + MLA_V)), MLA_KV_LORA ** -0.5),
        'mla_q_norm': gain((N_C, qk_dim)),
        'mla_k_norm': gain((N_C, qk_dim)),
        'mla_w_out': nrm((N_C, MLA_HEADS * MLA_V, D), (MLA_HEADS * MLA_V) ** -0.5),
    }

def first_block(x, ffn1_norm, ffn1_w_gu, ffn1_w_down, mix_norm, ffn2_norm, ffn2_w_gu, ffn2_w_down,
              hg_lb_logits, hg_w_in, hg_g_norm, hg_w_out,
              na_w_in, na_q_norm, na_k_norm, na_rpb, na_w_out,
              mla_w_in, mla_q_a_norm, mla_w_uq, mla_kv_a_norm, mla_w_ukv, mla_q_norm, mla_k_norm, mla_w_out):
    gam = jnp.cumsum(jax.nn.softmax(hg_lb_logits.astype(jnp.float32), axis=0), axis=0)
    lb_all = gam - gam[0:1]
    ia = ib = ic = 0
    for layer in range(DEPTH):
        x = x + 0.5 * _swiglu(_rms_norm(x, ffn1_norm[layer]), ffn1_w_gu[layer], ffn1_w_down[layer])
        h = _rms_norm(x, mix_norm[layer])
        kind = layer % N_MIXERS
        if kind == 0:
            y = _hgrn2_mixer(h, hg_w_in[ia], hg_g_norm[ia], hg_w_out[ia], lb_all[layer])
            ia += 1
        elif kind == 1:
            y = _na_mixer(h, na_w_in[ib], na_q_norm[ib], na_k_norm[ib], na_rpb[ib], na_w_out[ib])
            ib += 1
        else:
            y = _mla_mixer(h, mla_w_in[ic], mla_q_a_norm[ic], mla_w_uq[ic], mla_kv_a_norm[ic], mla_w_ukv[ic],
                           mla_q_norm[ic], mla_k_norm[ic], mla_w_out[ic])
            ic += 1
        x = x + y
        x = x + 0.5 * _swiglu(_rms_norm(x, ffn2_norm[layer]), ffn2_w_gu[layer], ffn2_w_down[layer])
    return x


DEPTH_2 = 2

HEAD_DIM = 64
CONV_CH = 256
CONV_K = 31
SC_CH = 256
SC_K = 3
SWA_Q_HEADS = 4
SWA_KV_HEADS = 2
WINDOW = 128
BLOCK = 128
FOX_HEADS = 4
N_BUCKETS = 32
MAX_DISTANCE = 128
N_BRANCH = 4
EPS = 1e-6
NEG_INF_2 = -1e30

SWA_COLS = (SWA_Q_HEADS + 2 * SWA_KV_HEADS) * HEAD_DIM
FOX_COLS = 3 * FOX_HEADS * HEAD_DIM + FOX_HEADS
_SIZES = (CONV_CH, CONV_CH,
          SC_CH, SC_CH, SC_CH,
          SWA_Q_HEADS * HEAD_DIM, SWA_KV_HEADS * HEAD_DIM, SWA_KV_HEADS * HEAD_DIM,
          FOX_HEADS * HEAD_DIM, FOX_HEADS * HEAD_DIM, FOX_HEADS * HEAD_DIM, FOX_HEADS,
          N_BRANCH * D_MODEL)
SPLITS = tuple(int(s) for s in np.cumsum(_SIZES)[:-1])
IN_COLS = int(sum(_SIZES))


def _rmsnorm(x, g):
    xf = x.astype(jnp.float32)
    y = xf * lax.rsqrt(jnp.mean(xf * xf, axis=-1, keepdims=True) + EPS)
    return (y * g.astype(jnp.float32)).astype(x.dtype)

def _layernorm(x, g, b):
    xf = x.astype(jnp.float32)
    mu = jnp.mean(xf, axis=-1, keepdims=True)
    var = jnp.mean(jnp.square(xf - mu), axis=-1, keepdims=True)
    y = (xf - mu) * lax.rsqrt(var + EPS)
    return (y * g.astype(jnp.float32) + b.astype(jnp.float32)).astype(x.dtype)

def _swiglu_2(x, w_gate, w_up, w_down):
    return (jax.nn.silu(x @ w_gate) * (x @ w_up)) @ w_down

def _causal_depthwise_conv(x, w):
    k = w.shape[0]
    return lax.conv_general_dilated(
        x, w[:, None, :].astype(x.dtype), window_strides=(1,), padding=[(k - 1, 0)],
        dimension_numbers=("NWC", "WIO", "NWC"), feature_group_count=x.shape[-1])

def _t5_bucket(dist):
    max_exact = N_BUCKETS // 2
    d = jnp.maximum(dist, 1).astype(jnp.float32)
    large = max_exact + (jnp.log(d / max_exact) / math.log(MAX_DISTANCE / max_exact)
                         * (N_BUCKETS - max_exact)).astype(jnp.int32)
    large = jnp.minimum(large, N_BUCKETS - 1)
    return jnp.where(dist < max_exact, dist, large)

def _sliding_window_attention(q, k, v, sink, rel_bias):
    b, t, hq, dh = q.shape
    hkv = k.shape[2]
    grp = hq // hkv
    nb = t // BLOCK
    qb = q.reshape(b, nb, BLOCK, hkv, grp, dh)
    kb = k.reshape(b, nb, BLOCK, hkv, dh)
    vb = v.reshape(b, nb, BLOCK, hkv, dh)
    pad = ((0, 0), (1, 0), (0, 0), (0, 0), (0, 0))
    kk = jnp.concatenate([jnp.pad(kb, pad)[:, :-1], kb], axis=2)
    vv = jnp.concatenate([jnp.pad(vb, pad)[:, :-1], vb], axis=2)
    s = jnp.einsum("bnqhgd,bnkhd->bnhgqk", qb, kk,
                   preferred_element_type=jnp.float32) * (dh ** -0.5)
    qi = jnp.arange(BLOCK)[:, None] + BLOCK
    ki = jnp.arange(2 * BLOCK)[None, :]
    dist = qi - ki
    local_ok = (dist >= 0) & (dist < WINDOW)
    blk_ok = (jnp.arange(nb)[:, None, None] > 0) | (ki[None] >= BLOCK)
    mask = local_ok[None] & blk_ok
    bias = rel_bias[_t5_bucket(jnp.maximum(dist, 0))]
    bias = bias.transpose(2, 0, 1).reshape(hkv, grp, BLOCK, 2 * BLOCK).astype(jnp.float32)
    s = jnp.where(mask[None, :, None, None], s + bias, NEG_INF_2)
    sk = sink.astype(jnp.float32).reshape(hkv, grp)[:, :, None, None]
    m = jnp.maximum(jnp.max(s, axis=-1, keepdims=True), sk)
    p = jnp.exp(s - m)
    p = p / (jnp.sum(p, axis=-1, keepdims=True) + jnp.exp(sk - m))
    o = jnp.einsum("bnhgqk,bnkhd->bnqhgd", p.astype(v.dtype), vv)
    return o.reshape(b, t, hq * dh)

def _forgetting_attention(q, k, v, log_f):
    b, t, h, dh = q.shape
    nb = t // BLOCK
    cum = jnp.cumsum(log_f, axis=1)
    cum_k = cum.transpose(0, 2, 1)
    qb = q.reshape(b, nb, BLOCK, h, dh).transpose(1, 0, 2, 3, 4)
    cq = cum.reshape(b, nb, BLOCK, h).transpose(1, 0, 3, 2)
    kpos = jnp.arange(t)

    def one_block(args):
        q_blk, c_blk, bi = args
        s = jnp.einsum("bqhd,bkhd->bhqk", q_blk, k,
                       preferred_element_type=jnp.float32) * (dh ** -0.5)
        s = s + (c_blk[..., :, None] - cum_k[:, :, None, :])
        qpos = bi * BLOCK + jnp.arange(BLOCK)
        s = jnp.where(kpos[None, :] <= qpos[:, None], s, NEG_INF_2)
        p = jax.nn.softmax(s, axis=-1)
        return jnp.einsum("bhqk,bkhd->bqhd", p.astype(v.dtype), v)

    o = lax.map(one_block, (qb, cq, jnp.arange(nb)))
    return o.transpose(1, 0, 2, 3, 4).reshape(b, t, h * dh)

def _normal(k, shape, scale):
    return scale * jax.random.normal(k, shape, jnp.float32)

def second_inputs(seed: int = 0) -> dict:
    key = jax.random.key(seed)
    ks = jax.random.split(key, 32)
    L, D = DEPTH_2, D_MODEL
    return {
        "x": _normal(ks[0], (BATCH, SEQ, D), 1.0),
        "rel_bias": _normal(ks[1], (N_BUCKETS, SWA_Q_HEADS), 0.5),
        "ffn1_norm": 1.0 + _normal(ks[2], (L, D), 0.05),
        "ffn1_w_gate": _normal(ks[3], (L, D, D_FF), D ** -0.5),
        "ffn1_w_up": _normal(ks[4], (L, D, D_FF), D ** -0.5),
        "ffn1_w_down": _normal(ks[5], (L, D_FF, D), D_FF ** -0.5),
        "mix_norm": 1.0 + _normal(ks[6], (L, D), 0.05),
        "w_in": _normal(ks[7], (L, D, IN_COLS), D ** -0.5),
        "b_forget": 3.0 + _normal(ks[8], (L, FOX_HEADS), 0.5),
        "conf_dw": _normal(ks[9], (L, CONV_K, CONV_CH), CONV_K ** -0.5),
        "conf_dw_b": _normal(ks[10], (L, CONV_CH), 0.02),
        "conf_ln_g": 1.0 + _normal(ks[11], (L, CONV_CH), 0.05),
        "conf_ln_b": _normal(ks[12], (L, CONV_CH), 0.02),
        "conf_w_out": _normal(ks[13], (L, CONV_CH, D), CONV_CH ** -0.5),
        "sc_conv": _normal(ks[14], (L, SC_K, SC_CH), SC_K ** -0.5),
        "sc_w_out": _normal(ks[15], (L, SC_CH, D), SC_CH ** -0.5),
        "swa_q_norm": 1.0 + _normal(ks[16], (L, HEAD_DIM), 0.05),
        "swa_k_norm": 1.0 + _normal(ks[17], (L, HEAD_DIM), 0.05),
        "swa_sink": _normal(ks[18], (L, SWA_Q_HEADS), 0.5),
        "swa_w_o": _normal(ks[19], (L, SWA_Q_HEADS * HEAD_DIM, D), (SWA_Q_HEADS * HEAD_DIM) ** -0.5),
        "fox_q_norm": 1.0 + _normal(ks[20], (L, HEAD_DIM), 0.05),
        "fox_k_norm": 1.0 + _normal(ks[21], (L, HEAD_DIM), 0.05),
        "fox_w_o": _normal(ks[22], (L, FOX_HEADS * HEAD_DIM, D), (FOX_HEADS * HEAD_DIM) ** -0.5),
        "w_out": _normal(ks[23], (L, D, D), D ** -0.5),
        "ffn2_norm": 1.0 + _normal(ks[24], (L, D), 0.05),
        "ffn2_w_gate": _normal(ks[25], (L, D, D_FF), D ** -0.5),
        "ffn2_w_up": _normal(ks[26], (L, D, D_FF), D ** -0.5),
        "ffn2_w_down": _normal(ks[27], (L, D_FF, D), D_FF ** -0.5),
    }

def second_block(x, rel_bias, ffn1_norm, ffn1_w_gate, ffn1_w_up, ffn1_w_down, mix_norm, w_in,
              b_forget, conf_dw, conf_dw_b, conf_ln_g, conf_ln_b, conf_w_out, sc_conv, sc_w_out,
              swa_q_norm, swa_k_norm, swa_sink, swa_w_o, fox_q_norm, fox_k_norm, fox_w_o, w_out,
              ffn2_norm, ffn2_w_gate, ffn2_w_up, ffn2_w_down):
    bsz, t = x.shape[0], x.shape[1]
    for l in range(DEPTH_2):
        x = x + 0.5 * _swiglu_2(_rmsnorm(x, ffn1_norm[l]), ffn1_w_gate[l], ffn1_w_up[l], ffn1_w_down[l])

        h = _rmsnorm(x, mix_norm[l])
        z = h @ w_in[l]
        (c_a, c_b, s_b, s_c, s_x, a_q, a_k, a_v,
         f_q, f_k, f_v, f_f, z_gate) = jnp.split(z, SPLITS, axis=-1)

        u = c_a * jax.nn.sigmoid(c_b)
        u = _causal_depthwise_conv(u, conf_dw[l]) + conf_dw_b[l]
        u = jax.nn.silu(_layernorm(u, conf_ln_g[l], conf_ln_b[l]))
        p_conf = u @ conf_w_out[l]

        p_sc = (s_b * _causal_depthwise_conv(s_c * s_x, sc_conv[l])) @ sc_w_out[l]

        q = _rmsnorm(a_q.reshape(bsz, t, SWA_Q_HEADS, HEAD_DIM), swa_q_norm[l])
        k = _rmsnorm(a_k.reshape(bsz, t, SWA_KV_HEADS, HEAD_DIM), swa_k_norm[l])
        v = a_v.reshape(bsz, t, SWA_KV_HEADS, HEAD_DIM)
        p_swa = _sliding_window_attention(q, k, v, swa_sink[l], rel_bias) @ swa_w_o[l]

        q2 = _rmsnorm(f_q.reshape(bsz, t, FOX_HEADS, HEAD_DIM), fox_q_norm[l])
        k2 = _rmsnorm(f_k.reshape(bsz, t, FOX_HEADS, HEAD_DIM), fox_k_norm[l])
        v2 = f_v.reshape(bsz, t, FOX_HEADS, HEAD_DIM)
        log_f = jax.nn.log_sigmoid(f_f.astype(jnp.float32) + b_forget[l].astype(jnp.float32))
        p_fox = _forgetting_attention(q2, k2, v2, log_f) @ fox_w_o[l]

        g = jax.nn.sigmoid(z_gate).reshape(bsz, t, N_BRANCH, D_MODEL)
        merged = (g[:, :, 0] * p_conf + g[:, :, 1] * p_sc
                  + g[:, :, 2] * p_swa + g[:, :, 3] * p_fox)
        x = x + merged @ w_out[l]

        x = x + 0.5 * _swiglu_2(_rmsnorm(x, ffn2_norm[l]), ffn2_w_gate[l], ffn2_w_up[l], ffn2_w_down[l])
    return x


def setup_inputs(seed=0):
    out = dict(first_inputs(seed))
    for name, value in second_inputs(seed + 1).items():
        if name != "x":
            out[name + "_2"] = value
    return out


def reference(
    x, ffn1_norm, ffn1_w_gu, ffn1_w_down, mix_norm, ffn2_norm, ffn2_w_gu, ffn2_w_down,
    hg_lb_logits, hg_w_in, hg_g_norm, hg_w_out, na_w_in, na_q_norm, na_k_norm, na_rpb, na_w_out,
    mla_w_in, mla_q_a_norm, mla_w_uq, mla_kv_a_norm, mla_w_ukv, mla_q_norm, mla_k_norm,
    mla_w_out, rel_bias_2, ffn1_norm_2, ffn1_w_gate_2, ffn1_w_up_2, ffn1_w_down_2, mix_norm_2,
    w_in_2, b_forget_2, conf_dw_2, conf_dw_b_2, conf_ln_g_2, conf_ln_b_2, conf_w_out_2,
    sc_conv_2, sc_w_out_2, swa_q_norm_2, swa_k_norm_2, swa_sink_2, swa_w_o_2, fox_q_norm_2,
    fox_k_norm_2, fox_w_o_2, w_out_2, ffn2_norm_2, ffn2_w_gate_2, ffn2_w_up_2, ffn2_w_down_2,
):
    x = first_block(
        x, ffn1_norm, ffn1_w_gu, ffn1_w_down, mix_norm, ffn2_norm, ffn2_w_gu, ffn2_w_down,
        hg_lb_logits, hg_w_in, hg_g_norm, hg_w_out, na_w_in, na_q_norm, na_k_norm, na_rpb,
        na_w_out, mla_w_in, mla_q_a_norm, mla_w_uq, mla_kv_a_norm, mla_w_ukv, mla_q_norm,
        mla_k_norm, mla_w_out,
    )
    return second_block(
        x, rel_bias_2, ffn1_norm_2, ffn1_w_gate_2, ffn1_w_up_2, ffn1_w_down_2, mix_norm_2,
        w_in_2, b_forget_2, conf_dw_2, conf_dw_b_2, conf_ln_g_2, conf_ln_b_2, conf_w_out_2,
        sc_conv_2, sc_w_out_2, swa_q_norm_2, swa_k_norm_2, swa_sink_2, swa_w_o_2, fox_q_norm_2,
        fox_k_norm_2, fox_w_o_2, w_out_2, ffn2_norm_2, ffn2_w_gate_2, ffn2_w_up_2,
        ffn2_w_down_2,
    )


_drawn_inputs = setup_inputs


def setup_inputs(seed=0):
    import zlib

    import numpy as np

    out = dict(_drawn_inputs(seed))
    spreads = {}
    factors = {'na_q_norm': 8.0,
     'na_k_norm': 8.0,
     'mla_q_a_norm': 8.0,
     'mla_kv_a_norm': 8.0,
     'mla_q_norm': 8.0,
     'mla_k_norm': 8.0,
     'conf_dw_b_2': 4.549,
     'conf_ln_g_2': 45.752,
     'conf_ln_b_2': 113.125,
     'swa_q_norm_2': 50.442,
     'swa_k_norm_2': 56.626,
     'swa_sink_2': 200.0,
     'fox_q_norm_2': 54.164,
     'fox_k_norm_2': 58.955,
     'ffn2_norm_2': 12.257,
     'rel_bias_2': 49.096,
     'ffn1_norm_2': 8.0,
     'b_forget_2': 28.056,
     'mix_norm_2': 2.68}
    for name, (base, spread) in spreads.items():
        noise = np.random.default_rng([zlib.crc32(name.encode()), seed]).standard_normal(out[name].shape)
        drawn = base * np.exp(spread * noise) if base else spread * noise
        out[name] = __import__('jax').numpy.asarray(drawn.astype(out[name].dtype))
    for name, factor in factors.items():
        out[name] = (out[name] * factor).astype(out[name].dtype)
    return out
```

```python
from contextlib import ExitStack

import numpy as np

import concourse.bass as bass
from concourse import mybir

F32 = mybir.dt.float32
BF16 = mybir.dt.bfloat16
U32 = mybir.dt.uint32
ACT = mybir.ActivationFunctionType
ALU = mybir.AluOpType
AX_X = mybir.AxisListType.X

P = 128
T = 256
TT = T // P
D = 1024
KC = D // P
F = 2816
FI = F // (2 * P)
EPS = 1e-6
RING = 6
TILES = 16
SLAB = TILES * P
NEG = -1e30

HG_HEADS = 8
HG_LAYERS = (0, 3)
HALVES = (1, 2, 4, 8, 16, 32, 64)
NA_HEADS = 16
NA_DIM = 64
GRID_W = 64
NA_WIN_C = 16
NA_RPB = (15, 31)
MLA_HEADS = 16
MLA_Q = 768
MLA_KV = 256
NOPE = 64
ROPE = 32
SWA_HEADS = 4
FOX_HEADS = 4
CONV_K = 31
SC_K = 3
BUCKETS = 32
MAX_DISTANCE = 128
LAYERS_1 = 4
LAYERS_2 = 2

FFN_SLABS = 3 * FI
MIX_SLABS = {"hg": 24, "na": 16, "mla": 16, "branches": 35}
MIXERS = ["hg", "na", "mla", "hg", "branches", "branches"]


def plan():
    at, out = 0, []
    for kind in MIXERS:
        ffn1 = at
        mix = ffn1 + FFN_SLABS
        ffn2 = mix + MIX_SLABS[kind]
        at = ffn2 + FFN_SLABS
        out.append((ffn1, mix, ffn2))
    return out, at


STAGES, SLABS = plan()

PARAMS = {}


def _params():
    at = 0
    for name, width in (
        [(f"norm{l}_{s}", KC) for l in range(LAYERS_1 + LAYERS_2) for s in range(3)]
        + [("hg_lb", LAYERS_1 * HG_HEADS), ("hg_g0", 1), ("hg_g3", 1), ("na_q", 1), ("na_k", 1)]
        + [("mla_qa", MLA_Q // P), ("mla_kva", MLA_KV // P), ("mla_qn", 1), ("mla_qr", 1), ("mla_kn", 1), ("mla_kr", 1)]
        + [("mla_wr", KC * P)]
        + [(f"{n}{l}", w) for l in range(LAYERS_2) for n, w in (
            ("dw", 2 * CONV_K), ("dwb", 2), ("lng", 2), ("lnb", 2), ("sc", 2 * SC_K), ("swq", 1), ("swk", 1),
            ("fxq", 1), ("fxk", 1), ("bf", 1), ("sink", SWA_HEADS), ("wf", KC * FOX_HEADS))]
        + [("relb", SWA_HEADS)]
    ):
        PARAMS[name] = (at, width)
        at += width
    return at


N_PARAMS = _params()

CONSTS = {}


def _consts():
    at = 0
    for name, width in (
        [("ident", P), ("ones", P), ("blk64", P), ("r2n", 2 * P), ("n2r", 2 * P), ("blk32", P), ("rot", P)]
        + [("cos", T), ("sin", T), ("namask", GRID_W), ("swmask", TT * T), ("fxmask", TT * T), ("hot", 2 * T)]
        + [("selrow", FOX_HEADS * T)]
        + [(f"lvl{h}", P) for h in HALVES]
    ):
        CONSTS[name] = (at, width)
        at += width
    return at


N_CONSTS = _consts()


class Counts(dict):

    def up(self, sem, n=1):
        self[sem] = self.get(sem, 0) + n
        return self[sem]

    def now(self, sem):
        return self.get(sem, 0)


def build(nc, W, PRM, CST, RPB, XIN, OUT, TOE):
    ctx = ExitStack()
    with ctx:
        def sb(name, shape, dt=F32):
            return ctx.enter_context(nc.sbuf_tensor(name, shape, dt))

        def sem(name):
            return ctx.enter_context(nc.semaphore(name))

        ring = sb("ring", [P, RING, SLAB])
        prm = sb("prm", [P, N_PARAMS])
        cst = sb("cst", [P, N_CONSTS])
        x = sb("x", [P, KC, T])
        xg = sb("xg", [P, KC, T])
        gs = sb("gs", [P, 2, T])
        sg = sb("sg", [P, 2, T])
        hid = sb("hid", [P, 2, T])
        sqsum = sb("sqsum", [P, T])
        rstd = sb("rstd", [P, T])
        rstdT = sb("rstdT", [P, TT])
        var = sb("var", [P, 2, 2 * T])
        guess = sb("guess", [P, 2, 2 * T])
        newt = sb("newt", [P, 2 * T])
        lbs = sb("lbs", [P, 2, HG_HEADS])
        oml = sb("oml", [P, 2, HG_HEADS])
        lbt = sb("lbt", [P, 6 * HG_HEADS])
        zero16 = sb("zero16", [1, 4 * P], BF16)
        small = sb("small", [P, 4, 8])
        toe = sb("toe", [P, TT, SWA_HEADS, T])
        toe_rows = sb("toe_rows", [SWA_HEADS, 2 * T])
        work = sb("work", [P, 11 * KC * T])

        acc = [ctx.enter_context(nc.psum_tensor(f"acc{i}", [P, 2, T], F32)) for i in range(4)]
        prod = [ctx.enter_context(nc.psum_tensor(f"prod{i}", [P, 2, T], F32)) for i in range(2)]
        stat = [ctx.enter_context(nc.psum_tensor(f"stat{i}", [P, 2, T], F32)) for i in range(2)]

        slab_loaded = [sem(f"slab_loaded{r}") for r in range(RING)]
        slab_done = [sem(f"slab_done{r}") for r in range(RING)]
        inputs_loaded = sem("inputs_loaded")
        bias_loaded = sem("bias_loaded")
        bias_ready = sem("bias_ready")
        toe_row = sem("toe_row")
        toe_stored = sem("toe_stored")
        toe_loaded = sem("toe_loaded")
        toe_ready = sem("toe_ready")
        toe_rows_done = sem("toe_rows_done")
        zeros_ready = sem("zeros_ready")
        vec_step = sem("vec_step")
        act_step = sem("act_step")
        lb_max = sem("lb_max")
        lb_exp = sem("lb_exp")
        xg_ready = sem("xg_ready")
        evac = sem("evac")
        mid_done = sem("mid_done")
        sig_ready = sem("sig_ready")
        sq_ready = sem("sq_ready")
        sum_ready = sem("sum_ready")
        stat_done = sem("stat_done")
        var_ready = sem("var_ready")
        guess_ready = sem("guess_ready")
        rstd_ready = sem("rstd_ready")
        norm_ready = sem("norm_ready")
        tree_ready = sem("tree_ready")
        tree_done = sem("tree_done")
        tree_taken = sem("tree_taken")
        mix_done = sem("mix_done")
        mix_ready = sem("mix_ready")
        s_done = sem("s_done")
        logits_ready = sem("logits_ready")
        exp_done = sem("exp_done")
        p_ready = sem("p_ready")
        t_done = sem("t_done")
        pt_ready = sem("pt_ready")
        pv_done = sem("pv_done")
        ot_ready = sem("ot_ready")
        aux_ready = sem("aux_ready")
        log_ready = sem("log_ready")
        rot_done = sem("rot_done")
        stored = sem("stored")

        def par(name, i=0, n=1, p=P):
            a, _ = PARAMS[name]
            return prm[0:p, a + i:a + i + n]

        def con(name, i=0, n=None, p=P):
            a, w = CONSTS[name]
            return cst[0:p, a + i:a + i + (w if n is None else n)]

        ident = con("ident")
        ones = con("ones")

        def region(at, n=1):
            return work[:, at * KC * T:(at + n) * KC * T]

        def act3(at):
            return region(at).rearrange("p (c t) -> p c t", c=KC)

        def over(ap, n):
            return ap.unsqueeze(1).to_broadcast([ap.shape[0], n, ap.shape[1]])

        def backwards(ap):
            dims = [list(d) for d in ap.ap]
            step, n = dims[-1]
            dims[-1] = [-step, n]
            return bass.AP(tensor=ap.tensor, offset=ap.offset + step * (n - 1), ap=dims)

        def tile_of(s, j, n=1):
            return ring[:, s % RING, j * P:(j + n) * P]

        def halves(ap):
            return ap.rearrange("p a (b t) -> p (a b) t", b=2)

        def half64(h):
            return slice(64 * (h % 2), 64 * (h % 2) + 64)

        def part32(h):
            return slice(32 * (h % 4), 32 * (h % 4) + 32)

        hg_q, hg_qf, hg_qy = act3(0), act3(1), act3(2)
        hg_kg, hg_kx = act3(3), act3(4)
        hg_f = (act3(5), act3(6))
        hg_ad, hg_ao = act3(7), act3(8)
        hg_ks = act3(8)
        hg_v = region(9).rearrange("p (a n) -> p a n", a=TT)
        hg_sg = act3(10)
        hg_o, hg_sq = act3(0), act3(3)

        at_o = act3(8)
        at_buf = region(9, 2)
        logits = [at_buf[:, i * 512:(i + 1) * 512].rearrange("p (a t) -> p a t", a=TT) for i in range(2)]
        probs = [at_buf[:, (2 + i) * 512:(3 + i) * 512].rearrange("p (a t) -> p a t", a=TT) for i in range(2)]
        probsT = [at_buf[:, (4 + i) * 512:(5 + i) * 512].rearrange("p (a t) -> p a t", a=TT) for i in range(2)]
        squares = [region(3)[:, i * 512:(i + 1) * 512].rearrange("p (a t) -> p a t", a=2) for i in range(2)]

        na_q, na_k = act3(0), act3(1)
        na_v = region(2).rearrange("p (a n) -> p a n", a=TT)
        na_b = region(4, 4).rearrange("p (h a r k) -> p h a r k", h=NA_HEADS, a=TT, r=4)

        ml_cq, ml_ckv, ml_sq = act3(0)[:, 0:6, :], act3(0)[:, 6:8, :], act3(1)
        ml_qn, ml_kn = act3(2), act3(5)
        ml_qr, ml_kr = act3(3)[:, 0:4, :], act3(3)[:, 4:8, :]
        ml_krr, ml_sqr, ml_krot = act3(4)[:, 0, :], act3(4)[:, 1:5, :], act3(4)[:, 5, :]
        ml_v = region(6).rearrange("p (a n) -> p a n", a=TT)
        ml_sqn = act3(7)

        br_q, br_k = act3(0)[:, 0:4, :], act3(0)[:, 4:8, :]
        br_v = region(1)[:, 0:TT * 3 * P].rearrange("p (a n) -> p a n", a=TT)
        br_conv = region(1)[:, 768:1280].rearrange("p (a t) -> p a t", a=2)
        br_sq = region(1)[:, 1280:1792].rearrange("p (a t) -> p a t", a=2)
        UPAD, SPAD = CONV_K - 1, SC_K - 1
        br_u = region(2)[:, 0:2 * (T + UPAD)].rearrange("p (a t) -> p a t", a=2)
        br_t = region(2)[:, 572:572 + 2 * (T + SPAD)].rearrange("p (a t) -> p a t", a=2)
        br_sb = region(2)[:, 1088:1600].rearrange("p (a t) -> p a t", a=2)
        br_x, br_l, br_cum, br_ncum = (region(3)[0:FOX_HEADS, 1024 + i * T:1024 + (i + 1) * T] for i in range(4))
        br_g = region(4, 4).rearrange("p (c t) -> p c t", t=T)
        br_sco, br_cvo = at_o[:, 4:6, :], at_o[:, 6:8, :]
        br_m = act3(0)

        block = ctx.enter_context(nc.Block())

        @block.sync
        def _(sp):
            sp.dma_start(prm[:, :], PRM).then_inc(inputs_loaded, 16)
            sp.dma_start(x[:, :, :], XIN).then_inc(inputs_loaded, 16)
            sp.dma_start(cst[:, :], CST).then_inc(inputs_loaded, 16)
            for r in range(RING):
                sp.dma_start(ring[:, r, :], W[r]).then_inc(slab_loaded[r], 16)
            rounds = SLABS // RING
            with sp.Fori(1, rounds) as i:
                for r in range(RING):
                    sp.wait_ge(slab_done[r], i)
                    sp.dma_start(ring[:, r, :], W[bass.ds(i * RING + r, 1)].rearrange("a p n -> p (a n)")).then_inc(slab_loaded[r], 16)
            for s in range(rounds * RING, SLABS):
                sp.wait_ge(slab_done[s % RING], rounds)
                sp.dma_start(ring[:, s % RING, :], W[s]).then_inc(slab_loaded[s % RING], 16)
            sp.wait_ge(xg_ready, KC * (3 * len(MIXERS)) + 4)
            sp.dma_start(OUT, x[:, :, :]).then_inc(stored, 16)
            sp.wait_ge(stored, 16)

        @block.tensor
        def _(pe):
            c = Counts()
            n_prod = [0]
            n_stat = [0]

            def slab_in(s):
                pe.wait_ge(slab_loaded[s % RING], 16 * (s // RING + 1))

            def bank():
                n = n_prod[0]
                n_prod[0] += 1
                if n >= 2:
                    pe.wait_ge(evac, n - 1)
                return prod[n % 2]

            def stat_bank():
                n = n_stat[0]
                n_stat[0] += 1
                if n >= 2:
                    pe.wait_ge(var_ready, n - 1)
                return stat[n % 2]

            def chunks(out, s, rhs, n_chunks=2, k_chunks=KC, first=0, wait=None, width=P):
                for n in range(n_chunks):
                    for k in range(k_chunks):
                        if wait is not None and n == 0:
                            pe.wait_ge(wait, c.up(wait))
                        last = nc.tensor.matmul(out[:, n, :], tile_of(s, first + n * k_chunks + k), rhs(k),
                                                start=(k == 0), stop=(k == k_chunks - 1))
                return last

            def stats(lhs_rhs, n=T):
                b = stat_bank()
                out = b[:, :, :].rearrange("p a t -> p (a t)")[:, 0:n]
                for i, (lhs, rhs) in enumerate(lhs_rhs):
                    last = nc.tensor.matmul(out, lhs, rhs, start=(i == 0), stop=(i == len(lhs_rhs) - 1))
                last.then_inc(stat_done, 1)

            def token_stats():
                pe.wait_ge(sum_ready, c.up(sum_ready))
                stats([(ones, sqsum[:, :])])
                c.up(rstd_ready)
                c.up(sq_ready)

            def token_columns():
                pe.wait_ge(rstd_ready, c.now(rstd_ready))
                b = stat_bank()
                for tt in range(TT):
                    last = nc.tensor.matmul(b[:, 0, tt:tt + 1], rstd[0:1, tt * P:(tt + 1) * P], ones[0:1, 0:1],
                                            start=True, stop=True)
                last.then_inc(stat_done, 1)

            def project(s, rhs=lambda k: xg[:, k, :], **kw):
                slab_in(s)
                chunks(bank(), s, rhs, **kw).then_inc(slab_done[s % RING], 1)

            def project_tokens(s, n_slabs, cols, k_per_slab):
                out = [bank() for _ in range(TT)]
                k = 0
                for j in range(n_slabs):
                    slab_in(s + j)
                    ks = list(range(k, min(k + k_per_slab, KC)))
                    for i, kk in enumerate(ks):
                        for tt in range(TT):
                            last = nc.tensor.matmul(
                                out[tt][:, :, :].rearrange("p a t -> p (a t)")[:, 0:cols],
                                xg[:, kk, tt * P:(tt + 1) * P],
                                ring[:, (s + j) % RING, i * cols:(i + 1) * cols],
                                start=(kk == 0), stop=(kk == KC - 1))
                    last.then_inc(slab_done[(s + j) % RING], 1)
                    k += len(ks)

            def ffn(s0):
                def gate(s, i=None, wait=None):
                    turn = s // RING + 1
                    pe.wait_ge(slab_loaded[s % RING], 16 * turn if i is None else (i + turn) * 16)
                    return chunks(prod[n_gate % 2], s, lambda k: xg[:, k, :], wait=wait)

                def down(s, i=None):
                    turn = s // RING + 1
                    pe.wait_ge(slab_loaded[s % RING], 16 * turn if i is None else (i + turn) * 16)
                    for n in range(KC):
                        for k in range(2):
                            last = nc.tensor.matmul(acc[n // 2][:, n % 2, :], tile_of(s, 2 * n + k), hid[:, k, :],
                                                    start=False, stop=True, skip_group_check=True)
                    return last

                n_gate = n_prod[0]
                assert n_gate % 2 == 0
                if n_gate:
                    pe.wait_ge(evac, n_gate)
                gate(s0, wait=xg_ready).then_inc(slab_done[s0 % RING], 1)
                token_stats()
                for i in range(4):
                    nc.tensor.matmul(acc[i][:, :, :], zero16[:, 0:P], zero16[:, 0:2 * T], start=True, stop=True,
                                     skip_group_check=True)
                n_gate += 1
                gate(s0 + 1).then_inc(slab_done[(s0 + 1) % RING], 1)
                base = n_prod[0]
                with pe.Fori(0, (FI - 1) // 2) as i:
                    for u in range(2):
                        s = s0 + 2 + 3 * u
                        taken = base + 2 * u
                        n_gate = 0
                        pe.wait_ge(evac, i * 4 + (taken + 1))
                        gate(s, i).then_inc(slab_done[s % RING], 1)
                        pe.wait_ge(evac, i * 4 + (taken + 2))
                        down(s + 1, i).then_inc(slab_done[(s + 1) % RING], 1)
                        n_gate = 1
                        gate(s + 2, i).then_inc(slab_done[(s + 2) % RING], 1)
                n_prod[0] += 2 * FI
                pe.wait_ge(evac, n_prod[0])
                down(s0 + FFN_SLABS - 1).then_inc(slab_done[(s0 + FFN_SLABS - 1) % RING], 1)

            def out_projection(s, rhs):
                for j in range(4):
                    project(s + j, rhs)

            def attention(heads, scores, values):
                for i in range(heads + 2):
                    if i < heads:
                        for tt in range(TT):
                            pairs = scores(i, tt)
                            for n, (lhs, rhs) in enumerate(pairs):
                                last = nc.tensor.matmul(acc[i % 2][:, tt, :], lhs, rhs, start=(n == 0),
                                                        stop=(n == len(pairs) - 1))
                        last.then_inc(s_done, 1)
                    if 1 <= i <= heads:
                        h = i - 1
                        pe.wait_ge(p_ready, c.up(p_ready))
                        for kt in range(TT):
                            for tt in range(TT):
                                last = nc.tensor.transpose(acc[2 + h % 2][:, kt, tt * P:(tt + 1) * P],
                                                           probs[h % 2][:, tt, kt * P:(kt + 1) * P], ident)
                        last.then_inc(t_done, 1)
                    if i >= 2:
                        h = i - 2
                        if h % 2 == 0 and h >= 4:
                            pe.wait_ge(ot_ready, ot_base + h // 2 - 1)
                        pe.wait_ge(pt_ready, c.up(pt_ready))
                        half = slice(64 * (h % 2), 64 * (h % 2) + 64)
                        for kt in range(TT):
                            last = nc.tensor.matmul(stat[h // 2 % 2][half, 0, :], values(h, kt), probsT[h % 2][:, kt, :],
                                                    start=(kt == 0), stop=(kt == TT - 1))
                        last.then_inc(pv_done, 1)

            def hg(s):
                project(s, wait=xg_ready)
                token_stats()
                for j in range(1, 12):
                    project(s + j)
                token_columns()
                pe.wait_ge(tree_ready, c.up(tree_ready))
                for h in range(HG_HEADS):
                    for tt in range(TT):
                        tok = slice(tt * P, (tt + 1) * P)
                        last = nc.tensor.matmul(acc[h // 2][:, h % 2, tok], hg_ks[:, h, tok], hg_q[:, h, tok],
                                                start=True, stop=True)
                last.then_inc(tree_done, 1)
                for n, half in enumerate(HALVES):
                    if n in (0, 2):
                        project_tokens(s + 12 + 2 * (n // 2), 2, 2 * T, 4)
                    elif n >= 3:
                        project(s + 16 + n - 3)
                    pe.wait_ge(tree_ready, c.up(tree_ready))
                    pe.wait_ge(tree_taken, c.up(tree_taken))
                    for h in range(HG_HEADS):
                        for tt in range(TT):
                            tok = slice(tt * P, (tt + 1) * P)
                            o4 = acc[h // 2][:, h % 2, tok].rearrange("p (b two l) -> p b two l", two=2, l=half)
                            for keys, queries, side in ((hg_kg, hg_qf, 1), (hg_kx, hg_qy, 0)):
                                q4 = queries[:, h, tok].rearrange("p (b two l) -> p b two l", two=2, l=half)
                                last = nc.tensor.matmul(o4[:, :, side, :], keys[:, h, tok], q4[:, :, side, :],
                                                        start=True, stop=True, skip_group_check=True)
                    last.then_inc(tree_done, 1)
                pe.wait_ge(tree_ready, c.up(tree_ready))
                pe.wait_ge(tree_taken, c.up(tree_taken))
                lo, hi = slice(0, P), slice(P, T)
                for h in range(HG_HEADS):
                    nc.tensor.matmul(acc[h // 2][:, h % 2, hi], hg_kg[:, h, lo], hg_qf[:, h, hi], start=True, stop=True)
                    last = nc.tensor.matmul(acc[h // 2][:, h % 2, lo], hg_kx[:, h, hi], hg_qy[:, h, lo], start=True, stop=True)
                last.then_inc(tree_done, 1)
                pe.wait_ge(tree_taken, c.up(tree_taken))
                for b in range(4):
                    for h in (2 * b, 2 * b + 1):
                        for tt in range(TT):
                            tok = slice(tt * P, (tt + 1) * P)
                            nc.tensor.matmul(acc[b][:, h % 2, tok], hg_v[:, tt, h * P:(h + 1) * P], hg_ad[:, h, tok],
                                             start=True, stop=False)
                            last = nc.tensor.matmul(acc[b][:, h % 2, tok], hg_v[:, 1 - tt, h * P:(h + 1) * P],
                                                    hg_ao[:, h, tok], start=False, stop=True)
                    last.then_inc(mix_done, 1)
                for b in range(4):
                    pe.wait_ge(sq_ready, c.up(sq_ready))
                    stats([(ones, hg_sq[:, 2 * b:2 * b + 2, :])], 2 * T)
                project(s + 20, lambda k: hg_o[:, k, :], wait=mix_ready)
                for j in range(1, 4):
                    project(s + 20 + j, lambda k: hg_o[:, k, :])

            def head_stats(j):
                pe.wait_ge(sq_ready, c.up(sq_ready))
                stats([(con("blk64"), squares[j % 2][:, :, :])], 2 * T)

            def na(s):
                project(s, wait=xg_ready)
                token_stats()
                for j in range(1, 8):
                    project(s + j)
                    head_stats(j - 1)
                token_columns()
                for g in range(2):
                    project_tokens(s + 8 + 2 * g, 2, 2 * T, 4)
                    if g == 0:
                        head_stats(7)
                pe.wait_ge(norm_ready, c.up(norm_ready, 8))
                attention(NA_HEADS,
                          lambda h, tt: [(na_q[half64(h), h // 2, tt * P:(tt + 1) * P], na_k[half64(h), h // 2, :])],
                          lambda h, kt: na_v[:, kt, h * NA_DIM:(h + 1) * NA_DIM])
                pe.wait_ge(ot_ready, ot_base + NA_HEADS // 2)
                out_projection(s + 12, lambda k: at_o[:, k, :])

            def mla(s):
                project(s, wait=xg_ready)
                token_stats()
                for j in range(1, 4):
                    project(s + j)
                b = bank()
                for k in range(KC):
                    last = nc.tensor.matmul(b[:, 0, :], par("mla_wr", k * P, P), xg[:, k, :], start=(k == 0), stop=(k == KC - 1))
                last.then_inc(mid_done, 1)
                for n in (MLA_Q // P, MLA_KV // P):
                    pe.wait_ge(sq_ready, c.up(sq_ready))
                    at = 0 if n == MLA_Q // P else MLA_Q // P
                    stats([(ones, ml_sq[:, at + i, :]) for i in range(n)])
                pe.wait_ge(norm_ready, c.up(norm_ready))
                for j in range(6):
                    project(s + 4 + j, lambda k: ml_cq[:, k, :], k_chunks=6)
                pe.wait_ge(norm_ready, c.up(norm_ready))
                for j in range(2):
                    slab_in(s + 10 + j)
                    for u in range(2):
                        last = chunks(bank(), s + 10 + j, lambda k: ml_ckv[:, k, :], k_chunks=2, first=8 * u)
                        last.then_inc(mid_done, 1)
                        b = bank()
                        for tt in range(TT):
                            for k in range(2):
                                last = nc.tensor.matmul(b[:, tt, :], ml_ckv[:, k, tt * P:(tt + 1) * P],
                                                        tile_of(s + 10 + j, 8 * u + 4 + 2 * k, 2),
                                                        start=(k == 0), stop=(k == 1))
                        last.then_inc(mid_done if u == 0 else slab_done[(s + 10 + j) % RING], 1)
                for pair in range(3):
                    pe.wait_ge(mix_ready, c.up(mix_ready))
                    b = bank()
                    n = 2 if pair < 2 else 1
                    for i in range(n):
                        src = ml_qr[:, 2 * pair + i, :] if pair < 2 else ml_kr[:, 0, :]
                        last = nc.tensor.matmul(b[:, i, :], con("rot"), src, start=True, stop=True)
                    last.then_inc(rot_done, 1)
                for keys in (False, True):
                    sn, sr = (ml_sqn, ml_sqr)
                    pe.wait_ge(sq_ready, c.up(sq_ready, 2))
                    for r in range(4):
                        b = stat_bank()
                        rope_sq = sr[:, 0 if keys else r, :]
                        for i in range(2):
                            nc.tensor.matmul(b[:, i, :], con("blk64"), sn[:, 2 * r + i, :], start=True, stop=False)
                            last = nc.tensor.matmul(b[:, i, :], con("r2n", i * P, P), rope_sq, start=False, stop=True)
                        last.then_inc(stat_done, 1)
                        b = stat_bank()
                        nc.tensor.matmul(b[:, 0, :], con("blk32"), rope_sq, start=True, stop=False)
                        for i in range(2):
                            last = nc.tensor.matmul(b[:, 0, :], con("n2r", i * P, P), sn[:, 2 * r + i, :],
                                                    start=False, stop=(i == 1))
                        last.then_inc(stat_done, 1)
                pe.wait_ge(norm_ready, c.up(norm_ready))
                attention(MLA_HEADS,
                          lambda h, tt: [(ml_qn[half64(h), h // 2, tt * P:(tt + 1) * P], ml_kn[half64(h), h // 2, :]),
                                         (ml_qr[part32(h), h // 4, tt * P:(tt + 1) * P], ml_kr[part32(h), h // 4, :])],
                          lambda h, kt: ml_v[:, kt, h * 64:(h + 1) * 64])
                pe.wait_ge(ot_ready, ot_base + MLA_HEADS // 2)
                out_projection(s + 12, lambda k: at_o[:, k, :])

            def branches(s):
                project(s, wait=xg_ready)
                token_stats()
                for j in range(1, 4):
                    project(s + j)
                    head_stats(j - 1)
                b = bank()
                for k in range(KC):
                    last = nc.tensor.matmul(b[0:FOX_HEADS, 0, :], par(f"wf{layer - LAYERS_1}", k * FOX_HEADS, FOX_HEADS),
                                            xg[:, k, :], start=(k == 0), stop=(k == KC - 1))
                last.then_inc(mid_done, 1)
                head_stats(3)
                token_columns()
                project_tokens(s + 4, 2, 3 * P, 5)
                for j in range(5):
                    project(s + 6 + j)
                for j in range(8):
                    project(s + 11 + j)
                pe.wait_ge(norm_ready, c.up(norm_ready, 5))
                attention(SWA_HEADS + FOX_HEADS, br_scores, br_values)
                for j in range(8, 16):
                    project(s + 11 + j)
                pe.wait_ge(ot_ready, ot_base + (SWA_HEADS + FOX_HEADS) // 2)
                pe.wait_ge(mix_ready, c.up(mix_ready))
                stats([(ones, br_conv[:, i, :]) for i in range(2)])
                pe.wait_ge(sq_ready, c.up(sq_ready))
                stats([(ones, br_sq[:, i, :]) for i in range(2)])
                for br in range(4):
                    src = (at_o[:, 0:2, :], at_o[:, 2:4, :], br_sco, br_cvo)[br]
                    if br >= 2:
                        pe.wait_ge(mix_ready, c.up(mix_ready))
                    slab_in(s + 27 + br)
                    for j in range(4):
                        last = chunks(bank(), s + 27 + br, lambda k: src[:, k, :], k_chunks=2, first=4 * j)
                        if j < 3:
                            last.then_inc(mid_done, 1)
                    last.then_inc(slab_done[(s + 27 + br) % RING], 1)
                pe.wait_ge(mix_ready, c.up(mix_ready))
                for j in range(4):
                    project(s + 31 + j, lambda k: br_m[:, k, :])

            def br_scores(h, tt):
                tok = slice(tt * P, (tt + 1) * P)
                if h < SWA_HEADS:
                    return [(br_q[half64(h), h // 2, tok], br_k[half64(h), h // 2, :])]
                g = h - SWA_HEADS
                return [(br_q[half64(g), 2 + g // 2, tok], br_k[half64(g), 2 + g // 2, :]),
                        (br_cum[0:FOX_HEADS, tok], con("selrow", g * T, T, FOX_HEADS)),
                        (con("selrow", g * T, P, FOX_HEADS), br_ncum[0:FOX_HEADS, :])]

            def br_values(h, kt):
                if h < SWA_HEADS:
                    return br_v[:, kt, (h // 2) * 64:(h // 2) * 64 + 64]
                return br_v[:, kt, P + (h - SWA_HEADS) * 64:P + (h - SWA_HEADS) * 64 + 64]

            pe.wait_ge(inputs_loaded, 48)
            nc.tensor.matmul(acc[0][0:SWA_HEADS, :, :].rearrange("p a t -> p (a t)"), par("relb", 0, SWA_HEADS, BUCKETS),
                             con("hot", 0, 2 * T, BUCKETS), start=True, stop=True).then_inc(toe_row, 1)
            pe.wait_ge(zeros_ready, 1)
            ot_base = 0
            for layer, kind in enumerate(MIXERS):
                s1, sm, s2 = STAGES[layer]
                ffn(s1)
                {"hg": hg, "na": na, "mla": mla, "branches": branches}[kind](sm)
                ot_base += {"hg": 0, "na": 8, "mla": 8, "branches": 4}[kind]
                ffn(s2)

        @block.scalar
        def _(act):
            c = Counts()
            table = [None]
            n_stat = [0]

            def tables(name):
                if table[0] != name:
                    table[0] = name
                    act.preload_act_table_set(name)

            def root(width):
                tables("natural_log_exp_and_others")
                q = n_stat[0] % 2
                n_stat[0] += 1
                act.wait_ge(var_ready, c.up(var_ready))
                nc.scalar.activation(guess[:, q, 0:width], var[:, q, 0:width], ACT.Ln).then_inc(act_step, 1)
                act.wait_ge(act_step, c.up(act_step))
                nc.scalar.activation(guess[:, q, 0:width], guess[:, q, 0:width], ACT.Exp, scale=-0.5).then_inc(guess_ready, 1)

            def skip_stat():
                n_stat[0] += 1
                c.up(var_ready)

            def square(out, src):
                nc.scalar.activation(out, src, ACT.Square).then_inc(sq_ready, 1)

            def token_norm(scratch):
                act.wait_ge(xg_ready, c.up(xg_ready, KC))
                square(scratch, x[:, :, :])
                root(T)

            def sigmoid(out, src):
                tables("sigmoid_and_others")
                act.wait_ge(evac, c.up(evac))
                nc.scalar.activation(out, src, ACT.Sigmoid).then_inc(sig_ready, 1)

            def ffn():
                token_norm(act3(0))
                sigmoid(sg[:, :, :], gs[:, :, :])
                base = c.now(evac)
                with act.Fori(1, FI) as f:
                    act.wait_ge(evac, f * 2 + base)
                    nc.scalar.activation(sg[:, :, :], gs[:, :, :], ACT.Sigmoid).then_inc(sig_ready, 1)
                c.up(evac, 2 * FI - 1)

            def attention(heads, scale, sink=None):
                tables("natural_log_exp_and_others")
                for i in range(heads + 2):
                    if i < heads:
                        act.wait_ge(logits_ready, c.up(logits_ready))
                        st = small[:, i % 2, :]
                        src = acc[i % 2] if scale else logits[i % 2]
                        for tt in range(TT):
                            last = nc.scalar.activation(probs[i % 2][:, tt, :], src[:, tt, :], ACT.Exp, bias=st[:, tt:tt + 1],
                                                        scale=scale or 1.0, accum_out=st[:, 2 + tt:3 + tt])
                        if sink is not None and i < SWA_HEADS:
                            last = nc.scalar.activation(st[:, 4:6], st[:, 0:2], ACT.Exp, bias=sink(i))
                        last.then_inc(exp_done, 1)
                    if 1 <= i <= heads:
                        act.wait_ge(t_done, c.up(t_done))
                        nc.scalar.activation(probsT[(i - 1) % 2][:, :, :], acc[2 + (i - 1) % 2][:, :, :], ACT.Copy).then_inc(pt_ready, 1)
                    if i >= 2:
                        act.wait_ge(pv_done, c.up(pv_done))
                        if i % 2:
                            pair = (i - 2) // 2
                            nc.scalar.activation(at_o[:, pair, :], stat[pair % 2][:, 0, :], ACT.Copy).then_inc(ot_ready, 1)

            def hg():
                token_norm(act3(0))
                for _ in range(8):
                    sigmoid(sg[:, :, :], gs[:, :, :])
                c.up(evac, 4)
                skip_stat()
                c.up(evac, 4)
                for _ in range(4):
                    sigmoid(sg[:, :, :], gs[:, :, :])
                for b in range(4):
                    act.wait_ge(mix_done, c.up(mix_done))
                    square(hg_sq[:, 2 * b:2 * b + 2, :], acc[b][:, :, :])
                for b in range(4):
                    root(2 * T)
                c.up(evac, 4)

            def head_square(j, src):
                act.wait_ge(evac, c.up(evac))
                square(squares[j % 2][:, :, :], src)

            def na():
                act.wait_ge(xg_ready, c.now(xg_ready) + KC)
                for r in range(4):
                    tt, rr = r // 2, r % 2
                    for key_row in range(4):
                        src = bass.AP(tensor=RPB.tensor, offset=(7 - r + key_row) * NA_RPB[1] + NA_WIN_C - GRID_W,
                                      ap=[[1, GRID_W], [NA_RPB[0] * NA_RPB[1], NA_HEADS], [1, GRID_W]])
                        act.dma_start(na_b[rr * GRID_W:(rr + 1) * GRID_W, :, tt, key_row, :], src).then_inc(bias_loaded, 16)
                token_norm(act3(0))
                for j in range(9):
                    if j < 8:
                        head_square(j, (na_q if j < 4 else na_k)[:, 2 * (j % 4):2 * (j % 4) + 2, :])
                    if j == 8:
                        skip_stat()
                    if j >= 1:
                        root(2 * T)
                c.up(evac, 4)
                attention(NA_HEADS, None)
                c.up(evac, 4)

            def mla():
                token_norm(act3(1))
                act.wait_ge(evac, c.up(evac, 3))
                square(ml_sq[:, 0:6, :], ml_cq)
                act.wait_ge(evac, c.up(evac, 1))
                square(ml_sq[:, 6:8, :], ml_ckv)
                c.up(evac)
                root(T)
                root(T)
                act.wait_ge(evac, c.up(evac, 4))
                square(ml_sqn, ml_qn)
                act.wait_ge(evac, c.up(evac, 2))
                square(ml_sqr, ml_qr)
                c.up(evac, 8 + 3)
                n = c.now(stat_done) + 2 + 1
                for keys in (False, True):
                    if keys:
                        act.wait_ge(stat_done, ml_stats + 8)
                        square(ml_sqn, ml_kn)
                        square(ml_sqr[:, 0, :], ml_krr)
                    for r in range(4):
                        root(2 * T)
                        root(T)
                attention(MLA_HEADS, (NOPE + ROPE) ** -0.5)
                c.up(evac, 4)

            def branches(l):
                token_norm(act3(2))
                for j in range(5):
                    if j < 4:
                        head_square(j, (br_q[:, 0:2, :], br_k[:, 0:2, :], br_q[:, 2:4, :], br_k[:, 2:4, :])[j])
                    if j >= 1:
                        root(2 * T)
                act.wait_ge(aux_ready, c.up(aux_ready))
                nc.scalar.activation(br_l, br_cum, ACT.Exp, scale=-1.0).then_inc(act_step, 1)
                act.wait_ge(act_step, c.up(act_step))
                nc.scalar.activation(br_l, br_l, ACT.Ln, bias=con("ones", 0, 1, FOX_HEADS)).then_inc(log_ready, 1)
                c.up(evac, 1)
                skip_stat()
                c.up(evac, 2)
                sigmoid(sg[:, :, :], gs[:, :, :])
                c.up(evac, 4)
                def gate(j):
                    sigmoid(br_g[:, 2 * j:2 * j + 2, :], (gs, hid)[j % 2][:, :, :])
                for j in range(8):
                    gate(j)
                attention(SWA_HEADS + FOX_HEADS, None, lambda h: par(f"sink{l}", h))
                for j in range(8, 16):
                    gate(j)
                skip_stat()
                act.wait_ge(aux_ready, c.up(aux_ready))
                square(br_sq, br_conv)
                root(T)
                tables("sigmoid_and_others")
                act.wait_ge(aux_ready, c.up(aux_ready))
                nc.scalar.activation(sg[:, :, :], br_conv, ACT.Sigmoid).then_inc(sig_ready, 1)
                c.up(evac, 16 + 4)

            act.wait_ge(toe_rows_done, 1)
            act.dma_start(TOE, toe_rows[:, :]).then_inc(toe_stored, 16)
            act.wait_ge(toe_stored, 16)
            for tt in range(TT):
                src = bass.AP(tensor=TOE.tensor, offset=tt * P, ap=[[1, P], [2 * T, SWA_HEADS], [1, T]])
                act.dma_start(toe[:, tt, :, :], src).then_inc(toe_loaded, 16)
            tables("natural_log_exp_and_others")
            act.wait_ge(lb_max, 1)
            nc.scalar.activation(lbt[:, 0:4 * HG_HEADS], lbt[:, 0:4 * HG_HEADS], ACT.Exp).then_inc(lb_exp, 1)
            ml_stats = 0
            for layer, kind in enumerate(MIXERS):
                ffn()
                if kind == "mla":
                    ml_stats = n_stat[0] + 3
                if kind == "branches":
                    branches(layer - LAYERS_1)
                else:
                    {"hg": hg, "na": na, "mla": mla}[kind]()
                ffn()

        @block.vector
        def _(dve):
            c = Counts()
            n_prod = [0]
            n_stat = [0]
            v = nc.vector

            def link(ins):
                ins.then_inc(vec_step, 1)
                dve.wait_ge(vec_step, c.up(vec_step))

            def own(ins, signal):
                ins.then_inc(signal, 1)
                dve.wait_ge(signal, c.up(signal))

            def product(s=None):
                n = n_prod[0]
                n_prod[0] += 1
                if s is None:
                    dve.wait_ge(mid_done, c.up(mid_done))
                else:
                    dve.wait_ge(slab_done[s % RING], s // RING + 1)
                return prod[n % 2]

            def variance(width, n):
                q = n_stat[0] % 2
                n_stat[0] += 1
                dve.wait_ge(stat_done, c.up(stat_done))
                v.tensor_scalar(var[:, q, 0:width], stat[q][:, :, :].rearrange("p a t -> p (a t)")[:, 0:width],
                                1.0 / n, EPS, ALU.mult, ALU.add).then_inc(var_ready, 1)
                c.up(var_ready)
                return q

            def inverse_root(q, width, out=None, signal=None):
                dve.wait_ge(guess_ready, c.up(guess_ready))
                y, w, t = guess[:, q, 0:width], var[:, q, 0:width], newt[:, 0:width]
                out = y if out is None else out
                link(v.scalar_tensor_tensor(t, y, -0.5, y, ALU.mult, ALU.mult))
                link(v.tensor_tensor(t, t, w, ALU.mult))
                own(v.scalar_tensor_tensor(out, t, 1.5, y, ALU.add, ALU.mult), signal or vec_step)
                return out

            def next_norm(chunk, gain):
                v.tensor_scalar(xg[:, chunk, :], x[:, chunk, :], par(gain, chunk), None, ALU.mult).then_inc(xg_ready, 1)

            def token_norm(scratch):
                dve.wait_ge(sq_ready, c.up(sq_ready))
                v.tensor_reduce(sqsum[:, :], scratch.rearrange("p c t -> p t c"), AX_X, ALU.add).then_inc(sum_ready, 1)
                q = variance(T, D)
                inverse_root(q, T, rstd[:, :], rstd_ready)

            def scaled(out, bank, factor=None):
                if factor is None:
                    own(v.tensor_tensor(out, bank, over(rstd[:, :], 2), ALU.mult), evac)
                else:
                    own(v.scalar_tensor_tensor(out, bank, factor, over(rstd[:, :], 2), ALU.mult, ALU.mult), evac)

            def columns():
                q = n_stat[0] % 2
                n_stat[0] += 1
                dve.wait_ge(stat_done, c.up(stat_done))
                own(v.tensor_copy(rstdT[:, :], stat[q][:, 0, 0:TT]), var_ready)

            def values(s, out, cols, at=0):
                for tt in range(TT):
                    b = product(s)
                    own(v.tensor_scalar(out[:, tt, at:at + cols], b[:, :, :].rearrange("p a t -> p (a t)")[:, 0:cols],
                                        rstdT[:, tt:tt + 1], None, ALU.mult), evac)

            def residual(s, gain):
                for j in range(4):
                    b = product(s + j)
                    pair = x[:, 2 * j:2 * j + 2, :]
                    own(v.tensor_tensor(pair, pair, b[:, :, :], ALU.add), evac)
                    for i in range(2):
                        next_norm(2 * j + i, gain)

            def ffn(s0, gain):
                def gated():
                    v.tensor_tensor(sg[:, :, :], sg[:, :, :], gs[:, :, :], ALU.mult).then_inc(vec_step, 1)

                def scale_by_token():
                    v.tensor_tensor(sg[:, :, :], sg[:, :, :], over(rstd[:, :], 2), ALU.mult).then_inc(vec_step, 1)

                token_norm(act3(0))
                scaled(gs[:, :, :], product(s0)[:, :, :])
                dve.wait_ge(sig_ready, c.up(sig_ready))
                gated()
                dve.wait_ge(vec_step, c.up(vec_step))
                scale_by_token()
                dve.wait_ge(vec_step, c.up(vec_step))
                own(v.tensor_tensor(hid[:, :, :], product(s0 + 1)[:, :, :], sg[:, :, :], ALU.mult), evac)
                e0, g0, t0 = c.now(evac), c.now(sig_ready), c.now(vec_step)
                with dve.Fori(0, (FI - 1) // 2) as i:
                    for u in range(2):
                        s = s0 + 2 + 3 * u
                        dve.wait_ge(slab_done[s % RING], i + (s // RING + 1))
                        v.tensor_tensor(gs[:, :, :], prod[0][:, :, :], over(rstd[:, :], 2), ALU.mult).then_inc(evac, 1)
                        dve.wait_ge(sig_ready, i * 2 + (g0 + u + 1))
                        gated()
                        dve.wait_ge(vec_step, i * 4 + (t0 + 2 * u + 1))
                        scale_by_token()
                        dve.wait_ge(vec_step, i * 4 + (t0 + 2 * u + 2))
                        s += 2
                        dve.wait_ge(slab_done[s % RING], i + (s // RING + 1))
                        v.tensor_tensor(hid[:, :, :], prod[1][:, :, :], sg[:, :, :], ALU.mult).then_inc(evac, 1)
                c.up(evac, 2 * (FI - 1))
                c.up(sig_ready, FI - 1)
                c.up(vec_step, 2 * (FI - 1))
                n_prod[0] += 2 * (FI - 1)
                last = s0 + FFN_SLABS - 1
                dve.wait_ge(slab_done[last % RING], last // RING + 1)
                for j in range(4):
                    pair = x[:, 2 * j:2 * j + 2, :]
                    ins = v.scalar_tensor_tensor(pair, acc[j][:, :, :], 0.5, pair, ALU.mult, ALU.add)
                    if gain is None:
                        ins.then_inc(xg_ready, 1)
                    else:
                        link(ins)
                        for i in range(2):
                            next_norm(2 * j + i, gain)

            def attention(heads, scale, bias=None, sink=None):
                for i in range(heads + 1):
                    if i < heads:
                        st, mx = small[:, i % 2, :], small[:, 2 + i % 2, 0:2]
                        dve.wait_ge(s_done, c.up(s_done))
                        if bias is None:
                            link(v.tensor_reduce(mx, acc[i % 2][:, :, :], AX_X, ALU.max))
                            ins = v.tensor_scalar(st[:, 0:2], mx, -scale, None, ALU.mult)
                        else:
                            b = bias(i)
                            k = b.shape[-1]
                            link(v.scalar_tensor_tensor(logits[i % 2].rearrange("p a (r k) -> p (a r) k", k=k),
                                                        acc[i % 2][:, :, :].rearrange("p a (r k) -> p (a r) k", k=k),
                                                        scale, b, ALU.mult, ALU.add))
                            if sink is not None and i < SWA_HEADS:
                                link(v.tensor_reduce(mx, logits[i % 2], AX_X, ALU.max))
                                ins = v.tensor_scalar(st[:, 0:2], mx, sink(i), -1.0, ALU.max, ALU.mult)
                            else:
                                ins = v.tensor_reduce(st[:, 0:2], logits[i % 2], AX_X, ALU.max, negate=True)
                        ins.then_inc(logits_ready, 1)
                    if i >= 1:
                        h = i - 1
                        st = small[:, h % 2, :]
                        dve.wait_ge(exp_done, c.up(exp_done))
                        if sink is not None and h < SWA_HEADS:
                            link(v.tensor_tensor(st[:, 2:4], st[:, 2:4], st[:, 4:6], ALU.add))
                        link(v.reciprocal(st[:, 6:8], st[:, 2:4]))
                        for tt in range(TT):
                            last = v.tensor_scalar(probs[h % 2][:, tt, :], probs[h % 2][:, tt, :], st[:, 6 + tt:7 + tt],
                                                   None, ALU.mult)
                        last.then_inc(p_ready, 1)

            def head_norm(q, out, gain, width=2 * T):
                y = inverse_root(q, width)
                y = y.rearrange("p (a t) -> p a t", t=T) if width > T else y
                v.scalar_tensor_tensor(out, out, par(gain), y, ALU.mult, ALU.mult).then_inc(norm_ready, 1)
                c.up(norm_ready)

            def hg(s, which, gain):
                token_norm(act3(0))
                for d in range(2):
                    for j in range(4):
                        scaled(gs[:, :, :], product(s + 4 * d + j)[:, :, :])
                        dve.wait_ge(sig_ready, c.up(sig_ready))
                        for i in range(2):
                            h = 2 * j + i
                            last = v.tensor_scalar(hg_f[d][:, h, :], sg[:, i, :], oml[:, which, h:h + 1], lbs[:, which, h:h + 1],
                                                   ALU.mult, ALU.add)
                        link(last)
                        link(v.tensor_scalar((hg_kg, hg_kx)[d][:, 2 * j:2 * j + 2, :], hg_f[d][:, 2 * j:2 * j + 2, :],
                                             -1.0, 1.0, ALU.mult, ALU.add))
                for j in range(4):
                    scaled(hg_q[:, 2 * j:2 * j + 2, :], product(s + 8 + j)[:, :, :], float(D // HG_HEADS) ** -0.5)
                columns()
                v.tensor_tensor(hg_ks, hg_kg, hg_kx, ALU.add).then_inc(tree_ready, 1)
                v.tensor_tensor(hg_qf, hg_q, hg_f[0], ALU.mult).then_inc(vec_step, 1)
                c.up(vec_step)
                v.tensor_tensor(hg_qy, hg_q, hg_f[1], ALU.mult).then_inc(tree_ready, 1)
                dve.wait_ge(tree_ready, c.up(tree_ready, 2))
                flat = [a.rearrange("p c t -> p (c t)") for a in (hg_qf, hg_qy, hg_kg, hg_kx)]
                total = [a.rearrange("p c t -> p (c t)") for a in hg_f]
                spare = region(8)
                dve.wait_ge(tree_done, c.up(tree_done))
                for b in range(4):
                    last = v.tensor_copy(hg_ad[:, 2 * b:2 * b + 2, :], acc[b][:, :, :])
                own(last, tree_taken)
                for n, half in enumerate(HALVES):
                    if n in (0, 2):
                        values(s + 13 + 2 * (n // 2), hg_v, 2 * T, 2 * T * (n // 2))
                    elif n >= 3:
                        scaled(gs[:, :, :], product(s + 16 + n - 3)[:, :, :])
                        dve.wait_ge(sig_ready, c.up(sig_ready))
                        j = n - 3
                        v.tensor_tensor(hg_sg[:, 2 * j:2 * j + 2, :], gs[:, :, :], sg[:, :, :], ALU.mult).then_inc(vec_step, 1)
                        c.up(vec_step)
                    dve.wait_ge(tree_done, c.up(tree_done))
                    mask = con(f"lvl{half}").bitcast(U32).unsqueeze(1).to_broadcast([P, 4, P])
                    for b in range(4):
                        last = v.copy_predicated(halves(hg_ad[:, 2 * b:2 * b + 2, :]), mask, halves(acc[b][:, :, :]))
                    own(last, tree_taken)
                    nb = KC * T // (2 * half)
                    pairs = [t[:, 0:2 * nb].rearrange("p (b two) -> p b two", two=2) for t in total]
                    for a, side, t in ((flat[0], 1, pairs[0]), (flat[1], 0, pairs[1]), (flat[2], 0, pairs[0]), (flat[3], 1, pairs[1])):
                        blocks = a.rearrange("p (b two l) -> p b two l", two=2, l=half)[:, :, side, :]
                        factor = t[:, :, 1 - side].unsqueeze(2).to_broadcast([P, nb, half])
                        last = v.tensor_tensor(blocks, blocks, factor, ALU.mult)
                    own(last, tree_ready)
                    if half < HALVES[-1]:
                        if n % 2 == 0:
                            new = [spare[:, d * 1024:d * 1024 + nb] for d in range(2)]
                        else:
                            new = [hg_f[d].rearrange("p c t -> p (c t)")[:, 0:nb] for d in range(2)]
                        for d in range(2):
                            last = v.tensor_tensor(new[d], pairs[d][:, :, 0], pairs[d][:, :, 1], ALU.mult)
                        link(last)
                        total = new
                dve.wait_ge(tree_done, c.up(tree_done))
                for b in range(4):
                    last = v.tensor_copy(hg_ao[:, 2 * b:2 * b + 2, :], acc[b][:, :, :])
                own(last, tree_taken)
                qs = {}
                for b in range(5):
                    if b < 4:
                        qs[b] = variance(2 * T, P)
                    if b >= 1:
                        a = b - 1
                        y = inverse_root(qs[a], 2 * T).rearrange("p (a t) -> p a t", a=2)
                        link(v.scalar_tensor_tensor(hg_o[:, 2 * a:2 * a + 2, :], acc[a][:, :, :], par(f"hg_g{HG_LAYERS[which]}"), y,
                                                    ALU.mult, ALU.mult))
                        for i in (2 * a, 2 * a + 1):
                            v.tensor_tensor(hg_o[:, i, :], hg_o[:, i, :], hg_sg[:, i, :], ALU.mult).then_inc(mix_ready, 1)
                c.up(sq_ready, 4)
                c.up(mix_ready, KC)
                residual(s + 20, gain)

            def na(s, gain):
                token_norm(act3(0))
                q = 0
                for j in range(9):
                    pair = (na_q if j < 4 else na_k)[:, 2 * (j % 4):2 * (j % 4) + 2, :]
                    if j < 8:
                        scaled(pair, product(s + j)[:, :, :])
                    if j == 8:
                        columns()
                        values(s + 9, na_v, 2 * T, 0)
                    if j >= 1:
                        q = variance(2 * T, NA_DIM)
                        before = (na_q if j - 1 < 4 else na_k)[:, 2 * ((j - 1) % 4):2 * ((j - 1) % 4) + 2, :]
                        head_norm(q, before, "na_q" if j - 1 < 4 else "na_k")
                c.up(sq_ready, 8)
                values(s + 11, na_v, 2 * T, 2 * T)
                dve.wait_ge(bias_ready, NA_HEADS)
                attention(NA_HEADS, NA_DIM ** -0.5, lambda h: backwards(na_b[:, h].rearrange("p a r k -> p (a r) k")))
                residual(s + 12, gain)

            def mla(s, gain):
                token_norm(act3(1))
                for j in range(4):
                    scaled(act3(0)[:, 2 * j:2 * j + 2, :], product(s + j)[:, :, :])
                own(v.tensor_tensor(ml_krr, product()[:, 0, :], rstd[:, :], ALU.mult), evac)
                for name, lat, n in (("mla_qa", ml_cq, MLA_Q), ("mla_kva", ml_ckv, MLA_KV)):
                    q = variance(T, n)
                    y = inverse_root(q, T)
                    for k in range(n // P):
                        last = v.scalar_tensor_tensor(lat[:, k, :], lat[:, k, :], par(name, k), y, ALU.mult, ALU.mult)
                    own(last, norm_ready)
                for j in range(4):
                    own(v.tensor_copy(ml_qn[:, 2 * j:2 * j + 2, :], product(s + 4 + j)[:, :, :]), evac)
                for j in range(2):
                    own(v.tensor_copy(ml_qr[:, 2 * j:2 * j + 2, :], product(s + 8 + j)[:, :, :]), evac)
                for m in range(4):
                    own(v.tensor_copy(ml_kn[:, 2 * m:2 * m + 2, :], product()[:, :, :]), evac)
                    own(v.tensor_copy(ml_v[:, :, m * T:(m + 1) * T], product(None if m % 2 == 0 else s + 10 + m // 2)[:, :, :]), evac)
                c.up(sq_ready, 2)
                dve.wait_ge(sq_ready, c.up(sq_ready, 2))
                for j in range(2):
                    v.tensor_scalar(ml_qr[:, 2 * j:2 * j + 2, :], ml_qr[:, 2 * j:2 * j + 2, :], par("mla_qr"), None, ALU.mult).then_inc(mix_ready, 1)
                v.tensor_scalar(ml_kr[:, 0, :], ml_krr, par("mla_kr"), None, ALU.mult).then_inc(mix_ready, 1)
                dve.wait_ge(mix_ready, c.up(mix_ready, 3))
                for j in range(3):
                    n = 2 if j < 2 else 1
                    src = ml_qr[:, 2 * j:2 * j + 2, :] if j < 2 else ml_kr[:, 0:1, :]
                    dst = src if j < 2 else act3(4)[:, 5:6, :]
                    dve.wait_ge(rot_done, c.up(rot_done))
                    b = prod[n_prod[0] % 2]
                    n_prod[0] += 1
                    own(v.tensor_tensor(gs[:, 0:n, :], b[:, 0:n, :], over(con("sin"), n), ALU.mult), evac)
                    link(v.tensor_tensor(sg[:, 0:n, :], src, over(con("cos"), n), ALU.mult))
                    link(v.tensor_tensor(dst, gs[:, 0:n, :], sg[:, 0:n, :], ALU.add))
                steps = [(keys, r, rope) for keys in range(2) for r in range(4) for rope in range(2)]
                qs = {}
                for i in range(len(steps) + 1):
                    if i < len(steps):
                        qs[i] = variance(T if steps[i][2] else 2 * T, NOPE + ROPE)
                    if i >= 1:
                        keys, r, rope = steps[i - 1]
                        y = inverse_root(qs[i - 1], T if rope else 2 * T)
                        if rope:
                            out = (ml_kr if keys else ml_qr)[:, r, :]
                            last = v.tensor_tensor(out, ml_krot if keys else out, y, ALU.mult)
                        else:
                            out = (ml_kn if keys else ml_qn)[:, 2 * r:2 * r + 2, :]
                            last = v.scalar_tensor_tensor(out, out, par("mla_kn" if keys else "mla_qn"),
                                                          y.rearrange("p (a t) -> p a t", a=2), ALU.mult, ALU.mult)
                        if i < len(steps):
                            link(last)
                        else:
                            own(last, norm_ready)
                c.up(sq_ready, 2)
                attention(MLA_HEADS, (NOPE + ROPE) ** -0.5)
                residual(s + 12, gain)

            def branches(s, l, gain):
                token_norm(act3(2))
                pads = (br_u[:, :, 0:UPAD], br_t[:, :, 0:SPAD])
                for pad in pads:
                    v.memset(pad, 0.0).then_inc(vec_step, 1)
                    c.up(vec_step)
                pairs = [(br_q[:, 0:2, :], f"swq{l}"), (br_k[:, 0:2, :], f"swk{l}"), (br_q[:, 2:4, :], f"fxq{l}"), (br_k[:, 2:4, :], f"fxk{l}")]
                for j in range(5):
                    if j < 4:
                        scaled(pairs[j][0], product(s + j)[:, :, :])
                    else:
                        own(v.tensor_tensor(br_x, product()[0:FOX_HEADS, 0, :], rstd[0:FOX_HEADS, :], ALU.mult), evac)
                    if j >= 1:
                        q = variance(2 * T, 64)
                        head_norm(q, *pairs[j - 1])
                c.up(sq_ready, 4)
                link(v.tensor_scalar(br_x, br_x, par(f"bf{l}", 0, 1, FOX_HEADS), None, ALU.add))
                link(v.tensor_scalar(br_ncum, br_x, -1.0, None, ALU.mult))
                own(v.tensor_tensor(br_cum, br_x, br_ncum, ALU.max), aux_ready)
                dve.wait_ge(log_ready, c.up(log_ready))
                link(v.scalar_tensor_tensor(br_x, br_x, 0.0, br_l, ALU.min, ALU.subtract))
                link(v.tensor_tensor_scan(br_l, con("ones", 0, 1, FOX_HEADS).to_broadcast([FOX_HEADS, T]), br_x, 0.0, ALU.mult, ALU.add))
                v.tensor_scalar(br_cum, br_l, 8.0, None, ALU.mult).then_inc(vec_step, 1)
                c.up(vec_step)
                own(v.tensor_scalar(br_ncum, br_l, -8.0, None, ALU.mult), norm_ready)
                columns()
                values(s + 5, br_v, 3 * P)
                scaled(gs[:, :, :], product(s + 6)[:, :, :])
                dve.wait_ge(sig_ready, c.up(sig_ready))
                link(v.tensor_tensor(sg[:, :, :], sg[:, :, :], over(rstd[:, :], 2), ALU.mult))
                own(v.tensor_tensor(br_u[:, :, UPAD:UPAD + T], product(s + 7)[:, :, :], sg[:, :, :], ALU.mult), evac)
                scaled(hid[:, :, :], product(s + 8)[:, :, :])
                link(v.tensor_tensor(hid[:, :, :], hid[:, :, :], over(rstd[:, :], 2), ALU.mult))
                own(v.tensor_tensor(br_t[:, :, SPAD:SPAD + T], product(s + 9)[:, :, :], hid[:, :, :], ALU.mult), evac)
                scaled(br_sb, product(s + 10)[:, :, :])

                def gate(j):
                    if j >= 2:
                        dve.wait_ge(sig_ready, c.up(sig_ready))
                    scaled((gs, hid)[j % 2][:, :, :], product(s + 11 + j)[:, :, :])

                def tap(out, src, w, k, first_bias=None):
                    for i in range(2):
                        shifted = src[:, i, k:k + T]
                        weight = w(i, k)
                        if k == 0:
                            last = v.tensor_scalar(out[:, i, :], shifted, weight, first_bias(i) if first_bias else 0.0,
                                                   ALU.mult, ALU.add)
                        else:
                            last = v.scalar_tensor_tensor(out[:, i, :], shifted, weight, out[:, i, :], ALU.mult, ALU.add)
                    link(last)

                for j in range(8):
                    gate(j)
                    for k in range(4 * j, min(4 * j + 4, CONV_K)):
                        tap(br_conv, br_u, lambda i, k: par(f"dw{l}", i * CONV_K + k), k, lambda i: par(f"dwb{l}", i))
                v.memset(small[:, 0, 0:1], 0.0).then_inc(mix_ready, 1)
                for k in range(SC_K):
                    tap(br_sco, br_t, lambda i, k: par(f"sc{l}", i * SC_K + k), k)
                own(v.tensor_tensor(br_sco, br_sco, br_sb, ALU.mult), mix_ready)
                c.up(mix_ready)
                dve.wait_ge(toe_ready, TT)
                attention(SWA_HEADS + FOX_HEADS, 64 ** -0.5,
                          lambda h: backwards(toe[:, :, h, :]) if h < SWA_HEADS else con("fxmask").rearrange("p (a t) -> p a t", a=TT),
                          lambda h: par(f"sink{l}", h))
                for j in range(8, 16):
                    gate(j)
                c.up(sig_ready, 2)
                q = n_stat[0] % 2
                n_stat[0] += 1
                dve.wait_ge(stat_done, c.up(stat_done))
                for i in range(2):
                    last = v.scalar_tensor_tensor(br_conv[:, i, :], stat[q][:, 0, :], -1.0 / (2 * P), br_conv[:, i, :], ALU.mult, ALU.add)
                    if i == 0:
                        link(last)
                own(last, var_ready)
                own(v.memset(small[:, 0, 0:1], 0.0), aux_ready)
                q = variance(T, 2 * P)
                y = inverse_root(q, T)
                link(v.tensor_tensor(br_conv, br_conv, over(y, 2), ALU.mult))
                for i in range(2):
                    last = v.tensor_scalar(br_conv[:, i, :], br_conv[:, i, :], par(f"lng{l}", i), par(f"lnb{l}", i), ALU.mult, ALU.add)
                own(last, aux_ready)
                dve.wait_ge(sig_ready, c.up(sig_ready))
                own(v.tensor_tensor(br_cvo, br_conv, sg[:, :, :], ALU.mult), mix_ready)
                c.up(sq_ready)
                for br in range(4):
                    for j in range(4):
                        b = product(None if j < 3 else s + 27 + br)
                        g = br_g[:, 8 * br + 2 * j:8 * br + 2 * j + 2, :]
                        pair = br_m[:, 2 * j:2 * j + 2, :]
                        if br == 0:
                            own(v.tensor_tensor(pair, b[:, :, :], g, ALU.mult), evac)
                        else:
                            own(v.tensor_tensor(gs[:, :, :], b[:, :, :], g, ALU.mult), evac)
                            link(v.tensor_tensor(pair, pair, gs[:, :, :], ALU.add))
                own(v.memset(small[:, 0, 0:1], 0.0), mix_ready)
                residual(s + 31, gain)

            own(v.memset(zero16[:, :], 0.0), zeros_ready)
            dve.wait_ge(inputs_loaded, 48)
            dve.wait_ge(toe_row, 1)
            v.tensor_copy(toe_rows[:, :], acc[0][0:SWA_HEADS, :, :].rearrange("p a t -> p (a t)")).then_inc(toe_rows_done, 1)
            for k in range(KC):
                next_norm(k, "norm0_0")
            n = HG_HEADS
            logit = par("hg_lb", 0, 4 * n)
            high = lbt[:, 4 * n:5 * n]
            link(v.tensor_reduce(high, logit.rearrange("p (l h) -> p h l", l=LAYERS_1), AX_X, ALU.max))
            own(v.tensor_tensor(lbt[:, 0:4 * n].rearrange("p (l h) -> p l h", l=LAYERS_1), logit.rearrange("p (l h) -> p l h", l=LAYERS_1),
                                over(high, LAYERS_1), ALU.subtract), lb_max)
            dve.wait_ge(lb_exp, 1)
            rest, whole = lbt[:, 4 * n:5 * n], lbt[:, 5 * n:6 * n]
            link(v.tensor_tensor(rest, lbt[:, n:2 * n], lbt[:, 2 * n:3 * n], ALU.add))
            link(v.tensor_tensor(rest, rest, lbt[:, 3 * n:4 * n], ALU.add))
            link(v.tensor_tensor(whole, rest, lbt[:, 0:n], ALU.add))
            link(v.reciprocal(whole, whole))
            link(v.tensor_tensor(lbs[:, 1, :], rest, whole, ALU.mult))
            link(v.memset(lbs[:, 0, :], 0.0))
            link(v.tensor_scalar(oml[:, :, :], lbs[:, :, :], -1.0, 1.0, ALU.mult, ALU.add))

            for layer, kind in enumerate(MIXERS):
                s1, sm, s2 = STAGES[layer]
                ffn(s1, f"norm{layer}_1")
                gain = f"norm{layer}_2"
                if kind == "hg":
                    hg(sm, HG_LAYERS.index(layer), gain)
                elif kind == "na":
                    na(sm, gain)
                elif kind == "mla":
                    mla(sm, gain)
                else:
                    branches(sm, layer - LAYERS_1, gain)
                ffn(s2, f"norm{layer + 1}_0" if layer + 1 < len(MIXERS) else None)

        @block.gpsimd
        def _(pool):
            pool.wait_ge(inputs_loaded, 48)
            pool.wait_ge(toe_loaded, 32)
            for tt in range(TT):
                nc.gpsimd.tensor_tensor(toe[:, tt, :, :], toe[:, tt, :, :], over(con("swmask", tt * T, T), SWA_HEADS), ALU.add).then_inc(toe_ready, 1)
            pool.wait_ge(bias_loaded, 16 * 16)
            for h in range(NA_HEADS):
                b = na_b[:, h].rearrange("p a r k -> p (a r) k")
                nc.gpsimd.tensor_tensor(b, b, over(con("namask"), 4 * TT), ALU.add).then_inc(bias_ready, 1)


def tiles(w, k_chunks, width=P):
    K, N = w.shape
    return w.reshape(k_chunks, P, N // width, width).transpose(2, 0, 1, 3)


def fill(stream, s, blocks):
    at = 0
    for b in blocks:
        stream[s, :, at:at + b.shape[1]] = b
        at += b.shape[1]


def features(stream, s, w, k_chunks=KC, per_slab=2):
    t = tiles(w, k_chunks)
    for j in range(0, t.shape[0], per_slab):
        fill(stream, s + j // per_slab, [t[n, k] for n in range(j, j + per_slab) for k in range(k_chunks)])


def token_major(stream, s, w, k_per_slab):
    rows = w.reshape(-1, P, w.shape[1])
    for j in range(0, len(rows), k_per_slab):
        fill(stream, s + j // k_per_slab, list(rows[j:j + k_per_slab]))


def ffn_slabs(stream, s, w_gate, w_up, w_down):
    n = 2 * P
    order = [("g", 0), ("u", 0)]
    for f in range(1, FI):
        order += [("g", f), ("d", f - 1), ("u", f)]
    order += [("d", FI - 1)]
    for i, (kind, f) in enumerate(order):
        if kind == "d":
            t = tiles(w_down[f * n:(f + 1) * n], 2)
            fill(stream, s + i, [t[c, k] for c in range(KC) for k in range(2)])
        else:
            features(stream, s + i, (w_gate if kind == "g" else w_up)[:, f * n:(f + 1) * n])


def constants():
    c = np.zeros((P, N_CONSTS), np.float32)

    def put(name, a):
        at, w = CONSTS[name]
        c[:a.shape[0], at:at + a.shape[1]] = a

    i = np.arange(P)
    t = np.arange(T)
    put("ident", np.eye(P))
    put("ones", np.ones((P, P)))
    put("blk64", (i[:, None] // 64 == i[None] // 64) * 1.0)
    put("blk32", (i[:, None] // 32 == i[None] // 32) * 1.0)
    put("r2n", np.concatenate([(i[:, None] // 32 == 2 * a + i[None] // 64) * 1.0 for a in range(2)], 1))
    put("n2r", np.concatenate([(2 * a + i[:, None] // 64 == i[None] // 32) * 1.0 for a in range(2)], 1))
    half = ROPE // 2
    rot = np.zeros((P, P))
    for o in range(P):
        if o % ROPE < half:
            rot[o + half, o] = -1.0
        else:
            rot[o - half, o] = 1.0
    put("rot", rot)
    freq = np.float32(10000.0) ** (-np.arange(half, dtype=np.float32) / np.float32(half))
    ang = t.astype(np.float32)[None] * freq.astype(np.float32)[:, None]
    put("cos", np.tile(np.cos(ang.astype(np.float32)), (P // half, 1)))
    put("sin", np.tile(np.sin(ang.astype(np.float32)), (P // half, 1)))
    cols = np.arange(GRID_W)
    start = np.clip(cols - NA_WIN_C // 2, 0, GRID_W - NA_WIN_C)
    inside = (cols[None] >= start[:, None]) & (cols[None] < start[:, None] + NA_WIN_C)
    put("namask", np.tile(np.where(inside, 0.0, NEG), (2, 1))[:, ::-1])
    dist = t[:, None] - t[None]
    for name, ok in (("swmask", (dist >= 0) & (dist < P)), ("fxmask", dist >= 0)):
        m = np.where(ok, 0.0, NEG)
        m = m[:, ::-1] if name == "swmask" else m
        put(name, m.reshape(TT, P, T).transpose(1, 0, 2).reshape(P, TT * T))
    exact = BUCKETS // 2
    d = np.arange(T)
    large = exact + (np.log(np.maximum(d, 1).astype(np.float32) / exact) / np.log(MAX_DISTANCE / exact)
                     * (BUCKETS - exact)).astype(np.int32)
    bucket = np.where(d < exact, d, np.minimum(large, BUCKETS - 1))
    hot = np.zeros((BUCKETS, 2 * T))
    for dd in range(P):
        hot[bucket[dd], T - 1 + dd] = 1.0
    put("hot", hot)
    sel = np.zeros((FOX_HEADS, FOX_HEADS, T))
    for h in range(FOX_HEADS):
        sel[h, h] = 1.0
    put("selrow", sel.reshape(FOX_HEADS, -1))
    for h in HALVES:
        put(f"lvl{h}", ((i[:, None] // (2 * h) == i[None] // (2 * h)) & (i[:, None] // h % 2 != i[None] // h % 2)) * 1.0)
    return c


def layout(z):
    stream = np.zeros((SLABS, P, SLAB), np.float32)
    prm = np.zeros((P, N_PARAMS), np.float32)

    def put(name, a):
        at, w = PARAMS[name]
        prm[:a.shape[0], at:at + a.shape[1]] = a

    def by_chunk(a):
        return a.reshape(-1, P).T

    def twice(a):
        return np.concatenate([a, a])[:, None]

    for layer, (s1, sm, s2) in enumerate(STAGES):
        l2 = layer - LAYERS_1
        if l2 < 0:
            for i, name in enumerate(("ffn1_norm", "mix_norm", "ffn2_norm")):
                put(f"norm{layer}_{i}", by_chunk(z[name][layer]))
            for s, n in ((s1, "ffn1"), (s2, "ffn2")):
                gu = z[f"{n}_w_gu"][layer]
                ffn_slabs(stream, s, gu[:, :F], gu[:, F:], z[f"{n}_w_down"][layer])
        else:
            for i, name in enumerate(("ffn1_norm_2", "mix_norm_2", "ffn2_norm_2")):
                put(f"norm{layer}_{i}", by_chunk(z[name][l2]))
            for s, n in ((s1, "ffn1"), (s2, "ffn2")):
                ffn_slabs(stream, s, z[f"{n}_w_gate_2"][l2], z[f"{n}_w_up_2"][l2], z[f"{n}_w_down_2"][l2])
        kind = MIXERS[layer]
        if kind == "hg":
            a = HG_LAYERS.index(layer)
            q, zf, zb, i, g = np.split(z["hg_w_in"][a], 5, axis=1)
            for n, w in enumerate((zf, zb, q)):
                features(stream, sm + 4 * n, w)
            for n in range(2):
                token_major(stream, sm + 12 + 2 * n, i[:, n * 512:(n + 1) * 512], 4)
            features(stream, sm + 16, g)
            features(stream, sm + 20, z["hg_w_out"][a])
            put(f"hg_g{layer}", z["hg_g_norm"][a][:, None])
        elif kind == "na":
            q, k, v = np.split(z["na_w_in"][0], 3, axis=1)
            features(stream, sm, q)
            features(stream, sm + 4, k)
            for n in range(2):
                token_major(stream, sm + 8 + 2 * n, v[:, n * 512:(n + 1) * 512], 4)
            features(stream, sm + 12, z["na_w_out"][0])
        elif kind == "mla":
            w = z["mla_w_in"][0]
            features(stream, sm, w[:, :D])
            put("mla_wr", np.tile(w[:, D:].reshape(KC, P, ROPE), (1, 1, P // ROPE)).transpose(1, 0, 2).reshape(P, KC * P))
            uq = z["mla_w_uq"][0].reshape(MLA_Q, MLA_HEADS, NOPE + ROPE)
            features(stream, sm + 4, uq[:, :, :NOPE].reshape(MLA_Q, -1), MLA_Q // P)
            features(stream, sm + 8, uq[:, :, NOPE:].reshape(MLA_Q, -1), MLA_Q // P)
            ukv = z["mla_w_ukv"][0].reshape(MLA_KV, MLA_HEADS, NOPE + 64)
            kn, vv = tiles(ukv[:, :, :NOPE].reshape(MLA_KV, -1), 2), ukv[:, :, NOPE:].reshape(2, P, -1)
            for j in range(2):
                blocks = []
                for m in (2 * j, 2 * j + 1):
                    blocks += [kn[n, k] for n in (2 * m, 2 * m + 1) for k in range(2)]
                    blocks += [vv[k][:, m * T:(m + 1) * T] for k in range(2)]
                fill(stream, sm + 10 + j, blocks)
            features(stream, sm + 12, z["mla_w_out"][0])
        else:
            w = z["w_in_2"][l2]
            cuts = np.cumsum([256, 256, 256, 256, 256, 256, 128, 128, 256, 256, 256, 4])
            c_a, c_b, s_b, s_c, s_x, a_q, a_k, a_v, f_q, f_k, f_v, f_f, gates = np.split(w, cuts, axis=1)
            kk = a_k.reshape(D, 2, 1, 64)
            features(stream, sm, a_q)
            features(stream, sm + 1, np.concatenate([kk, kk], axis=2).reshape(D, 256))
            features(stream, sm + 2, f_q)
            features(stream, sm + 3, f_k)
            token_major(stream, sm + 4, np.concatenate([a_v, f_v], axis=1), 5)
            for n, a in enumerate((c_b, c_a, s_c, s_x, s_b)):
                features(stream, sm + 6 + n, a)
            g = np.split(gates, 4, axis=1)
            for n, b in enumerate((2, 3, 1, 0)):
                features(stream, sm + 11 + 4 * n, g[b])
            for n, name in enumerate(("swa_w_o_2", "fox_w_o_2", "sc_w_out_2", "conf_w_out_2")):
                features(stream, sm + 27 + n, z[name][l2], 2, 8)
            features(stream, sm + 31, z["w_out_2"][l2])
            put(f"dw{l2}", z["conf_dw_2"][l2].reshape(CONV_K, 2, P).transpose(2, 1, 0).reshape(P, -1))
            put(f"sc{l2}", z["sc_conv_2"][l2].reshape(SC_K, 2, P).transpose(2, 1, 0).reshape(P, -1))
            for n, name in (("dwb", "conf_dw_b_2"), ("lng", "conf_ln_g_2"), ("lnb", "conf_ln_b_2")):
                put(f"{n}{l2}", by_chunk(z[name][l2]))
            for n, name in (("swq", "swa_q_norm_2"), ("swk", "swa_k_norm_2"), ("fxq", "fox_q_norm_2"), ("fxk", "fox_k_norm_2")):
                put(f"{n}{l2}", twice(z[name][l2]))
            put(f"bf{l2}", z["b_forget_2"][l2][:, None])
            put(f"sink{l2}", np.tile(z["swa_sink_2"][l2][None], (P, 1)))
            put(f"wf{l2}", f_f.reshape(KC, P, FOX_HEADS).transpose(1, 0, 2).reshape(P, -1))
    put("hg_lb", by_chunk(z["hg_lb_logits"]))
    put("na_q", twice(z["na_q_norm"][0]))
    put("na_k", twice(z["na_k_norm"][0]))
    put("mla_qa", by_chunk(z["mla_q_a_norm"][0]))
    put("mla_kva", by_chunk(z["mla_kv_a_norm"][0]))
    for n in "qk":
        g = z[f"mla_{n}_norm"][0]
        put(f"mla_{n}n", twice(g[:NOPE]))
        put(f"mla_{n}r", np.tile(g[NOPE:], 4)[:, None])
    put("relb", z["rel_bias_2"])
    return stream, prm


def kernel(**inputs):
    import concourse.bacc as bacc
    from concourse.bass_utils import run_bass_kernel_spmd

    z = {k: np.asarray(a) for k, a in inputs.items()}
    stream, prm = layout(z)
    arrays = {
        "stream": stream,
        "params": prm,
        "consts": constants(),
        "rpb": np.ascontiguousarray(z["na_rpb"][..., ::-1]).reshape(-1),
        "x_in": np.ascontiguousarray(z["x"][0].T.reshape(KC, P, T).transpose(1, 0, 2)),
    }
    nc = bacc.Bacc("TRN2", target_bir_lowering=False, num_devices=1)
    args = [nc.dram_tensor(k, arrays[k].shape, F32, kind="ExternalInput").ap() for k in ("stream", "params", "consts", "rpb", "x_in")]
    out = nc.dram_tensor("x_out", (P, KC, T), F32, kind="ExternalOutput").ap()
    by_distance = nc.dram_tensor("bias_by_distance", (SWA_HEADS, 2 * T), F32, kind="Internal").ap()
    build(nc, *args, out, by_distance)
    r = run_bass_kernel_spmd(nc, [arrays], core_ids=[0])
    y = r.results[0]["x_out"]
    return np.ascontiguousarray(y.transpose(1, 0, 2).reshape(D, T).T)[None]
```

```python
from contextlib import ExitStack

import numpy as np

import concourse.bass as bass
from concourse import mybir

F32 = mybir.dt.float32
F32R = mybir.dt.float32r
BF16 = mybir.dt.bfloat16
U8 = mybir.dt.uint8
ACT = mybir.ActivationFunctionType
ALU = mybir.AluOpType
AX_X = mybir.AxisListType.X

P = 128
T = 256
TT = T // P
D = 1024
KC = D // P
F = 2816
FI = F // (2 * P)
EPS = 1e-6
RAW = 3
HIGH = 3
LOW = 2
TURN = 6
SPARE = 2
TILES = 16
SLAB = TILES * P
NEG = -1e30

HG_HEADS = 8
HG_LAYERS = (0, 3)
HALVES = (1, 2, 4, 8, 16, 32, 64)
NA_HEADS = 16
NA_DIM = 64
GRID_W = 64
NA_WIN_C = 16
NA_RPB = (15, 31)
MLA_HEADS = 16
MLA_Q = 768
MLA_KV = 256
NOPE = 64
ROPE = 32
SWA_HEADS = 4
FOX_HEADS = 4
CONV_K = 31
SC_K = 3
BUCKETS = 32
MAX_DISTANCE = 128
LAYERS_1 = 4
LAYERS_2 = 2

FFN_SLABS = 3 * FI
MIX_SLABS = {"hg": 24, "na": 16, "mla": 17, "branches": 36}
MIXERS = ["hg", "na", "mla", "hg", "branches", "branches"]


def plan():
    at, out = 0, []
    for kind in MIXERS:
        ffn1 = at
        mix = ffn1 + FFN_SLABS
        ffn2 = mix + MIX_SLABS[kind]
        at = ffn2 + FFN_SLABS
        out.append((ffn1, mix, ffn2))
    return out, at


STAGES, SLABS = plan()

PARAMS = {}


def _params():
    at = 0
    for name, width in (
        [(f"norm{l}_{s}", KC) for l in range(LAYERS_1 + LAYERS_2) for s in range(3)]
        + [("hg_lb", LAYERS_1 * HG_HEADS), ("hg_g0", 1), ("hg_g3", 1), ("na_q", 1), ("na_k", 1)]
        + [("mla_qa", MLA_Q // P), ("mla_kva", MLA_KV // P), ("mla_qn", 1), ("mla_qr", 1), ("mla_kn", 1), ("mla_kr", 1)]
        + [(f"{n}{l}", w) for l in range(LAYERS_2) for n, w in (
            ("dw", 2 * CONV_K), ("dwb", 2), ("lng", 2), ("lnb", 2), ("sc", 2 * SC_K), ("swq", 1), ("swk", 1),
            ("fxq", 1), ("fxk", 1), ("bf", 1), ("sink", SWA_HEADS))]
        + [("relb", SWA_HEADS)]
    ):
        PARAMS[name] = (at, width)
        at += width
    return at


N_PARAMS = _params()

CONSTS = {}


def _consts():
    at = 0
    for name, width in (
        [("ident", P), ("ones", P), ("blk64", P), ("r2n", 2 * P), ("n2r", 2 * P), ("blk32", P), ("rot", P)]
        + [("cos", T), ("sin", T), ("namask", GRID_W), ("fxmask", TT * T), ("select", FOX_HEADS)]
    ):
        CONSTS[name] = (at, width)
        at += width
    return at


N_CONSTS = _consts()
HOT, SWMASK = 0, 2 * T
LEVELS = SWMASK + TT * T
N_START = LEVELS + len(HALVES) * P


class Counts(dict):

    def up(self, sem, n=1):
        self[sem] = self.get(sem, 0) + n
        return self[sem]

    def now(self, sem):
        return self.get(sem, 0)


def build(nc, W, PRM, CST, START, RPB, XIN, OUT, TOE_ROWS, TOE):
    ctx = ExitStack()
    with ctx:
        def sb(name, shape, dt=F32):
            return ctx.enter_context(nc.sbuf_tensor(name, shape, dt))

        def sem(name):
            return ctx.enter_context(nc.semaphore(name))

        raw = sb("raw", [P, RAW, SLAB])
        high = sb("high", [P, HIGH, SLAB], F32R)
        low = sb("low", [P, LOW, SLAB], F32R)
        levels = sb("levels", [P, len(HALVES), P], U8)
        prm = sb("prm", [P, N_PARAMS])
        cst = sb("cst", [P, N_CONSTS])
        x = sb("x", [P, KC, T])
        xh = sb("xh", [P, KC, T], F32R)
        xl = sb("xl", [P, KC, T], F32R)
        gs = sb("gs", [P, 2, T])
        sg = sb("sg", [P, 2, T])
        hidh = sb("hidh", [P, 2, T], F32R)
        hidl = sb("hidl", [P, 2, T], F32R)
        rstd = sb("rstd", [P, T])
        rstdT = sb("rstdT", [P, TT])
        var = sb("var", [P, 2, 2 * T])
        guess = sb("guess", [P, 2, 2 * T])
        newt = sb("newt", [P, 2 * T])
        sqsum = newt[:, 0:T]
        hid = newt.rearrange("p (a t) -> p a t", a=2)
        lbs = sb("lbs", [P, 2, HG_HEADS])
        oml = sb("oml", [P, 2, HG_HEADS])
        lbt = sb("lbt", [P, 6 * HG_HEADS])
        zero16 = sb("zero16", [1, 4 * P], BF16)
        small = sb("small", [P, 4, 8])
        work = sb("work", [P, 11 * KC * T])

        acc = [ctx.enter_context(nc.psum_tensor(f"acc{i}", [P, 2, T], F32)) for i in range(4)]
        prod = [ctx.enter_context(nc.psum_tensor(f"prod{i}", [P, 2, T], F32)) for i in range(2)]
        stat = [ctx.enter_context(nc.psum_tensor(f"stat{i}", [P, 2, T], F32)) for i in range(2)]

        slab_loaded = [sem(f"slab_loaded{r}") for r in range(RAW)]
        high_ready = sem("high_ready")
        low_ready = sem("low_ready")
        slab_done = sem("slab_done")
        hid_ready = sem("hid_ready")
        inputs_loaded = sem("inputs_loaded")
        bias_loaded = sem("bias_loaded")
        toe_row = sem("toe_row")
        toe_stored = sem("toe_stored")
        toe_loaded = sem("toe_loaded")
        toe_rows_done = sem("toe_rows_done")
        toe_masked = sem("toe_masked")
        toe_kept = sem("toe_kept")
        zeros_ready = sem("zeros_ready")
        vec_step = sem("vec_step")
        act_step = sem("act_step")
        lb_max = sem("lb_max")
        lb_exp = sem("lb_exp")
        xg_ready = sem("xg_ready")
        evac = sem("evac")
        mid_done = sem("mid_done")
        sig_ready = sem("sig_ready")
        sq_ready = sem("sq_ready")
        sum_ready = sem("sum_ready")
        stat_done = sem("stat_done")
        var_ready = sem("var_ready")
        guess_ready = sem("guess_ready")
        rstd_ready = sem("rstd_ready")
        norm_ready = sem("norm_ready")
        tree_ready = sem("tree_ready")
        tree_done = sem("tree_done")
        tree_taken = sem("tree_taken")
        mix_done = sem("mix_done")
        mix_ready = sem("mix_ready")
        s_done = sem("s_done")
        logits_ready = sem("logits_ready")
        exp_done = sem("exp_done")
        p_ready = sem("p_ready")
        t_done = sem("t_done")
        pt_ready = sem("pt_ready")
        pv_done = sem("pv_done")
        ot_high = sem("ot_high")
        ot_ready = sem("ot_ready")
        aux_ready = sem("aux_ready")
        log_ready = sem("log_ready")
        rot_done = sem("rot_done")
        stored = sem("stored")

        def par(name, i=0, n=1, p=P):
            a, _ = PARAMS[name]
            return prm[0:p, a + i:a + i + n]

        def con(name, i=0, n=None, p=P):
            a, w = CONSTS[name]
            return cst[0:p, a + i:a + i + (w if n is None else n)]

        ident = con("ident")
        ones = con("ones")

        def region(at, n=1):
            return work[:, at * KC * T:(at + n) * KC * T]

        def act3(at):
            return region(at).rearrange("p (c t) -> p c t", c=KC)

        def over(ap, n):
            return ap.unsqueeze(1).to_broadcast([ap.shape[0], n, ap.shape[1]])

        def backwards(ap):
            dims = [list(d) for d in ap.ap]
            step, n = dims[-1]
            dims[-1] = [-step, n]
            return bass.AP(tensor=ap.tensor, offset=ap.offset + step * (n - 1), ap=dims)

        def tile_of(s, j, n=1):
            return high[:, s % HIGH, j * P:(j + n) * P], low[:, s % LOW, j * P:(j + n) * P]

        def halves(ap):
            return ap.rearrange("p a (b t) -> p (a b) t", b=2)

        def half64(h):
            return slice(64 * (h % 2), 64 * (h % 2) + 64)

        def part32(h):
            return slice(32 * (h % 4), 32 * (h % 4) + 32)

        hg_q, hg_qf, hg_qy = act3(0), act3(1), act3(2)
        hg_kg, hg_kx = act3(3), act3(4)
        hg_f = (act3(5), act3(6))
        hg_ad, hg_ao = act3(7), act3(8)
        hg_ks = act3(8)
        hg_v = region(9).rearrange("p (a n) -> p a n", a=TT)
        hg_sg = act3(10)
        hg_o, hg_sq = act3(0), act3(3)

        at_buf = region(9, 2)
        logits = [at_buf[:, i * 512:(i + 1) * 512].rearrange("p (a t) -> p a t", a=TT) for i in range(2)]
        probs = [at_buf[:, (2 + i) * 512:(3 + i) * 512].rearrange("p (a t) -> p a t", a=TT) for i in range(2)]
        probsT = [at_buf[:, (4 + i) * 512:(5 + i) * 512].rearrange("p (a t) -> p a t", a=TT) for i in range(2)]
        squares = [region(3)[:, i * 512:(i + 1) * 512].rearrange("p (a t) -> p a t", a=2) for i in range(2)]

        na_q, na_k = act3(0), act3(1)
        na_v = region(2).rearrange("p (a n) -> p a n", a=TT)
        na_b = region(4, 4).rearrange("p (h a r k) -> p h a r k", h=NA_HEADS, a=TT, r=4)

        ml_cq, ml_ckv, ml_sq = act3(0)[:, 0:6, :], act3(0)[:, 6:8, :], act3(1)
        ml_qn, ml_kn = act3(2), act3(5)
        ml_qr, ml_kr = act3(3)[:, 0:4, :], act3(3)[:, 4:8, :]
        ml_krr, ml_sqr, ml_krot = act3(4)[:, 0, :], act3(4)[:, 1:5, :], act3(4)[:, 5, :]
        ml_v = region(6).rearrange("p (a n) -> p a n", a=TT)
        ml_sqn = act3(7)

        br_q, br_k = act3(0)[:, 0:4, :], act3(0)[:, 4:8, :]
        br_v = region(1)[:, 0:TT * 3 * P].rearrange("p (a n) -> p a n", a=TT)
        br_conv = region(1)[:, 768:1280].rearrange("p (a t) -> p a t", a=2)
        br_sq = region(1)[:, 1280:1792].rearrange("p (a t) -> p a t", a=2)
        UPAD, SPAD = CONV_K - 1, SC_K - 1
        br_u = region(2)[:, 0:2 * (T + UPAD)].rearrange("p (a t) -> p a t", a=2)
        br_t = region(2)[:, 572:572 + 2 * (T + SPAD)].rearrange("p (a t) -> p a t", a=2)
        br_sb = region(2)[:, 1088:1600].rearrange("p (a t) -> p a t", a=2)
        br_x, br_l, br_cum, br_ncum = (region(3)[0:FOX_HEADS, 1024 + i * T:1024 + (i + 1) * T] for i in range(4))
        br_g = region(4, 4).rearrange("p (c t) -> p c t", t=T)
        br_m = act3(9)
        br_sc = region(10)[:, 1024:1536].rearrange("p (a t) -> p a t", a=2)
        toe = region(8).rearrange("p (a h t) -> p a h t", a=TT, h=SWA_HEADS)
        toe_rows = region(2)[0:SWA_HEADS, 0:2 * T]
        start_const = region(1)[:, 0:N_START]

        block = ctx.enter_context(nc.Block())

        @block.sync
        def _(sp):
            sp.dma_start(prm[:, :], PRM).then_inc(inputs_loaded, 16)
            sp.dma_start(x[:, :, :], XIN).then_inc(inputs_loaded, 16)
            sp.dma_start(cst[:, :], CST).then_inc(inputs_loaded, 16)
            sp.dma_start(start_const, START).then_inc(inputs_loaded, 16)
            for r in range(RAW):
                sp.dma_start(raw[:, r, :], W[r]).then_inc(slab_loaded[r], 16)
            rounds = (SLABS + SPARE) // RAW
            with sp.Fori(1, rounds) as i:
                for r in range(RAW):
                    sp.wait_ge(low_ready, i * RAW + (r - RAW + 1))
                    sp.dma_start(raw[:, r, :], W[bass.ds(i * RAW + r, 1)].rearrange("a p n -> p (a n)")).then_inc(slab_loaded[r], 16)
            for s in range(rounds * RAW, SLABS + SPARE):
                sp.wait_ge(low_ready, s - RAW + 1)
                sp.dma_start(raw[:, s % RAW, :], W[s]).then_inc(slab_loaded[s % RAW], 16)
            sp.wait_ge(xg_ready, KC * (3 * len(MIXERS)) + 4)
            sp.dma_start(OUT, x[:, :, :]).then_inc(stored, 16)
            sp.wait_ge(stored, 16)

        @block.tensor
        def _(pe):
            c = Counts()
            n_prod = [0]
            n_stat = [0]

            def slab_in(s):
                pe.wait_ge(low_ready, s + 1)

            def three(out, w, a, start, stop, **kw):
                (wh, wl), (ah, al) = w, a
                nc.tensor.matmul(out, wh, ah, start=start, stop=False, **kw)
                nc.tensor.matmul(out, wh, al, start=False, stop=False, **kw)
                return nc.tensor.matmul(out, wl, ah, start=False, stop=stop, **kw)

            def operand(k):
                return xh[:, k, :], xl[:, k, :]

            def bank():
                n = n_prod[0]
                n_prod[0] += 1
                if n >= 2:
                    pe.wait_ge(evac, n - 1)
                return prod[n % 2]

            def stat_bank():
                n = n_stat[0]
                n_stat[0] += 1
                if n >= 2:
                    pe.wait_ge(var_ready, n - 1)
                return stat[n % 2]

            def chunks(out, s, rhs, n_chunks=2, k_chunks=KC, first=0, wait=None, width=P):
                for n in range(n_chunks):
                    for k in range(k_chunks):
                        if wait is not None and n == 0:
                            pe.wait_ge(wait, c.up(wait))
                        last = three(out[:, n, :], tile_of(s, first + n * k_chunks + k), rhs(k), k == 0, k == k_chunks - 1)
                return last

            def stats(lhs_rhs, n=T):
                b = stat_bank()
                out = b[:, :, :].rearrange("p a t -> p (a t)")[:, 0:n]
                for i, (lhs, rhs) in enumerate(lhs_rhs):
                    last = nc.tensor.matmul(out, lhs, rhs, start=(i == 0), stop=(i == len(lhs_rhs) - 1))
                last.then_inc(stat_done, 1)

            def token_stats():
                pe.wait_ge(sum_ready, c.up(sum_ready))
                stats([(ones, sqsum)])
                c.up(rstd_ready)
                c.up(sq_ready)

            def token_columns():
                pe.wait_ge(rstd_ready, c.now(rstd_ready))
                b = stat_bank()
                for tt in range(TT):
                    last = nc.tensor.matmul(b[:, 0, tt:tt + 1], rstd[0:1, tt * P:(tt + 1) * P], ones[0:1, 0:1],
                                            start=True, stop=True)
                last.then_inc(stat_done, 1)

            def project(s, rhs=operand, **kw):
                slab_in(s)
                chunks(bank(), s, rhs, **kw).then_inc(slab_done, 1)

            def project_tokens(s, n_slabs, cols, k_per_slab):
                out = [bank() for _ in range(TT)]
                k = 0
                for j in range(n_slabs):
                    slab_in(s + j)
                    ks = list(range(k, min(k + k_per_slab, KC)))
                    for i, kk in enumerate(ks):
                        for tt in range(TT):
                            tok = slice(tt * P, (tt + 1) * P)
                            w = (high[:, (s + j) % HIGH, i * cols:(i + 1) * cols], low[:, (s + j) % LOW, i * cols:(i + 1) * cols])
                            last = three(out[tt][:, :, :].rearrange("p a t -> p (a t)")[:, 0:cols],
                                         (xh[:, kk, tok], xl[:, kk, tok]), w, kk == 0, kk == KC - 1)
                    last.then_inc(slab_done, 1)
                    k += len(ks)

            def ffn(s0):
                def gate(out, s, wait=None):
                    return chunks(out, s, operand, wait=wait)

                def down(s):
                    for n in range(KC):
                        for k in range(2):
                            last = three(acc[n // 2][:, n % 2, :], tile_of(s, 2 * n + k), (hidh[:, k, :], hidl[:, k, :]),
                                         False, True, skip_group_check=True)
                    return last

                base, hids = n_prod[0], c.now(hid_ready)
                assert base % 2 == 0
                if base:
                    pe.wait_ge(evac, base)
                slab_in(s0)
                gate(prod[0], s0, wait=xg_ready).then_inc(slab_done, 1)
                token_stats()
                for i in range(4):
                    nc.tensor.matmul(acc[i][:, :, :], zero16[:, 0:P], zero16[:, 0:2 * T], start=True, stop=True,
                                     skip_group_check=True)
                slab_in(s0 + 1)
                gate(prod[1], s0 + 1).then_inc(slab_done, 1)
                with pe.Fori(0, (FI - 1) // 2) as i:
                    for u in range(2):
                        s = s0 + 2 + 3 * u
                        pe.wait_ge(low_ready, i * TURN + (s + 1))
                        pe.wait_ge(evac, i * 4 + (base + 2 * u + 1))
                        gate(prod[0], s).then_inc(slab_done, 1)
                        pe.wait_ge(low_ready, i * TURN + (s + 2))
                        pe.wait_ge(hid_ready, i * 2 + (hids + u + 1))
                        down(s + 1).then_inc(slab_done, 1)
                        pe.wait_ge(low_ready, i * TURN + (s + 3))
                        gate(prod[1], s + 2).then_inc(slab_done, 1)
                n_prod[0] += 2 * FI
                slab_in(s0 + FFN_SLABS - 1)
                pe.wait_ge(hid_ready, c.up(hid_ready, FI))
                down(s0 + FFN_SLABS - 1).then_inc(slab_done, 1)

            def out_projection(s):
                for j in range(4):
                    project(s + j)

            def attention(heads, scores, values):
                for i in range(heads + 2):
                    if i < heads:
                        for tt in range(TT):
                            pairs = scores(i, tt)
                            for n, (lhs, rhs) in enumerate(pairs):
                                last = nc.tensor.matmul(acc[i % 2][:, tt, :], lhs, rhs, start=(n == 0),
                                                        stop=(n == len(pairs) - 1))
                        last.then_inc(s_done, 1)
                    if 1 <= i <= heads:
                        h = i - 1
                        pe.wait_ge(p_ready, c.up(p_ready))
                        for kt in range(TT):
                            for tt in range(TT):
                                last = nc.tensor.transpose(acc[2 + h % 2][:, kt, tt * P:(tt + 1) * P],
                                                           probs[h % 2][:, tt, kt * P:(kt + 1) * P], ident)
                        last.then_inc(t_done, 1)
                    if i >= 2:
                        h = i - 2
                        if h % 2 == 0 and h >= 4:
                            pe.wait_ge(ot_ready, ot_base + h // 2 - 1)
                        pe.wait_ge(pt_ready, c.up(pt_ready))
                        half = slice(64 * (h % 2), 64 * (h % 2) + 64)
                        for kt in range(TT):
                            last = nc.tensor.matmul(stat[h // 2 % 2][half, 0, :], values(h, kt), probsT[h % 2][:, kt, :],
                                                    start=(kt == 0), stop=(kt == TT - 1))
                        last.then_inc(pv_done, 1)

            def hg(s):
                project(s, wait=xg_ready)
                token_stats()
                for j in range(1, 12):
                    project(s + j)
                token_columns()
                pe.wait_ge(tree_ready, c.up(tree_ready))
                for h in range(HG_HEADS):
                    for tt in range(TT):
                        tok = slice(tt * P, (tt + 1) * P)
                        last = nc.tensor.matmul(acc[h // 2][:, h % 2, tok], hg_ks[:, h, tok], hg_q[:, h, tok],
                                                start=True, stop=True)
                last.then_inc(tree_done, 1)
                for n, half in enumerate(HALVES):
                    if n in (0, 2):
                        project_tokens(s + 12 + 2 * (n // 2), 2, 2 * T, 4)
                    elif n >= 3:
                        project(s + 16 + n - 3)
                    pe.wait_ge(tree_ready, c.up(tree_ready))
                    pe.wait_ge(tree_taken, c.up(tree_taken))
                    for h in range(HG_HEADS):
                        for tt in range(TT):
                            tok = slice(tt * P, (tt + 1) * P)
                            o4 = acc[h // 2][:, h % 2, tok].rearrange("p (b two l) -> p b two l", two=2, l=half)
                            for keys, queries, side in ((hg_kg, hg_qf, 1), (hg_kx, hg_qy, 0)):
                                q4 = queries[:, h, tok].rearrange("p (b two l) -> p b two l", two=2, l=half)
                                last = nc.tensor.matmul(o4[:, :, side, :], keys[:, h, tok], q4[:, :, side, :],
                                                        start=True, stop=True, skip_group_check=True)
                    last.then_inc(tree_done, 1)
                pe.wait_ge(tree_ready, c.up(tree_ready))
                pe.wait_ge(tree_taken, c.up(tree_taken))
                lo, hi = slice(0, P), slice(P, T)
                for h in range(HG_HEADS):
                    nc.tensor.matmul(acc[h // 2][:, h % 2, hi], hg_kg[:, h, lo], hg_qf[:, h, hi], start=True, stop=True)
                    last = nc.tensor.matmul(acc[h // 2][:, h % 2, lo], hg_kx[:, h, hi], hg_qy[:, h, lo], start=True, stop=True)
                last.then_inc(tree_done, 1)
                pe.wait_ge(tree_taken, c.up(tree_taken))
                for b in range(4):
                    for h in (2 * b, 2 * b + 1):
                        for tt in range(TT):
                            tok = slice(tt * P, (tt + 1) * P)
                            nc.tensor.matmul(acc[b][:, h % 2, tok], hg_v[:, tt, h * P:(h + 1) * P], hg_ad[:, h, tok],
                                             start=True, stop=False)
                            last = nc.tensor.matmul(acc[b][:, h % 2, tok], hg_v[:, 1 - tt, h * P:(h + 1) * P],
                                                    hg_ao[:, h, tok], start=False, stop=True)
                    last.then_inc(mix_done, 1)
                for b in range(4):
                    pe.wait_ge(sq_ready, c.up(sq_ready))
                    stats([(ones, hg_sq[:, 2 * b:2 * b + 2, :])], 2 * T)
                project(s + 20, wait=mix_ready)
                for j in range(1, 4):
                    project(s + 20 + j)

            def head_stats(j):
                pe.wait_ge(sq_ready, c.up(sq_ready))
                stats([(con("blk64"), squares[j % 2][:, :, :])], 2 * T)

            def na(s):
                project(s, wait=xg_ready)
                token_stats()
                for j in range(1, 8):
                    project(s + j)
                    head_stats(j - 1)
                token_columns()
                for g in range(2):
                    project_tokens(s + 8 + 2 * g, 2, 2 * T, 4)
                    if g == 0:
                        head_stats(7)
                pe.wait_ge(norm_ready, c.up(norm_ready, 8))
                attention(NA_HEADS,
                          lambda h, tt: [(na_q[half64(h), h // 2, tt * P:(tt + 1) * P], na_k[half64(h), h // 2, :])],
                          lambda h, kt: na_v[:, kt, h * NA_DIM:(h + 1) * NA_DIM])
                pe.wait_ge(ot_ready, ot_base + NA_HEADS // 2)
                out_projection(s + 12)

            def mla(s):
                project(s, wait=xg_ready)
                token_stats()
                for j in range(1, 4):
                    project(s + j)
                project(s + 4, n_chunks=1)
                for n in (MLA_Q // P, MLA_KV // P):
                    pe.wait_ge(sq_ready, c.up(sq_ready))
                    at = 0 if n == MLA_Q // P else MLA_Q // P
                    stats([(ones, ml_sq[:, at + i, :]) for i in range(n)])
                pe.wait_ge(norm_ready, c.up(norm_ready))
                for j in range(6):
                    project(s + 5 + j, k_chunks=6)
                pe.wait_ge(norm_ready, c.up(norm_ready))
                for j in range(2):
                    slab_in(s + 11 + j)
                    for u in range(2):
                        chunks(bank(), s + 11 + j, lambda k: operand(6 + k), k_chunks=2, first=8 * u).then_inc(mid_done, 1)
                        b = bank()
                        for tt in range(TT):
                            tok = slice(tt * P, (tt + 1) * P)
                            for k in range(2):
                                last = three(b[:, tt, :], (xh[:, 6 + k, tok], xl[:, 6 + k, tok]),
                                             tile_of(s + 11 + j, 8 * u + 4 + 2 * k, 2), k == 0, k == 1)
                        last.then_inc(mid_done if u == 0 else slab_done, 1)
                for pair in range(3):
                    pe.wait_ge(mix_ready, c.up(mix_ready))
                    b = bank()
                    n = 2 if pair < 2 else 1
                    for i in range(n):
                        src = ml_qr[:, 2 * pair + i, :] if pair < 2 else ml_kr[:, 0, :]
                        last = nc.tensor.matmul(b[:, i, :], con("rot"), src, start=True, stop=True)
                    last.then_inc(rot_done, 1)
                for keys in (False, True):
                    sn, sr = (ml_sqn, ml_sqr)
                    pe.wait_ge(sq_ready, c.up(sq_ready, 2))
                    for r in range(4):
                        b = stat_bank()
                        rope_sq = sr[:, 0 if keys else r, :]
                        for i in range(2):
                            nc.tensor.matmul(b[:, i, :], con("blk64"), sn[:, 2 * r + i, :], start=True, stop=False)
                            last = nc.tensor.matmul(b[:, i, :], con("r2n", i * P, P), rope_sq, start=False, stop=True)
                        last.then_inc(stat_done, 1)
                        b = stat_bank()
                        nc.tensor.matmul(b[:, 0, :], con("blk32"), rope_sq, start=True, stop=False)
                        for i in range(2):
                            last = nc.tensor.matmul(b[:, 0, :], con("n2r", i * P, P), sn[:, 2 * r + i, :],
                                                    start=False, stop=(i == 1))
                        last.then_inc(stat_done, 1)
                pe.wait_ge(norm_ready, c.up(norm_ready))
                attention(MLA_HEADS,
                          lambda h, tt: [(ml_qn[half64(h), h // 2, tt * P:(tt + 1) * P], ml_kn[half64(h), h // 2, :]),
                                         (ml_qr[part32(h), h // 4, tt * P:(tt + 1) * P], ml_kr[part32(h), h // 4, :])],
                          lambda h, kt: ml_v[:, kt, h * 64:(h + 1) * 64])
                pe.wait_ge(ot_ready, ot_base + MLA_HEADS // 2)
                out_projection(s + 13)

            def branches(s):
                project(s, wait=xg_ready)
                token_stats()
                for j in range(1, 4):
                    project(s + j)
                    head_stats(j - 1)
                project(s + 4, n_chunks=1)
                head_stats(3)
                token_columns()
                project_tokens(s + 5, 2, 3 * P, 5)
                for j in range(5 + 16):
                    project(s + 7 + j)
                pe.wait_ge(norm_ready, c.up(norm_ready, 5))
                pe.wait_ge(mix_ready, c.up(mix_ready))
                stats([(ones, br_conv[:, i, :]) for i in range(2)])
                pe.wait_ge(sq_ready, c.up(sq_ready))
                stats([(ones, br_sq[:, i, :]) for i in range(2)])
                pe.wait_ge(var_ready, n_stat[0])
                attention(SWA_HEADS + FOX_HEADS, br_scores, br_values)
                pe.wait_ge(ot_ready, ot_base + (SWA_HEADS + FOX_HEADS) // 2)
                for br in range(4):
                    if br >= 2:
                        pe.wait_ge(mix_ready, c.up(mix_ready))
                    slab_in(s + 28 + br)
                    for j in range(4):
                        last = chunks(bank(), s + 28 + br, lambda k: operand(2 * br + k), k_chunks=2, first=4 * j)
                        if j < 3:
                            last.then_inc(mid_done, 1)
                    last.then_inc(slab_done, 1)
                project(s + 32, wait=mix_ready)
                for j in range(1, 4):
                    project(s + 32 + j)

            def br_scores(h, tt):
                tok = slice(tt * P, (tt + 1) * P)
                if h < SWA_HEADS:
                    return [(br_q[half64(h), h // 2, tok], br_k[half64(h), h // 2, :])]
                g = h - SWA_HEADS
                return [(br_q[half64(g), 2 + g // 2, tok], br_k[half64(g), 2 + g // 2, :]),
                        (br_cum[0:FOX_HEADS, tok], con("select", g, 1, FOX_HEADS).to_broadcast([FOX_HEADS, T])),
                        (con("select", g, 1, FOX_HEADS).to_broadcast([FOX_HEADS, P]), br_ncum[0:FOX_HEADS, :])]

            def br_values(h, kt):
                if h < SWA_HEADS:
                    return br_v[:, kt, (h // 2) * 64:(h // 2) * 64 + 64]
                return br_v[:, kt, P + (h - SWA_HEADS) * 64:P + (h - SWA_HEADS) * 64 + 64]

            pe.wait_ge(inputs_loaded, 64)
            nc.tensor.matmul(acc[0][0:SWA_HEADS, :, :].rearrange("p a t -> p (a t)"), par("relb", 0, SWA_HEADS, BUCKETS),
                             start_const[0:BUCKETS, HOT:HOT + 2 * T], start=True, stop=True).then_inc(toe_row, 1)
            pe.wait_ge(zeros_ready, 1)
            ot_base = 0
            for layer, kind in enumerate(MIXERS):
                s1, sm, s2 = STAGES[layer]
                ffn(s1)
                {"hg": hg, "na": na, "mla": mla, "branches": branches}[kind](sm)
                ot_base += {"hg": 0, "na": 8, "mla": 8, "branches": 4}[kind]
                ffn(s2)

        @block.scalar
        def _(act):
            c = Counts()
            table = [None]
            n_stat = [0]

            def tables(name):
                if table[0] != name:
                    table[0] = name
                    act.preload_act_table_set(name)

            def root(width):
                tables("natural_log_exp_and_others")
                q = n_stat[0] % 2
                n_stat[0] += 1
                act.wait_ge(var_ready, c.up(var_ready))
                nc.scalar.activation(guess[:, q, 0:width], var[:, q, 0:width], ACT.Ln).then_inc(act_step, 1)
                act.wait_ge(act_step, c.up(act_step))
                nc.scalar.activation(guess[:, q, 0:width], guess[:, q, 0:width], ACT.Exp, scale=-0.5).then_inc(guess_ready, 1)

            def split(s, i=None, turn=0):
                at = s if i is None else i * TURN + s
                loads = 16 * (s // RAW + 1)
                act.wait_ge(slab_loaded[s % RAW], loads if i is None else i * (16 * TURN // RAW) + loads)
                if s >= HIGH:
                    act.wait_ge(slab_done, at + (1 - HIGH))
                nc.scalar.activation(high[:, s % HIGH, :], raw[:, s % RAW, :], ACT.Copy).then_inc(high_ready, 1)

            def ahead(s, n=1):
                for j in range(s + HIGH, s + n + HIGH):
                    if j < SLABS + SPARE:
                        split(j)

            def skip_stat():
                n_stat[0] += 1
                c.up(var_ready)

            def square(out, src):
                nc.scalar.activation(out, src, ACT.Square).then_inc(sq_ready, 1)

            def token_norm(scratch):
                act.wait_ge(xg_ready, c.up(xg_ready, KC))
                square(scratch, x[:, :, :])
                root(T)

            def sigmoid(out, src):
                tables("sigmoid_and_others")
                act.wait_ge(evac, c.up(evac))
                nc.scalar.activation(out, src, ACT.Sigmoid).then_inc(sig_ready, 1)

            def ffn(s0, between=None):
                token_norm(act3(0))
                sigmoid(sg[:, :, :], gs[:, :, :])
                ahead(s0, 2)
                if between:
                    between()
                base = c.now(evac)
                with act.Fori(0, (FI - 1) // 2) as i:
                    for u in range(2):
                        act.wait_ge(evac, i * 4 + (base + 2 * u + 2))
                        nc.scalar.activation(sg[:, :, :], gs[:, :, :], ACT.Sigmoid).then_inc(sig_ready, 1)
                        for n in range(3):
                            split(s0 + 2 + 3 * u + n + HIGH, i)
                c.up(evac, 2 * FI - 1)
                ahead(s0 + FFN_SLABS - 1)

            def attention(heads, scale, sink=None):
                tables("natural_log_exp_and_others")
                for i in range(heads + 2):
                    if i < heads:
                        act.wait_ge(logits_ready, c.up(logits_ready))
                        st = small[:, i % 2, :]
                        src = acc[i % 2] if scale else logits[i % 2]
                        for tt in range(TT):
                            last = nc.scalar.activation(probs[i % 2][:, tt, :], src[:, tt, :], ACT.Exp, bias=st[:, tt:tt + 1],
                                                        scale=scale or 1.0, accum_out=st[:, 2 + tt:3 + tt])
                        if sink is not None and i < SWA_HEADS:
                            last = nc.scalar.activation(st[:, 4:6], st[:, 0:2], ACT.Exp, bias=sink(i))
                        last.then_inc(exp_done, 1)
                    if 1 <= i <= heads:
                        act.wait_ge(t_done, c.up(t_done))
                        nc.scalar.activation(probsT[(i - 1) % 2][:, :, :], acc[2 + (i - 1) % 2][:, :, :], ACT.Copy).then_inc(pt_ready, 1)
                    if i >= 2:
                        act.wait_ge(pv_done, c.up(pv_done))
                        if i % 2:
                            pair = (i - 2) // 2
                            nc.scalar.activation(xh[:, pair, :], stat[pair % 2][:, 0, :], ACT.Copy).then_inc(ot_high, 1)

            def hg(s):
                token_norm(act3(0))
                for j in range(8):
                    sigmoid(sg[:, :, :], gs[:, :, :])
                    ahead(s + j)
                c.up(evac, 4)
                skip_stat()
                c.up(evac, 4)
                ahead(s + 8, 8)
                for j in range(4):
                    sigmoid(sg[:, :, :], gs[:, :, :])
                    ahead(s + 16 + j)
                for b in range(4):
                    act.wait_ge(mix_done, c.up(mix_done))
                    square(hg_sq[:, 2 * b:2 * b + 2, :], acc[b][:, :, :])
                for b in range(4):
                    root(2 * T)
                c.up(evac, 4)
                ahead(s + 20, 4)

            def head_square(j, src):
                act.wait_ge(evac, c.up(evac))
                square(squares[j % 2][:, :, :], src)

            def na(s):
                act.wait_ge(xg_ready, c.now(xg_ready) + KC)
                for r in range(4):
                    tt, rr = r // 2, r % 2
                    for key_row in range(4):
                        src = bass.AP(tensor=RPB.tensor, offset=(7 - r + key_row) * NA_RPB[1] + NA_WIN_C - GRID_W,
                                      ap=[[1, GRID_W], [NA_RPB[0] * NA_RPB[1], NA_HEADS], [1, GRID_W]])
                        act.dma_start(na_b[rr * GRID_W:(rr + 1) * GRID_W, :, tt, key_row, :], src).then_inc(bias_loaded, 16)
                token_norm(act3(0))
                for j in range(9):
                    if j < 8:
                        head_square(j, (na_q if j < 4 else na_k)[:, 2 * (j % 4):2 * (j % 4) + 2, :])
                        ahead(s + j)
                    if j == 8:
                        skip_stat()
                    if j >= 1:
                        root(2 * T)
                c.up(evac, 4)
                ahead(s + 8, 4)
                attention(NA_HEADS, None)
                c.up(evac, 4)
                ahead(s + 12, 4)

            def mla(s):
                token_norm(act3(1))
                ahead(s, 2)
                act.wait_ge(evac, c.up(evac, 3))
                square(ml_sq[:, 0:6, :], ml_cq)
                ahead(s + 2)
                act.wait_ge(evac, c.up(evac, 1))
                square(ml_sq[:, 6:8, :], ml_ckv)
                ahead(s + 3, 2)
                c.up(evac)
                root(T)
                root(T)
                ahead(s + 5, 3)
                act.wait_ge(evac, c.up(evac, 4))
                square(ml_sqn, ml_qn)
                ahead(s + 8, 2)
                act.wait_ge(evac, c.up(evac, 2))
                square(ml_sqr, ml_qr)
                ahead(s + 10, 3)
                c.up(evac, 8 + 3)
                for keys in (False, True):
                    if keys:
                        act.wait_ge(stat_done, n_stat[0])
                        square(ml_sqn, ml_kn)
                        square(ml_sqr[:, 0, :], ml_krr)
                    for r in range(4):
                        root(2 * T)
                        root(T)
                attention(MLA_HEADS, (NOPE + ROPE) ** -0.5)
                c.up(evac, 4)
                ahead(s + 13, 4)

            def branches(s, l):
                act.wait_ge(xg_ready, c.now(xg_ready) + KC)
                act.wait_ge(toe_kept, 16)
                act.dma_start(toe, TOE).then_inc(toe_loaded, 16)
                token_norm(act3(2))
                for j in range(5):
                    if j < 4:
                        head_square(j, (br_q[:, 0:2, :], br_k[:, 0:2, :], br_q[:, 2:4, :], br_k[:, 2:4, :])[j])
                        ahead(s + j)
                    if j >= 1:
                        root(2 * T)
                act.wait_ge(aux_ready, c.up(aux_ready))
                nc.scalar.activation(br_l, br_cum, ACT.Exp, scale=-1.0).then_inc(act_step, 1)
                act.wait_ge(act_step, c.up(act_step))
                nc.scalar.activation(br_l, br_l, ACT.Ln, bias=con("ones", 0, 1, FOX_HEADS)).then_inc(log_ready, 1)
                c.up(evac, 1)
                skip_stat()
                c.up(evac, 2)
                ahead(s + 4, 3)
                sigmoid(sg[:, :, :], gs[:, :, :])
                ahead(s + 7, 5)
                c.up(evac, 4)
                for j in range(16):
                    sigmoid(br_g[:, 2 * j:2 * j + 2, :], (gs, hid)[j % 2][:, :, :])
                    ahead(s + 12 + j)
                skip_stat()
                act.wait_ge(aux_ready, c.up(aux_ready))
                square(br_sq, br_conv)
                root(T)
                tables("sigmoid_and_others")
                act.wait_ge(aux_ready, c.up(aux_ready))
                nc.scalar.activation(sg[:, :, :], br_conv, ACT.Sigmoid).then_inc(sig_ready, 1)
                attention(SWA_HEADS + FOX_HEADS, None, lambda h: par(f"sink{l}", h))
                c.up(evac, 16 + 4)
                ahead(s + 28, 8)

            def shifted_rows():
                act.wait_ge(toe_stored, 16)
                for tt in range(TT):
                    src = bass.AP(tensor=TOE_ROWS.tensor, offset=tt * P, ap=[[1, P], [2 * T, SWA_HEADS], [1, T]])
                    act.dma_start(toe[:, tt, :, :], src).then_inc(toe_loaded, 16)

            for r in range(HIGH):
                split(r)
            act.wait_ge(toe_rows_done, 1)
            act.dma_start(TOE_ROWS, toe_rows).then_inc(toe_stored, 16)
            tables("natural_log_exp_and_others")
            act.wait_ge(lb_max, 1)
            nc.scalar.activation(lbt[:, 0:4 * HG_HEADS], lbt[:, 0:4 * HG_HEADS], ACT.Exp).then_inc(lb_exp, 1)
            for layer, kind in enumerate(MIXERS):
                s1, sm, s2 = STAGES[layer]
                ffn(s1, shifted_rows if layer == 0 else None)
                if layer == 0:
                    act.wait_ge(toe_masked, TT)
                    act.dma_start(TOE, toe).then_inc(toe_kept, 16)
                if kind == "branches":
                    branches(sm, layer - LAYERS_1)
                else:
                    {"hg": hg, "na": na, "mla": mla}[kind](sm)
                ffn(s2)

        @block.vector
        def _(dve):
            c = Counts()
            n_prod = [0]
            n_stat = [0]
            v = nc.vector

            def link(ins):
                ins.then_inc(vec_step, 1)
                dve.wait_ge(vec_step, c.up(vec_step))

            def own(ins, signal):
                ins.then_inc(signal, 1)
                dve.wait_ge(signal, c.up(signal))

            def product(s=None):
                n = n_prod[0]
                n_prod[0] += 1
                if s is None:
                    dve.wait_ge(mid_done, c.up(mid_done))
                else:
                    dve.wait_ge(slab_done, s + 1)
                return prod[n % 2]

            def variance(width, n):
                q = n_stat[0] % 2
                n_stat[0] += 1
                dve.wait_ge(stat_done, c.up(stat_done))
                v.tensor_scalar(var[:, q, 0:width], stat[q][:, :, :].rearrange("p a t -> p (a t)")[:, 0:width],
                                1.0 / n, EPS, ALU.mult, ALU.add).then_inc(var_ready, 1)
                c.up(var_ready)
                return q

            def inverse_root(q, width, out=None, signal=None):
                dve.wait_ge(guess_ready, c.up(guess_ready))
                y, w, t = guess[:, q, 0:width], var[:, q, 0:width], newt[:, 0:width]
                out = y if out is None else out
                link(v.scalar_tensor_tensor(t, y, -0.5, y, ALU.mult, ALU.mult))
                link(v.tensor_tensor(t, t, w, ALU.mult))
                own(v.scalar_tensor_tensor(out, t, 1.5, y, ALU.add, ALU.mult), signal or vec_step)
                return out

            def next_norm(chunk, gain):
                link(v.tensor_scalar(xh[:, chunk, :], x[:, chunk, :], par(gain, chunk), None, ALU.mult))
                v.scalar_tensor_tensor(xl[:, chunk, :], x[:, chunk, :], par(gain, chunk), xh[:, chunk, :].bitcast(F32),
                                       ALU.mult, ALU.subtract).then_inc(xg_ready, 1)

            def split(src, at, n, signal):
                link(v.tensor_copy(xh[:, at:at + n, :], src))
                own(v.tensor_tensor(xl[:, at:at + n, :], src, xh[:, at:at + n, :].bitcast(F32), ALU.subtract), signal)

            def token_norm(scratch):
                dve.wait_ge(sq_ready, c.up(sq_ready))
                v.tensor_reduce(sqsum, scratch.rearrange("p c t -> p t c"), AX_X, ALU.add).then_inc(sum_ready, 1)
                q = variance(T, D)
                inverse_root(q, T, rstd[:, :], rstd_ready)

            def scaled(out, bank, factor=None):
                if factor is None:
                    own(v.tensor_tensor(out, bank, over(rstd[:, :], 2), ALU.mult), evac)
                else:
                    own(v.scalar_tensor_tensor(out, bank, factor, over(rstd[:, :], 2), ALU.mult, ALU.mult), evac)

            def columns():
                q = n_stat[0] % 2
                n_stat[0] += 1
                dve.wait_ge(stat_done, c.up(stat_done))
                own(v.tensor_copy(rstdT[:, :], stat[q][:, 0, 0:TT]), var_ready)

            def values(s, out, cols, at=0):
                for tt in range(TT):
                    b = product(s)
                    own(v.tensor_scalar(out[:, tt, at:at + cols], b[:, :, :].rearrange("p a t -> p (a t)")[:, 0:cols],
                                        rstdT[:, tt:tt + 1], None, ALU.mult), evac)

            def residual(s, gain):
                for j in range(4):
                    b = product(s + j)
                    pair = x[:, 2 * j:2 * j + 2, :]
                    own(v.tensor_tensor(pair, pair, b[:, :, :], ALU.add), evac)
                for k in range(KC):
                    next_norm(k, gain)

            def ffn(s0, gain):
                def gated():
                    v.tensor_tensor(sg[:, :, :], sg[:, :, :], gs[:, :, :], ALU.mult).then_inc(vec_step, 1)

                def scale_by_token():
                    v.tensor_tensor(sg[:, :, :], sg[:, :, :], over(rstd[:, :], 2), ALU.mult).then_inc(vec_step, 1)

                def split_hidden():
                    v.tensor_copy(hidh[:, :, :], hid[:, :, :]).then_inc(vec_step, 1)

                def split_rest():
                    v.tensor_tensor(hidl[:, :, :], hid[:, :, :], hidh[:, :, :].bitcast(F32), ALU.subtract).then_inc(hid_ready, 1)

                token_norm(act3(0))
                scaled(gs[:, :, :], product(s0)[:, :, :])
                dve.wait_ge(sig_ready, c.up(sig_ready))
                gated()
                dve.wait_ge(vec_step, c.up(vec_step))
                scale_by_token()
                dve.wait_ge(vec_step, c.up(vec_step))
                own(v.tensor_tensor(hid[:, :, :], product(s0 + 1)[:, :, :], sg[:, :, :], ALU.mult), evac)
                split_hidden()
                dve.wait_ge(vec_step, c.up(vec_step))
                split_rest()
                e0, g0, t0 = c.now(evac), c.now(sig_ready), c.now(vec_step)
                with dve.Fori(0, (FI - 1) // 2) as i:
                    for u in range(2):
                        s = s0 + 2 + 3 * u
                        dve.wait_ge(slab_done, i * TURN + (s + 1))
                        v.tensor_tensor(gs[:, :, :], prod[0][:, :, :], over(rstd[:, :], 2), ALU.mult).then_inc(evac, 1)
                        dve.wait_ge(sig_ready, i * 2 + (g0 + u + 1))
                        gated()
                        dve.wait_ge(vec_step, i * 6 + (t0 + 3 * u + 1))
                        scale_by_token()
                        dve.wait_ge(vec_step, i * 6 + (t0 + 3 * u + 2))
                        dve.wait_ge(slab_done, i * TURN + (s + 3))
                        v.tensor_tensor(hid[:, :, :], prod[1][:, :, :], sg[:, :, :], ALU.mult).then_inc(evac, 1)
                        dve.wait_ge(evac, i * 4 + (e0 + 2 * u + 2))
                        split_hidden()
                        dve.wait_ge(vec_step, i * 6 + (t0 + 3 * u + 3))
                        split_rest()
                c.up(evac, 2 * (FI - 1))
                c.up(sig_ready, FI - 1)
                c.up(vec_step, 3 * (FI - 1))
                n_prod[0] += 2 * (FI - 1)
                dve.wait_ge(slab_done, s0 + FFN_SLABS)
                for j in range(4):
                    pair = x[:, 2 * j:2 * j + 2, :]
                    ins = v.scalar_tensor_tensor(pair, acc[j][:, :, :], 0.5, pair, ALU.mult, ALU.add)
                    if gain is None:
                        ins.then_inc(xg_ready, 1)
                    else:
                        link(ins)
                        for i in range(2):
                            next_norm(2 * j + i, gain)

            def attention(heads, scale, bias=None, sink=None):
                for i in range(heads + 1):
                    if i < heads:
                        st, mx = small[:, i % 2, :], small[:, 2 + i % 2, 0:2]
                        dve.wait_ge(s_done, c.up(s_done))
                        if bias is None:
                            link(v.tensor_reduce(mx, acc[i % 2][:, :, :], AX_X, ALU.max))
                            ins = v.tensor_scalar(st[:, 0:2], mx, -scale, None, ALU.mult)
                        else:
                            b = bias(i)
                            k = b.shape[-1]
                            link(v.scalar_tensor_tensor(logits[i % 2].rearrange("p a (r k) -> p (a r) k", k=k),
                                                        acc[i % 2][:, :, :].rearrange("p a (r k) -> p (a r) k", k=k),
                                                        scale, b, ALU.mult, ALU.add))
                            if sink is not None and i < SWA_HEADS:
                                link(v.tensor_reduce(mx, logits[i % 2], AX_X, ALU.max))
                                ins = v.tensor_scalar(st[:, 0:2], mx, sink(i), -1.0, ALU.max, ALU.mult)
                            else:
                                ins = v.tensor_reduce(st[:, 0:2], logits[i % 2], AX_X, ALU.max, negate=True)
                        ins.then_inc(logits_ready, 1)
                    if i >= 1:
                        h = i - 1
                        st = small[:, h % 2, :]
                        dve.wait_ge(exp_done, c.up(exp_done))
                        if sink is not None and h < SWA_HEADS:
                            link(v.tensor_tensor(st[:, 2:4], st[:, 2:4], st[:, 4:6], ALU.add))
                        link(v.reciprocal(st[:, 6:8], st[:, 2:4]))
                        for tt in range(TT):
                            last = v.tensor_scalar(probs[h % 2][:, tt, :], probs[h % 2][:, tt, :], st[:, 6 + tt:7 + tt],
                                                   None, ALU.mult)
                        last.then_inc(p_ready, 1)
                    if i >= 3 and i % 2:
                        low_out((i - 3) // 2)
                low_out(heads // 2 - 1)

            def low_out(pair):
                dve.wait_ge(ot_high, c.up(ot_high))
                v.tensor_tensor(xl[:, pair, :], stat[pair % 2][:, 0, :], xh[:, pair, :].bitcast(F32), ALU.subtract).then_inc(ot_ready, 1)

            def head_norm(q, out, gain, width=2 * T):
                y = inverse_root(q, width)
                y = y.rearrange("p (a t) -> p a t", t=T) if width > T else y
                v.scalar_tensor_tensor(out, out, par(gain), y, ALU.mult, ALU.mult).then_inc(norm_ready, 1)
                c.up(norm_ready)

            def hg(s, which, gain):
                token_norm(act3(0))
                for d in range(2):
                    for j in range(4):
                        scaled(gs[:, :, :], product(s + 4 * d + j)[:, :, :])
                        dve.wait_ge(sig_ready, c.up(sig_ready))
                        for i in range(2):
                            h = 2 * j + i
                            last = v.tensor_scalar(hg_f[d][:, h, :], sg[:, i, :], oml[:, which, h:h + 1], lbs[:, which, h:h + 1],
                                                   ALU.mult, ALU.add)
                        link(last)
                        link(v.tensor_scalar((hg_kg, hg_kx)[d][:, 2 * j:2 * j + 2, :], hg_f[d][:, 2 * j:2 * j + 2, :],
                                             -1.0, 1.0, ALU.mult, ALU.add))
                for j in range(4):
                    scaled(hg_q[:, 2 * j:2 * j + 2, :], product(s + 8 + j)[:, :, :], float(D // HG_HEADS) ** -0.5)
                columns()
                v.tensor_tensor(hg_ks, hg_kg, hg_kx, ALU.add).then_inc(tree_ready, 1)
                v.tensor_tensor(hg_qf, hg_q, hg_f[0], ALU.mult).then_inc(vec_step, 1)
                c.up(vec_step)
                v.tensor_tensor(hg_qy, hg_q, hg_f[1], ALU.mult).then_inc(tree_ready, 1)
                dve.wait_ge(tree_ready, c.up(tree_ready, 2))
                flat = [a.rearrange("p c t -> p (c t)") for a in (hg_qf, hg_qy, hg_kg, hg_kx)]
                total = [a.rearrange("p c t -> p (c t)") for a in hg_f]
                spare = region(8)
                dve.wait_ge(tree_done, c.up(tree_done))
                for b in range(4):
                    last = v.tensor_copy(hg_ad[:, 2 * b:2 * b + 2, :], acc[b][:, :, :])
                own(last, tree_taken)
                for n, half in enumerate(HALVES):
                    if n in (0, 2):
                        values(s + 13 + 2 * (n // 2), hg_v, 2 * T, 2 * T * (n // 2))
                    elif n >= 3:
                        scaled(gs[:, :, :], product(s + 16 + n - 3)[:, :, :])
                        dve.wait_ge(sig_ready, c.up(sig_ready))
                        j = n - 3
                        v.tensor_tensor(hg_sg[:, 2 * j:2 * j + 2, :], gs[:, :, :], sg[:, :, :], ALU.mult).then_inc(vec_step, 1)
                        c.up(vec_step)
                    dve.wait_ge(tree_done, c.up(tree_done))
                    mask = levels[:, n, :].unsqueeze(1).to_broadcast([P, 4, P])
                    for b in range(4):
                        last = v.copy_predicated(halves(hg_ad[:, 2 * b:2 * b + 2, :]), mask, halves(acc[b][:, :, :]))
                    own(last, tree_taken)
                    nb = KC * T // (2 * half)
                    pairs = [t[:, 0:2 * nb].rearrange("p (b two) -> p b two", two=2) for t in total]
                    for a, side, t in ((flat[0], 1, pairs[0]), (flat[1], 0, pairs[1]), (flat[2], 0, pairs[0]), (flat[3], 1, pairs[1])):
                        blocks = a.rearrange("p (b two l) -> p b two l", two=2, l=half)[:, :, side, :]
                        factor = t[:, :, 1 - side].unsqueeze(2).to_broadcast([P, nb, half])
                        last = v.tensor_tensor(blocks, blocks, factor, ALU.mult)
                    own(last, tree_ready)
                    if half < HALVES[-1]:
                        if n % 2 == 0:
                            new = [spare[:, d * 1024:d * 1024 + nb] for d in range(2)]
                        else:
                            new = [hg_f[d].rearrange("p c t -> p (c t)")[:, 0:nb] for d in range(2)]
                        for d in range(2):
                            last = v.tensor_tensor(new[d], pairs[d][:, :, 0], pairs[d][:, :, 1], ALU.mult)
                        link(last)
                        total = new
                dve.wait_ge(tree_done, c.up(tree_done))
                for b in range(4):
                    last = v.tensor_copy(hg_ao[:, 2 * b:2 * b + 2, :], acc[b][:, :, :])
                own(last, tree_taken)
                qs = {}
                for b in range(5):
                    if b < 4:
                        qs[b] = variance(2 * T, P)
                    if b >= 1:
                        a = b - 1
                        y = inverse_root(qs[a], 2 * T).rearrange("p (a t) -> p a t", a=2)
                        link(v.scalar_tensor_tensor(hg_o[:, 2 * a:2 * a + 2, :], acc[a][:, :, :], par(f"hg_g{HG_LAYERS[which]}"), y,
                                                    ALU.mult, ALU.mult))
                        pair = hg_o[:, 2 * a:2 * a + 2, :]
                        link(v.tensor_tensor(pair, pair, hg_sg[:, 2 * a:2 * a + 2, :], ALU.mult))
                        for k in (2 * a, 2 * a + 1):
                            split(hg_o[:, k:k + 1, :], k, 1, mix_ready)
                c.up(sq_ready, 4)
                residual(s + 20, gain)

            def na(s, gain):
                token_norm(act3(0))
                q = 0
                for j in range(9):
                    pair = (na_q if j < 4 else na_k)[:, 2 * (j % 4):2 * (j % 4) + 2, :]
                    if j < 8:
                        scaled(pair, product(s + j)[:, :, :])
                        if j == 0:
                            dve.wait_ge(bias_loaded, 16 * 16)
                        for h in (2 * j, 2 * j + 1):
                            b = na_b[:, h].rearrange("p a r k -> p (a r) k")
                            link(v.tensor_tensor(b, b, over(con("namask"), 4 * TT), ALU.add))
                    if j == 8:
                        columns()
                        values(s + 9, na_v, 2 * T, 0)
                    if j >= 1:
                        q = variance(2 * T, NA_DIM)
                        before = (na_q if j - 1 < 4 else na_k)[:, 2 * ((j - 1) % 4):2 * ((j - 1) % 4) + 2, :]
                        head_norm(q, before, "na_q" if j - 1 < 4 else "na_k")
                c.up(sq_ready, 8)
                values(s + 11, na_v, 2 * T, 2 * T)
                attention(NA_HEADS, NA_DIM ** -0.5, lambda h: backwards(na_b[:, h].rearrange("p a r k -> p (a r) k")))
                residual(s + 12, gain)

            def mla(s, gain):
                token_norm(act3(1))
                for j in range(4):
                    scaled(act3(0)[:, 2 * j:2 * j + 2, :], product(s + j)[:, :, :])
                own(v.tensor_tensor(ml_krr, product(s + 4)[:, 0, :], rstd[:, :], ALU.mult), evac)
                for name, lat, n in (("mla_qa", ml_cq, MLA_Q), ("mla_kva", ml_ckv, MLA_KV)):
                    q = variance(T, n)
                    y = inverse_root(q, T)
                    for k in range(n // P):
                        last = v.scalar_tensor_tensor(lat[:, k, :], lat[:, k, :], par(name, k), y, ALU.mult, ALU.mult)
                    link(last)
                    split(lat, 0 if n == MLA_Q else MLA_Q // P, n // P, norm_ready)
                for j in range(4):
                    own(v.tensor_copy(ml_qn[:, 2 * j:2 * j + 2, :], product(s + 5 + j)[:, :, :]), evac)
                for j in range(2):
                    own(v.tensor_copy(ml_qr[:, 2 * j:2 * j + 2, :], product(s + 9 + j)[:, :, :]), evac)
                for m in range(4):
                    own(v.tensor_copy(ml_kn[:, 2 * m:2 * m + 2, :], product()[:, :, :]), evac)
                    own(v.tensor_copy(ml_v[:, :, m * T:(m + 1) * T], product(None if m % 2 == 0 else s + 11 + m // 2)[:, :, :]), evac)
                c.up(sq_ready, 2)
                dve.wait_ge(sq_ready, c.up(sq_ready, 2))
                for j in range(2):
                    v.tensor_scalar(ml_qr[:, 2 * j:2 * j + 2, :], ml_qr[:, 2 * j:2 * j + 2, :], par("mla_qr"), None, ALU.mult).then_inc(mix_ready, 1)
                v.tensor_scalar(ml_kr[:, 0, :], ml_krr, par("mla_kr"), None, ALU.mult).then_inc(mix_ready, 1)
                dve.wait_ge(mix_ready, c.up(mix_ready, 3))
                for j in range(3):
                    n = 2 if j < 2 else 1
                    src = ml_qr[:, 2 * j:2 * j + 2, :] if j < 2 else ml_kr[:, 0:1, :]
                    dst = src if j < 2 else act3(4)[:, 5:6, :]
                    dve.wait_ge(rot_done, c.up(rot_done))
                    b = prod[n_prod[0] % 2]
                    n_prod[0] += 1
                    own(v.tensor_tensor(gs[:, 0:n, :], b[:, 0:n, :], over(con("sin"), n), ALU.mult), evac)
                    link(v.tensor_tensor(sg[:, 0:n, :], src, over(con("cos"), n), ALU.mult))
                    link(v.tensor_tensor(dst, gs[:, 0:n, :], sg[:, 0:n, :], ALU.add))
                steps = [(keys, r, rope) for keys in range(2) for r in range(4) for rope in range(2)]
                qs = {}
                for i in range(len(steps) + 1):
                    if i < len(steps):
                        qs[i] = variance(T if steps[i][2] else 2 * T, NOPE + ROPE)
                    if i >= 1:
                        keys, r, rope = steps[i - 1]
                        y = inverse_root(qs[i - 1], T if rope else 2 * T)
                        if rope:
                            out = (ml_kr if keys else ml_qr)[:, r, :]
                            last = v.tensor_tensor(out, ml_krot if keys else out, y, ALU.mult)
                        else:
                            out = (ml_kn if keys else ml_qn)[:, 2 * r:2 * r + 2, :]
                            last = v.scalar_tensor_tensor(out, out, par("mla_kn" if keys else "mla_qn"),
                                                          y.rearrange("p (a t) -> p a t", a=2), ALU.mult, ALU.mult)
                        if i < len(steps):
                            link(last)
                        else:
                            own(last, norm_ready)
                c.up(sq_ready, 2)
                attention(MLA_HEADS, (NOPE + ROPE) ** -0.5)
                residual(s + 13, gain)

            def branches(s, l, gain):
                token_norm(act3(2))
                pads = (br_u[:, :, 0:UPAD], br_t[:, :, 0:SPAD])
                for pad in pads:
                    v.memset(pad, 0.0).then_inc(vec_step, 1)
                    c.up(vec_step)
                pairs = [(br_q[:, 0:2, :], f"swq{l}"), (br_k[:, 0:2, :], f"swk{l}"), (br_q[:, 2:4, :], f"fxq{l}"), (br_k[:, 2:4, :], f"fxk{l}")]
                for j in range(5):
                    if j < 4:
                        scaled(pairs[j][0], product(s + j)[:, :, :])
                    else:
                        own(v.tensor_tensor(br_x, product(s + 4)[0:FOX_HEADS, 0, :], rstd[0:FOX_HEADS, :], ALU.mult), evac)
                    if j >= 1:
                        q = variance(2 * T, 64)
                        head_norm(q, *pairs[j - 1])
                c.up(sq_ready, 4)
                link(v.tensor_scalar(br_x, br_x, par(f"bf{l}", 0, 1, FOX_HEADS), None, ALU.add))
                link(v.tensor_scalar(br_ncum, br_x, -1.0, None, ALU.mult))
                own(v.tensor_tensor(br_cum, br_x, br_ncum, ALU.max), aux_ready)
                dve.wait_ge(log_ready, c.up(log_ready))
                link(v.scalar_tensor_tensor(br_x, br_x, 0.0, br_l, ALU.min, ALU.subtract))
                link(v.tensor_tensor_scan(br_l, con("ones", 0, 1, FOX_HEADS).to_broadcast([FOX_HEADS, T]), br_x, 0.0, ALU.mult, ALU.add))
                v.tensor_scalar(br_cum, br_l, 8.0, None, ALU.mult).then_inc(vec_step, 1)
                c.up(vec_step)
                own(v.tensor_scalar(br_ncum, br_l, -8.0, None, ALU.mult), norm_ready)
                columns()
                values(s + 6, br_v, 3 * P)
                scaled(gs[:, :, :], product(s + 7)[:, :, :])
                dve.wait_ge(sig_ready, c.up(sig_ready))
                link(v.tensor_tensor(sg[:, :, :], sg[:, :, :], over(rstd[:, :], 2), ALU.mult))
                own(v.tensor_tensor(br_u[:, :, UPAD:UPAD + T], product(s + 8)[:, :, :], sg[:, :, :], ALU.mult), evac)
                scaled(hid[:, :, :], product(s + 9)[:, :, :])
                link(v.tensor_tensor(hid[:, :, :], hid[:, :, :], over(rstd[:, :], 2), ALU.mult))
                own(v.tensor_tensor(br_t[:, :, SPAD:SPAD + T], product(s + 10)[:, :, :], hid[:, :, :], ALU.mult), evac)
                scaled(br_sb, product(s + 11)[:, :, :])

                def gate(j):
                    if j >= 2:
                        dve.wait_ge(sig_ready, c.up(sig_ready))
                    scaled((gs, hid)[j % 2][:, :, :], product(s + 12 + j)[:, :, :])

                def tap(out, src, w, k, first_bias=None):
                    for i in range(2):
                        shifted = src[:, i, k:k + T]
                        weight = w(i, k)
                        if k == 0:
                            last = v.tensor_scalar(out[:, i, :], shifted, weight, first_bias(i) if first_bias else 0.0,
                                                   ALU.mult, ALU.add)
                        else:
                            last = v.scalar_tensor_tensor(out[:, i, :], shifted, weight, out[:, i, :], ALU.mult, ALU.add)
                    link(last)

                for j in range(16):
                    gate(j)
                    for k in range(4 * j, min(4 * j + 4, CONV_K)):
                        tap(br_conv, br_u, lambda i, k: par(f"dw{l}", i * CONV_K + k), k, lambda i: par(f"dwb{l}", i))
                    if 8 <= j < 8 + SC_K:
                        tap(br_sc, br_t, lambda i, k: par(f"sc{l}", i * SC_K + k), j - 8)
                c.up(sig_ready, 2)
                own(v.tensor_tensor(br_sc, br_sc, br_sb, ALU.mult), mix_ready)
                q = n_stat[0] % 2
                n_stat[0] += 1
                dve.wait_ge(stat_done, c.up(stat_done))
                for i in range(2):
                    last = v.scalar_tensor_tensor(br_conv[:, i, :], stat[q][:, 0, :], -1.0 / (2 * P), br_conv[:, i, :], ALU.mult, ALU.add)
                    if i == 0:
                        link(last)
                own(last, var_ready)
                own(v.memset(small[:, 0, 0:1], 0.0), aux_ready)
                q = variance(T, 2 * P)
                y = inverse_root(q, T)
                c.up(sq_ready)
                link(v.tensor_tensor(br_conv, br_conv, over(y, 2), ALU.mult))
                for i in range(2):
                    last = v.tensor_scalar(br_conv[:, i, :], br_conv[:, i, :], par(f"lng{l}", i), par(f"lnb{l}", i), ALU.mult, ALU.add)
                own(last, aux_ready)
                split(br_sc, 4, 2, mix_ready)
                dve.wait_ge(sig_ready, c.up(sig_ready))
                link(v.tensor_tensor(br_conv, br_conv, sg[:, :, :], ALU.mult))
                split(br_conv, 6, 2, mix_ready)
                dve.wait_ge(toe_loaded, 16 * (TT + 1 + l))
                attention(SWA_HEADS + FOX_HEADS, 64 ** -0.5,
                          lambda h: backwards(toe[:, :, h, :]) if h < SWA_HEADS else con("fxmask").rearrange("p (a t) -> p a t", a=TT),
                          lambda h: par(f"sink{l}", h))
                for br in range(4):
                    for j in range(4):
                        b = product(None if j < 3 else s + 28 + br)
                        g = br_g[:, 8 * br + 2 * j:8 * br + 2 * j + 2, :]
                        pair = br_m[:, 2 * j:2 * j + 2, :]
                        if br == 0:
                            own(v.tensor_tensor(pair, b[:, :, :], g, ALU.mult), evac)
                        else:
                            own(v.tensor_tensor(gs[:, :, :], b[:, :, :], g, ALU.mult), evac)
                            link(v.tensor_tensor(pair, pair, gs[:, :, :], ALU.add))
                for k in range(KC):
                    split(br_m[:, k:k + 1, :], k, 1, mix_ready)
                residual(s + 32, gain)

            own(v.memset(zero16[:, :], 0.0), zeros_ready)
            dve.wait_ge(inputs_loaded, 64)
            dve.wait_ge(toe_row, 1)
            v.tensor_copy(toe_rows, acc[0][0:SWA_HEADS, :, :].rearrange("p a t -> p (a t)")).then_inc(toe_rows_done, 1)
            for k in range(KC):
                next_norm(k, "norm0_0")
            link(v.tensor_copy(levels.rearrange("p n t -> p (n t)"), start_const[:, LEVELS:N_START]))
            n = HG_HEADS
            logit = par("hg_lb", 0, 4 * n)
            top = lbt[:, 4 * n:5 * n]
            link(v.tensor_reduce(top, logit.rearrange("p (l h) -> p h l", l=LAYERS_1), AX_X, ALU.max))
            own(v.tensor_tensor(lbt[:, 0:4 * n].rearrange("p (l h) -> p l h", l=LAYERS_1), logit.rearrange("p (l h) -> p l h", l=LAYERS_1),
                                over(top, LAYERS_1), ALU.subtract), lb_max)
            dve.wait_ge(lb_exp, 1)
            rest, whole = lbt[:, 4 * n:5 * n], lbt[:, 5 * n:6 * n]
            link(v.tensor_tensor(rest, lbt[:, n:2 * n], lbt[:, 2 * n:3 * n], ALU.add))
            link(v.tensor_tensor(rest, rest, lbt[:, 3 * n:4 * n], ALU.add))
            link(v.tensor_tensor(whole, rest, lbt[:, 0:n], ALU.add))
            link(v.reciprocal(whole, whole))
            link(v.tensor_tensor(lbs[:, 1, :], rest, whole, ALU.mult))
            link(v.memset(lbs[:, 0, :], 0.0))
            link(v.tensor_scalar(oml[:, :, :], lbs[:, :, :], -1.0, 1.0, ALU.mult, ALU.add))

            for layer, kind in enumerate(MIXERS):
                s1, sm, s2 = STAGES[layer]
                ffn(s1, f"norm{layer}_1")
                gain = f"norm{layer}_2"
                if layer == 0:
                    dve.wait_ge(toe_kept, 16)
                if kind == "hg":
                    hg(sm, HG_LAYERS.index(layer), gain)
                elif kind == "na":
                    na(sm, gain)
                elif kind == "mla":
                    mla(sm, gain)
                else:
                    branches(sm, layer - LAYERS_1, gain)
                ffn(s2, f"norm{layer + 1}_0" if layer + 1 < len(MIXERS) else None)

        @block.gpsimd
        def _(pool):
            def split(s, i=None):
                at = s if i is None else i * TURN + s
                pool.wait_ge(high_ready, at + 1)
                if s >= LOW:
                    pool.wait_ge(slab_done, at + (1 - LOW))
                nc.gpsimd.tensor_tensor(low[:, s % LOW, :], raw[:, s % RAW, :], high[:, s % HIGH, :].bitcast(F32),
                                        ALU.subtract).then_inc(low_ready, 1)

            def split_many(first, turns):
                with pool.Fori(0, turns) as i:
                    for s in range(first, first + TURN):
                        split(s, i)

            early = 4
            for s in range(TURN):
                split(s)
            split_many(TURN, early)
            pool.wait_ge(inputs_loaded, 64)
            pool.wait_ge(toe_loaded, 16 * TT)
            for tt in range(TT):
                nc.gpsimd.tensor_tensor(toe[:, tt, :, :], toe[:, tt, :, :],
                                        over(start_const[:, SWMASK + tt * T:SWMASK + (tt + 1) * T], SWA_HEADS),
                                        ALU.add).then_inc(toe_masked, 1)
            at = TURN * (early + 1)
            turns = (SLABS - at) // TURN
            split_many(at, turns)
            for s in range(at + TURN * turns, SLABS):
                split(s)


def tiles(w, k_chunks, width=P):
    K, N = w.shape
    return w.reshape(k_chunks, P, N // width, width).transpose(2, 0, 1, 3)


def fill(stream, s, blocks):
    at = 0
    for b in blocks:
        stream[s, :, at:at + b.shape[1]] = b
        at += b.shape[1]


def features(stream, s, w, k_chunks=KC, per_slab=2):
    t = tiles(w, k_chunks)
    for j in range(0, t.shape[0], per_slab):
        fill(stream, s + j // per_slab, [t[n, k] for n in range(j, j + per_slab) for k in range(k_chunks)])


def token_major(stream, s, w, k_per_slab):
    rows = w.reshape(-1, P, w.shape[1])
    for j in range(0, len(rows), k_per_slab):
        fill(stream, s + j // k_per_slab, list(rows[j:j + k_per_slab]))


def ffn_slabs(stream, s, w_gate, w_up, w_down):
    n = 2 * P
    order = [("g", 0), ("u", 0)]
    for f in range(1, FI):
        order += [("g", f), ("d", f - 1), ("u", f)]
    order += [("d", FI - 1)]
    for i, (kind, f) in enumerate(order):
        if kind == "d":
            t = tiles(w_down[f * n:(f + 1) * n], 2)
            fill(stream, s + i, [t[c, k] for c in range(KC) for k in range(2)])
        else:
            features(stream, s + i, (w_gate if kind == "g" else w_up)[:, f * n:(f + 1) * n])


def constants():
    c = np.zeros((P, N_CONSTS), np.float32)
    start = np.zeros((P, N_START), np.float32)

    def put(name, a):
        at, w = CONSTS[name]
        c[:a.shape[0], at:at + a.shape[1]] = a

    i = np.arange(P)
    t = np.arange(T)
    put("ident", np.eye(P))
    put("ones", np.ones((P, P)))
    put("blk64", (i[:, None] // 64 == i[None] // 64) * 1.0)
    put("blk32", (i[:, None] // 32 == i[None] // 32) * 1.0)
    put("r2n", np.concatenate([(i[:, None] // 32 == 2 * a + i[None] // 64) * 1.0 for a in range(2)], 1))
    put("n2r", np.concatenate([(2 * a + i[:, None] // 64 == i[None] // 32) * 1.0 for a in range(2)], 1))
    half = ROPE // 2
    rot = np.zeros((P, P))
    for o in range(P):
        if o % ROPE < half:
            rot[o + half, o] = -1.0
        else:
            rot[o - half, o] = 1.0
    put("rot", rot)
    freq = np.float32(10000.0) ** (-np.arange(half, dtype=np.float32) / np.float32(half))
    ang = t.astype(np.float32)[None] * freq.astype(np.float32)[:, None]
    put("cos", np.tile(np.cos(ang.astype(np.float32)), (P // half, 1)))
    put("sin", np.tile(np.sin(ang.astype(np.float32)), (P // half, 1)))
    cols = np.arange(GRID_W)
    first = np.clip(cols - NA_WIN_C // 2, 0, GRID_W - NA_WIN_C)
    inside = (cols[None] >= first[:, None]) & (cols[None] < first[:, None] + NA_WIN_C)
    put("namask", np.tile(np.where(inside, 0.0, NEG), (2, 1))[:, ::-1])
    dist = t[:, None] - t[None]
    for name, ok in (("swmask", (dist >= 0) & (dist < P)), ("fxmask", dist >= 0)):
        m = np.where(ok, 0.0, NEG)
        m = m[:, ::-1] if name == "swmask" else m
        m = m.reshape(TT, P, T).transpose(1, 0, 2).reshape(P, TT * T)
        if name == "swmask":
            start[:, SWMASK:SWMASK + TT * T] = m
        else:
            put(name, m)
    exact = BUCKETS // 2
    d = np.arange(T)
    large = exact + (np.log(np.maximum(d, 1).astype(np.float32) / exact) / np.log(MAX_DISTANCE / exact)
                     * (BUCKETS - exact)).astype(np.int32)
    bucket = np.where(d < exact, d, np.minimum(large, BUCKETS - 1))
    hot = np.zeros((BUCKETS, 2 * T))
    for dd in range(P):
        hot[bucket[dd], T - 1 + dd] = 1.0
    start[:BUCKETS, HOT:HOT + 2 * T] = hot
    put("select", np.eye(FOX_HEADS))
    for n, h in enumerate(HALVES):
        start[:, LEVELS + n * P:LEVELS + (n + 1) * P] = ((i[:, None] // (2 * h) == i[None] // (2 * h))
                                                         & (i[:, None] // h % 2 != i[None] // h % 2))
    return c, start


def layout(z):
    stream = np.zeros((SLABS + SPARE, P, SLAB), np.float32)
    prm = np.zeros((P, N_PARAMS), np.float32)

    def put(name, a):
        at, w = PARAMS[name]
        prm[:a.shape[0], at:at + a.shape[1]] = a

    def by_chunk(a):
        return a.reshape(-1, P).T

    def twice(a):
        return np.concatenate([a, a])[:, None]

    for layer, (s1, sm, s2) in enumerate(STAGES):
        l2 = layer - LAYERS_1
        if l2 < 0:
            for i, name in enumerate(("ffn1_norm", "mix_norm", "ffn2_norm")):
                put(f"norm{layer}_{i}", by_chunk(z[name][layer]))
            for s, n in ((s1, "ffn1"), (s2, "ffn2")):
                gu = z[f"{n}_w_gu"][layer]
                ffn_slabs(stream, s, gu[:, :F], gu[:, F:], z[f"{n}_w_down"][layer])
        else:
            for i, name in enumerate(("ffn1_norm_2", "mix_norm_2", "ffn2_norm_2")):
                put(f"norm{layer}_{i}", by_chunk(z[name][l2]))
            for s, n in ((s1, "ffn1"), (s2, "ffn2")):
                ffn_slabs(stream, s, z[f"{n}_w_gate_2"][l2], z[f"{n}_w_up_2"][l2], z[f"{n}_w_down_2"][l2])
        kind = MIXERS[layer]
        if kind == "hg":
            a = HG_LAYERS.index(layer)
            q, zf, zb, i, g = np.split(z["hg_w_in"][a], 5, axis=1)
            for n, w in enumerate((zf, zb, q)):
                features(stream, sm + 4 * n, w)
            for n in range(2):
                token_major(stream, sm + 12 + 2 * n, i[:, n * 512:(n + 1) * 512], 4)
            features(stream, sm + 16, g)
            features(stream, sm + 20, z["hg_w_out"][a])
            put(f"hg_g{layer}", z["hg_g_norm"][a][:, None])
        elif kind == "na":
            q, k, v = np.split(z["na_w_in"][0], 3, axis=1)
            features(stream, sm, q)
            features(stream, sm + 4, k)
            for n in range(2):
                token_major(stream, sm + 8 + 2 * n, v[:, n * 512:(n + 1) * 512], 4)
            features(stream, sm + 12, z["na_w_out"][0])
        elif kind == "mla":
            w = z["mla_w_in"][0]
            features(stream, sm, w[:, :D])
            features(stream, sm + 4, np.tile(w[:, D:], (1, P // ROPE)), per_slab=1)
            uq = z["mla_w_uq"][0].reshape(MLA_Q, MLA_HEADS, NOPE + ROPE)
            features(stream, sm + 5, uq[:, :, :NOPE].reshape(MLA_Q, -1), MLA_Q // P)
            features(stream, sm + 9, uq[:, :, NOPE:].reshape(MLA_Q, -1), MLA_Q // P)
            ukv = z["mla_w_ukv"][0].reshape(MLA_KV, MLA_HEADS, NOPE + 64)
            kn, vv = tiles(ukv[:, :, :NOPE].reshape(MLA_KV, -1), 2), ukv[:, :, NOPE:].reshape(2, P, -1)
            for j in range(2):
                blocks = []
                for m in (2 * j, 2 * j + 1):
                    blocks += [kn[n, k] for n in (2 * m, 2 * m + 1) for k in range(2)]
                    blocks += [vv[k][:, m * T:(m + 1) * T] for k in range(2)]
                fill(stream, sm + 11 + j, blocks)
            features(stream, sm + 13, z["mla_w_out"][0])
        else:
            w = z["w_in_2"][l2]
            cuts = np.cumsum([256, 256, 256, 256, 256, 256, 128, 128, 256, 256, 256, 4])
            c_a, c_b, s_b, s_c, s_x, a_q, a_k, a_v, f_q, f_k, f_v, f_f, gates = np.split(w, cuts, axis=1)
            kk = a_k.reshape(D, 2, 1, 64)
            features(stream, sm, a_q)
            features(stream, sm + 1, np.concatenate([kk, kk], axis=2).reshape(D, 256))
            features(stream, sm + 2, f_q)
            features(stream, sm + 3, f_k)
            features(stream, sm + 4, np.concatenate([f_f, np.zeros((D, P - FOX_HEADS), np.float32)], axis=1), per_slab=1)
            token_major(stream, sm + 5, np.concatenate([a_v, f_v], axis=1), 5)
            for n, a in enumerate((c_b, c_a, s_c, s_x, s_b)):
                features(stream, sm + 7 + n, a)
            g = np.split(gates, 4, axis=1)
            for n, b in enumerate((2, 3, 1, 0)):
                features(stream, sm + 12 + 4 * n, g[b])
            for n, name in enumerate(("swa_w_o_2", "fox_w_o_2", "sc_w_out_2", "conf_w_out_2")):
                features(stream, sm + 28 + n, z[name][l2], 2, 8)
            features(stream, sm + 32, z["w_out_2"][l2])
            put(f"dw{l2}", z["conf_dw_2"][l2].reshape(CONV_K, 2, P).transpose(2, 1, 0).reshape(P, -1))
            put(f"sc{l2}", z["sc_conv_2"][l2].reshape(SC_K, 2, P).transpose(2, 1, 0).reshape(P, -1))
            for n, name in (("dwb", "conf_dw_b_2"), ("lng", "conf_ln_g_2"), ("lnb", "conf_ln_b_2")):
                put(f"{n}{l2}", by_chunk(z[name][l2]))
            for n, name in (("swq", "swa_q_norm_2"), ("swk", "swa_k_norm_2"), ("fxq", "fox_q_norm_2"), ("fxk", "fox_k_norm_2")):
                put(f"{n}{l2}", twice(z[name][l2]))
            put(f"bf{l2}", z["b_forget_2"][l2][:, None])
            put(f"sink{l2}", np.tile(z["swa_sink_2"][l2][None], (P, 1)))
    put("hg_lb", by_chunk(z["hg_lb_logits"]))
    put("na_q", twice(z["na_q_norm"][0]))
    put("na_k", twice(z["na_k_norm"][0]))
    put("mla_qa", by_chunk(z["mla_q_a_norm"][0]))
    put("mla_kva", by_chunk(z["mla_kv_a_norm"][0]))
    for n in "qk":
        g = z[f"mla_{n}_norm"][0]
        put(f"mla_{n}n", twice(g[:NOPE]))
        put(f"mla_{n}r", np.tile(g[NOPE:], 4)[:, None])
    put("relb", z["rel_bias_2"])
    return stream, prm


def kernel(**inputs):
    import concourse.bacc as bacc
    from concourse.bass_utils import run_bass_kernel_spmd

    z = {k: np.asarray(a) for k, a in inputs.items()}
    stream, prm = layout(z)
    consts, start = constants()
    arrays = {
        "stream": stream,
        "params": prm,
        "consts": consts,
        "start": start,
        "rpb": np.ascontiguousarray(z["na_rpb"][..., ::-1]).reshape(-1),
        "x_in": np.ascontiguousarray(z["x"][0].T.reshape(KC, P, T).transpose(1, 0, 2)),
    }
    nc = bacc.Bacc("TRN2", target_bir_lowering=False, num_devices=1)
    args = [nc.dram_tensor(k, a.shape, mybir.dt.from_np(a.dtype), kind="ExternalInput").ap() for k, a in arrays.items()]
    out = nc.dram_tensor("x_out", (P, KC, T), F32, kind="ExternalOutput").ap()
    by_distance = nc.dram_tensor("bias_by_distance", (SWA_HEADS, 2 * T), F32, kind="Internal").ap()
    shifted = nc.dram_tensor("bias_shifted", (P, TT, SWA_HEADS, T), F32, kind="Internal").ap()
    build(nc, *args, out, by_distance, shifted)
    r = run_bass_kernel_spmd(nc, [arrays], core_ids=[0])
    y = r.results[0]["x_out"]
    return np.ascontiguousarray(y.transpose(1, 0, 2).reshape(D, T).T)[None]
```

```python
from contextlib import ExitStack

import numpy as np

import concourse.bass as bass
from concourse import mybir

F32 = mybir.dt.float32
F32R = mybir.dt.float32r
BF16 = mybir.dt.bfloat16
U8 = mybir.dt.uint8
ACT = mybir.ActivationFunctionType
ALU = mybir.AluOpType
AX_X = mybir.AxisListType.X

P = 128
T = 256
TT = T // P
D = 1024
KC = D // P
F = 2816
FI = F // (2 * P)
EPS = 1e-6
RAW = 3
HIGH = 3
LOW = 2
TURN = 6
SPARE = 2
TILES = 16
SLAB = TILES * P
NEG = -1e30

HG_HEADS = 8
HG_LAYERS = (0, 3)
HALVES = (1, 2, 4, 8, 16, 32, 64)
NA_HEADS = 16
NA_DIM = 64
GRID_W = 64
NA_WIN_C = 16
NA_RPB = (15, 31)
MLA_HEADS = 16
MLA_Q = 768
MLA_KV = 256
NOPE = 64
ROPE = 32
SWA_HEADS = 4
FOX_HEADS = 4
CONV_K = 31
SC_K = 3
BUCKETS = 32
MAX_DISTANCE = 128
LAYERS_1 = 4
LAYERS_2 = 2

FFN_SLABS = 3 * FI
MIX_SLABS = {"hg": 24, "na": 16, "mla": 17, "branches": 36}
MIXERS = ["hg", "na", "mla", "hg", "branches", "branches"]


def plan():
    at, out = 0, []
    for kind in MIXERS:
        ffn1 = at
        mix = ffn1 + FFN_SLABS
        ffn2 = mix + MIX_SLABS[kind]
        at = ffn2 + FFN_SLABS
        out.append((ffn1, mix, ffn2))
    return out, at


STAGES, SLABS = plan()

PARAMS = {}


def _params():
    at = 0
    for name, width in (
        [(f"norm{l}_{s}", KC) for l in range(LAYERS_1 + LAYERS_2) for s in range(3)]
        + [("hg_lb", LAYERS_1 * HG_HEADS), ("hg_g0", 1), ("hg_g3", 1), ("na_q", 1), ("na_k", 1)]
        + [("mla_qa", MLA_Q // P), ("mla_kva", MLA_KV // P), ("mla_qn", 1), ("mla_qr", 1), ("mla_kn", 1), ("mla_kr", 1)]
        + [(f"{n}{l}", w) for l in range(LAYERS_2) for n, w in (
            ("dw", 2 * CONV_K), ("dwb", 2), ("lng", 2), ("lnb", 2), ("sc", 2 * SC_K), ("swq", 1), ("swk", 1),
            ("fxq", 1), ("fxk", 1), ("bf", 1), ("sink", SWA_HEADS))]
        + [("relb", SWA_HEADS)]
    ):
        PARAMS[name] = (at, width)
        at += width
    return at


N_PARAMS = _params()

CONSTS = {}


def _consts():
    at = 0
    for name, width in (
        [("ident", P), ("ones", P), ("blk64", P), ("r2n", 2 * P), ("n2r", 2 * P), ("blk32", P), ("rot", P)]
        + [("cos", T), ("sin", T), ("namask", GRID_W), ("fxmask", TT * T), ("select", FOX_HEADS)]
    ):
        CONSTS[name] = (at, width)
        at += width
    return at


N_CONSTS = _consts()
HOT, SWMASK = 0, 2 * T
LEVELS = SWMASK + TT * T
N_START = LEVELS + len(HALVES) * P


class Counts(dict):

    def up(self, sem, n=1):
        self[sem] = self.get(sem, 0) + n
        return self[sem]

    def now(self, sem):
        return self.get(sem, 0)


def build(nc, W, PRM, CST, START, RPB, XIN, OUT, TOE_ROWS, TOE):
    ctx = ExitStack()
    with ctx:
        def sb(name, shape, dt=F32):
            return ctx.enter_context(nc.sbuf_tensor(name, shape, dt))

        def sem(name):
            return ctx.enter_context(nc.semaphore(name))

        raw = sb("raw", [P, RAW, SLAB])
        high = sb("high", [P, HIGH, SLAB], F32R)
        low = sb("low", [P, LOW, SLAB], F32R)
        levels = sb("levels", [P, len(HALVES), P], U8)
        prm = sb("prm", [P, N_PARAMS])
        cst = sb("cst", [P, N_CONSTS])
        x = sb("x", [P, KC, T])
        xh = sb("xh", [P, KC, T], F32R)
        xl = sb("xl", [P, KC, T], F32R)
        gs = sb("gs", [P, 2, T])
        sg = sb("sg", [P, 2, T])
        hidh = sb("hidh", [P, 2, T], F32R)
        hidl = sb("hidl", [P, 2, T], F32R)
        rstd = sb("rstd", [P, T])
        rstdT = sb("rstdT", [P, TT])
        var = sb("var", [P, 2, 2 * T])
        guess = sb("guess", [P, 2, 2 * T])
        newt = sb("newt", [P, 2 * T])
        sqsum = newt[:, 0:T]
        hid = newt.rearrange("p (a t) -> p a t", a=2)
        lbs = sb("lbs", [P, 2, HG_HEADS])
        oml = sb("oml", [P, 2, HG_HEADS])
        lbt = sb("lbt", [P, 6 * HG_HEADS])
        zero16 = sb("zero16", [1, 4 * P], BF16)
        small = sb("small", [P, 4, 8])
        work = sb("work", [P, 11 * KC * T])

        acc = [ctx.enter_context(nc.psum_tensor(f"acc{i}", [P, 2, T], F32)) for i in range(4)]
        prod = [ctx.enter_context(nc.psum_tensor(f"prod{i}", [P, 2, T], F32)) for i in range(2)]
        stat = [ctx.enter_context(nc.psum_tensor(f"stat{i}", [P, 2, T], F32)) for i in range(2)]

        slab_loaded = [sem(f"slab_loaded{r}") for r in range(RAW)]
        high_ready = sem("high_ready")
        low_ready = sem("low_ready")
        slab_done = sem("slab_done")
        hid_ready = sem("hid_ready")
        inputs_loaded = sem("inputs_loaded")
        bias_loaded = sem("bias_loaded")
        toe_row = sem("toe_row")
        toe_stored = sem("toe_stored")
        toe_loaded = sem("toe_loaded")
        toe_rows_done = sem("toe_rows_done")
        toe_masked = sem("toe_masked")
        toe_kept = sem("toe_kept")
        zeros_ready = sem("zeros_ready")
        vec_step = sem("vec_step")
        act_step = sem("act_step")
        lb_max = sem("lb_max")
        lb_exp = sem("lb_exp")
        x_ready = sem("x_ready")
        xh_ready = sem("xh_ready")
        xg_ready = sem("xg_ready")
        evac = sem("evac")
        mid_done = sem("mid_done")
        sig_ready = sem("sig_ready")
        sq_ready = sem("sq_ready")
        sum_ready = sem("sum_ready")
        stat_done = sem("stat_done")
        var_ready = sem("var_ready")
        guess_ready = sem("guess_ready")
        rstd_ready = sem("rstd_ready")
        norm_ready = sem("norm_ready")
        tree_ready = sem("tree_ready")
        keys_ready = sem("keys_ready")
        tree_done = sem("tree_done")
        tree_taken = sem("tree_taken")
        mix_done = sem("mix_done")
        mix_ready = sem("mix_ready")
        s_done = sem("s_done")
        logits_ready = sem("logits_ready")
        exp_done = sem("exp_done")
        p_ready = sem("p_ready")
        t_done = sem("t_done")
        pt_ready = sem("pt_ready")
        pv_done = sem("pv_done")
        ot_high = sem("ot_high")
        ot_ready = sem("ot_ready")
        aux_ready = sem("aux_ready")
        log_ready = sem("log_ready")
        rot_done = sem("rot_done")
        stored = sem("stored")

        def par(name, i=0, n=1, p=P):
            a, _ = PARAMS[name]
            return prm[0:p, a + i:a + i + n]

        def con(name, i=0, n=None, p=P):
            a, w = CONSTS[name]
            return cst[0:p, a + i:a + i + (w if n is None else n)]

        ident = con("ident")
        ones = con("ones")

        def region(at, n=1):
            return work[:, at * KC * T:(at + n) * KC * T]

        def act3(at):
            return region(at).rearrange("p (c t) -> p c t", c=KC)

        def over(ap, n):
            return ap.unsqueeze(1).to_broadcast([ap.shape[0], n, ap.shape[1]])

        def backwards(ap):
            dims = [list(d) for d in ap.ap]
            step, n = dims[-1]
            dims[-1] = [-step, n]
            return bass.AP(tensor=ap.tensor, offset=ap.offset + step * (n - 1), ap=dims)

        def sides(ap, half):
            return bass.AP(tensor=ap.tensor, offset=ap.offset,
                           ap=[list(ap.ap[0]), [2 * half, ap.shape[-1] // (2 * half)], [KC * T + half, 2], [1, half]])

        def tile_of(s, j, n=1):
            return high[:, s % HIGH, j * P:(j + n) * P], low[:, s % LOW, j * P:(j + n) * P]

        def halves(ap):
            return ap.rearrange("p a (b t) -> p (a b) t", b=2)

        def half64(h):
            return slice(64 * (h % 2), 64 * (h % 2) + 64)

        def part32(h):
            return slice(32 * (h % 4), 32 * (h % 4) + 32)

        hg_q, hg_qy, hg_qf = act3(0), act3(1), act3(2)
        hg_kg, hg_kx = act3(3), act3(4)
        hg_f = (act3(5), act3(6))
        hg_ad, hg_ao = act3(7), act3(8)
        hg_ks = act3(8)
        hg_v = region(9).rearrange("p (a n) -> p a n", a=TT)
        hg_sg = act3(10)
        hg_km = act3(0)
        hg_o, hg_sq = act3(0), act3(3)

        at_buf = region(9, 2)
        logits = [at_buf[:, i * 512:(i + 1) * 512].rearrange("p (a t) -> p a t", a=TT) for i in range(2)]
        probs = [at_buf[:, (2 + i) * 512:(3 + i) * 512].rearrange("p (a t) -> p a t", a=TT) for i in range(2)]
        probsT = [at_buf[:, (4 + i) * 512:(5 + i) * 512].rearrange("p (a t) -> p a t", a=TT) for i in range(2)]
        squares = [region(3)[:, i * 512:(i + 1) * 512].rearrange("p (a t) -> p a t", a=2) for i in range(2)]

        na_q, na_k = act3(0), act3(1)
        na_v = region(2).rearrange("p (a n) -> p a n", a=TT)
        na_b = region(4, 4).rearrange("p (h a r k) -> p h a r k", h=NA_HEADS, a=TT, r=4)

        ml_cq, ml_ckv, ml_sq = act3(0)[:, 0:6, :], act3(0)[:, 6:8, :], act3(1)
        ml_qn, ml_kn = act3(2), act3(5)
        ml_qr, ml_kr = act3(3)[:, 0:4, :], act3(3)[:, 4:8, :]
        ml_krr, ml_sqr, ml_krot = act3(4)[:, 0, :], act3(4)[:, 1:5, :], act3(4)[:, 5, :]
        ml_v = region(6).rearrange("p (a n) -> p a n", a=TT)
        ml_sqn = act3(7)

        br_q, br_k = act3(0)[:, 0:4, :], act3(0)[:, 4:8, :]
        br_v = region(1)[:, 0:TT * 3 * P].rearrange("p (a n) -> p a n", a=TT)
        br_conv = region(1)[:, 768:1280].rearrange("p (a t) -> p a t", a=2)
        br_sq = region(1)[:, 1280:1792].rearrange("p (a t) -> p a t", a=2)
        UPAD, SPAD = CONV_K - 1, SC_K - 1
        br_u = region(2)[:, 0:2 * (T + UPAD)].rearrange("p (a t) -> p a t", a=2)
        br_t = region(2)[:, 572:572 + 2 * (T + SPAD)].rearrange("p (a t) -> p a t", a=2)
        br_sb = region(2)[:, 1088:1600].rearrange("p (a t) -> p a t", a=2)
        br_x, br_l, br_cum, br_ncum = (region(3)[0:FOX_HEADS, 1024 + i * T:1024 + (i + 1) * T] for i in range(4))
        br_g = region(4, 4).rearrange("p (c t) -> p c t", t=T)
        br_m = act3(9)
        br_sc = region(10)[:, 1024:1536].rearrange("p (a t) -> p a t", a=2)
        toe = region(8).rearrange("p (a h t) -> p a h t", a=TT, h=SWA_HEADS)
        toe_rows = region(3)[0:SWA_HEADS, 0:2 * T]
        x_squares = act3(2)
        start_const = region(1)[:, 0:N_START]

        block = ctx.enter_context(nc.Block())

        @block.sync
        def _(sp):
            sp.dma_start(prm[:, :], PRM).then_inc(inputs_loaded, 16)
            sp.dma_start(x[:, :, :], XIN).then_inc(inputs_loaded, 16)
            sp.dma_start(cst[:, :], CST).then_inc(inputs_loaded, 16)
            sp.dma_start(start_const, START).then_inc(inputs_loaded, 16)
            for r in range(RAW):
                sp.dma_start(raw[:, r, :], W[r]).then_inc(slab_loaded[r], 16)
            rounds = (SLABS + SPARE) // RAW
            with sp.Fori(1, rounds) as i:
                for r in range(RAW):
                    sp.wait_ge(low_ready, i * RAW + (r - RAW + 1))
                    sp.dma_start(raw[:, r, :], W[bass.ds(i * RAW + r, 1)].rearrange("a p n -> p (a n)")).then_inc(slab_loaded[r], 16)
            for s in range(rounds * RAW, SLABS + SPARE):
                sp.wait_ge(low_ready, s - RAW + 1)
                sp.dma_start(raw[:, s % RAW, :], W[s]).then_inc(slab_loaded[s % RAW], 16)
            sp.wait_ge(xg_ready, KC * (3 * len(MIXERS)) + 4)
            sp.dma_start(OUT, x[:, :, :]).then_inc(stored, 16)
            sp.wait_ge(stored, 16)

        @block.tensor
        def _(pe):
            c = Counts()
            n_prod = [0]
            n_stat = [0]

            def slab_in(s):
                pe.wait_ge(low_ready, s + 1)

            def three(out, w, a, start, stop, **kw):
                (wh, wl), (ah, al) = w, a
                nc.tensor.matmul(out, wh, ah, start=start, stop=False, **kw)
                nc.tensor.matmul(out, wh, al, start=False, stop=False, **kw)
                return nc.tensor.matmul(out, wl, ah, start=False, stop=stop, **kw)

            def operand(k):
                return xh[:, k, :], xl[:, k, :]

            def bank():
                n = n_prod[0]
                n_prod[0] += 1
                if n >= 2:
                    pe.wait_ge(evac, n - 1)
                return prod[n % 2]

            def stat_bank():
                n = n_stat[0]
                n_stat[0] += 1
                if n >= 2:
                    pe.wait_ge(var_ready, n - 1)
                return stat[n % 2]

            def zero(out):
                nc.tensor.matmul(out[:, :, :], zero16[:, 0:P], zero16[:, 0:2 * T], start=True, stop=True, skip_group_check=True)

            def chunks(out, s, rhs, n_chunks=2, k_chunks=KC, first=0, wait=None):
                if wait is not None:
                    zero(out)
                    for k in range(k_chunks):
                        pe.wait_ge(wait, c.up(wait))
                        for n in range(n_chunks):
                            last = three(out[:, n, :], tile_of(s, first + n * k_chunks + k), rhs(k), False, True,
                                         skip_group_check=True)
                    return last
                for n in range(n_chunks):
                    for k in range(k_chunks):
                        last = three(out[:, n, :], tile_of(s, first + n * k_chunks + k), rhs(k), k == 0, k == k_chunks - 1)
                return last

            def stats(lhs_rhs, n=T):
                b = stat_bank()
                out = b[:, :, :].rearrange("p a t -> p (a t)")[:, 0:n]
                for i, (lhs, rhs) in enumerate(lhs_rhs):
                    last = nc.tensor.matmul(out, lhs, rhs, start=(i == 0), stop=(i == len(lhs_rhs) - 1))
                last.then_inc(stat_done, 1)

            def token_stats():
                pe.wait_ge(sum_ready, c.up(sum_ready))
                stats([(ones, sqsum)])
                c.up(rstd_ready)
                c.up(sq_ready)

            def token_columns():
                pe.wait_ge(rstd_ready, c.now(rstd_ready))
                b = stat_bank()
                for tt in range(TT):
                    last = nc.tensor.matmul(b[:, 0, tt:tt + 1], rstd[0:1, tt * P:(tt + 1) * P], ones[0:1, 0:1],
                                            start=True, stop=True)
                last.then_inc(stat_done, 1)

            def project(s, rhs=operand, **kw):
                slab_in(s)
                chunks(bank(), s, rhs, **kw).then_inc(slab_done, 1)

            def project_tokens(s, n_slabs, cols, k_per_slab):
                out = [bank() for _ in range(TT)]
                k = 0
                for j in range(n_slabs):
                    slab_in(s + j)
                    ks = list(range(k, min(k + k_per_slab, KC)))
                    for i, kk in enumerate(ks):
                        for tt in range(TT):
                            tok = slice(tt * P, (tt + 1) * P)
                            w = (high[:, (s + j) % HIGH, i * cols:(i + 1) * cols], low[:, (s + j) % LOW, i * cols:(i + 1) * cols])
                            last = three(out[tt][:, :, :].rearrange("p a t -> p (a t)")[:, 0:cols],
                                         (xh[:, kk, tok], xl[:, kk, tok]), w, kk == 0, kk == KC - 1)
                    last.then_inc(slab_done, 1)
                    k += len(ks)

            def ffn(s0):
                def gate(out, s, wait=None):
                    return chunks(out, s, operand, wait=wait)

                def down(s):
                    for n in range(KC):
                        for k in range(2):
                            last = three(acc[n // 2][:, n % 2, :], tile_of(s, 2 * n + k), (hidh[:, k, :], hidl[:, k, :]),
                                         False, True, skip_group_check=True)
                    return last

                base, hids = n_prod[0], c.now(hid_ready)
                assert base % 2 == 0
                if base:
                    pe.wait_ge(evac, base)
                slab_in(s0)
                gate(prod[0], s0, wait=xg_ready).then_inc(slab_done, 1)
                token_stats()
                for bank_of_sums in acc:
                    zero(bank_of_sums)
                slab_in(s0 + 1)
                gate(prod[1], s0 + 1).then_inc(slab_done, 1)
                with pe.Fori(0, (FI - 1) // 2) as i:
                    for u in range(2):
                        s = s0 + 2 + 3 * u
                        pe.wait_ge(low_ready, i * TURN + (s + 1))
                        pe.wait_ge(evac, i * 4 + (base + 2 * u + 1))
                        gate(prod[0], s).then_inc(slab_done, 1)
                        pe.wait_ge(low_ready, i * TURN + (s + 2))
                        pe.wait_ge(hid_ready, i * 2 + (hids + u + 1))
                        down(s + 1).then_inc(slab_done, 1)
                        pe.wait_ge(low_ready, i * TURN + (s + 3))
                        gate(prod[1], s + 2).then_inc(slab_done, 1)
                n_prod[0] += 2 * FI
                slab_in(s0 + FFN_SLABS - 1)
                pe.wait_ge(hid_ready, c.up(hid_ready, FI))
                down(s0 + FFN_SLABS - 1).then_inc(slab_done, 1)

            def out_projection(s):
                for j in range(4):
                    project(s + j)

            def attention(heads, scores, values):
                for i in range(heads + 3):
                    if 2 <= i < heads + 2:
                        pe.wait_ge(p_ready, c.up(p_ready))
                    if i < heads:
                        for tt in range(TT):
                            pairs = scores(i, tt)
                            for n, (lhs, rhs) in enumerate(pairs):
                                last = nc.tensor.matmul(acc[i % 2][:, tt, :], lhs, rhs, start=(n == 0),
                                                        stop=(n == len(pairs) - 1))
                        last.then_inc(s_done, 1)
                    if 2 <= i < heads + 2:
                        h = i - 2
                        for kt in range(TT):
                            for tt in range(TT):
                                last = nc.tensor.transpose(acc[2 + h % 2][:, kt, tt * P:(tt + 1) * P],
                                                           probs[h % 2][:, tt, kt * P:(kt + 1) * P], ident)
                        last.then_inc(t_done, 1)
                    if i >= 3:
                        h = i - 3
                        if h % 2 == 0 and h >= 4:
                            pe.wait_ge(ot_ready, ot_base + h // 2 - 1)
                        pe.wait_ge(pt_ready, c.up(pt_ready))
                        half = slice(64 * (h % 2), 64 * (h % 2) + 64)
                        for kt in range(TT):
                            last = nc.tensor.matmul(stat[h // 2 % 2][half, 0, :], values(h, kt), probsT[h % 2][:, kt, :],
                                                    start=(kt == 0), stop=(kt == TT - 1))
                        last.then_inc(pv_done, 1)

            def hg(s):
                project(s, wait=xg_ready)
                token_stats()
                for j in range(1, 12):
                    project(s + j)
                token_columns()
                def half_of_heads(g):
                    return range(g * HG_HEADS // 2, (g + 1) * HG_HEADS // 2)

                for g in range(2):
                    pe.wait_ge(tree_ready, c.up(tree_ready))
                    for h in half_of_heads(g):
                        for tt in range(TT):
                            tok = slice(tt * P, (tt + 1) * P)
                            last = nc.tensor.matmul(acc[h // 2][:, h % 2, tok], hg_ks[:, h, tok], hg_q[:, h, tok],
                                                    start=True, stop=True)
                    last.then_inc(tree_done, 1)
                for n, half in enumerate(HALVES):
                    if n in (0, 2):
                        project_tokens(s + 12 + 2 * (n // 2), 2, 2 * T, 4)
                    elif n >= 3:
                        project(s + 16 + n - 3)
                    for g in range(2):
                        if n:
                            c.up(tree_ready)
                            pe.wait_ge(keys_ready, c.up(keys_ready))
                        pe.wait_ge(tree_taken, c.up(tree_taken))
                        for h in half_of_heads(g):
                            for tt in range(TT):
                                tok = slice(tt * P, (tt + 1) * P)
                                if n:
                                    last = nc.tensor.matmul(acc[h // 2][:, h % 2, tok], hg_km[:, h, tok],
                                                            sides(hg_qy[:, h, tok], half), start=True, stop=True)
                                    continue
                                o4 = acc[h // 2][:, h % 2, tok].rearrange("p (b two l) -> p b two l", two=2, l=half)
                                for keys, queries, side in ((hg_kg, hg_qf, 1), (hg_kx, hg_qy, 0)):
                                    q4 = queries[:, h, tok].rearrange("p (b two l) -> p b two l", two=2, l=half)
                                    last = nc.tensor.matmul(o4[:, :, side, :], keys[:, h, tok], q4[:, :, side, :],
                                                            start=True, stop=True, skip_group_check=True)
                        last.then_inc(tree_done, 1)
                lo, hi = slice(0, P), slice(P, T)
                for g in range(2):
                    pe.wait_ge(tree_ready, c.up(tree_ready))
                    pe.wait_ge(tree_taken, c.up(tree_taken))
                    for h in half_of_heads(g):
                        nc.tensor.matmul(acc[h // 2][:, h % 2, hi], hg_kg[:, h, lo], hg_qf[:, h, hi], start=True, stop=True)
                        last = nc.tensor.matmul(acc[h // 2][:, h % 2, lo], hg_kx[:, h, hi], hg_qy[:, h, lo], start=True, stop=True)
                    last.then_inc(tree_done, 1)
                pe.wait_ge(tree_taken, c.up(tree_taken, 2))
                for b in range(4):
                    for h in (2 * b, 2 * b + 1):
                        for tt in range(TT):
                            tok = slice(tt * P, (tt + 1) * P)
                            nc.tensor.matmul(acc[b][:, h % 2, tok], hg_v[:, tt, h * P:(h + 1) * P], hg_ad[:, h, tok],
                                             start=True, stop=False)
                            last = nc.tensor.matmul(acc[b][:, h % 2, tok], hg_v[:, 1 - tt, h * P:(h + 1) * P],
                                                    hg_ao[:, h, tok], start=False, stop=True)
                    last.then_inc(mix_done, 1)
                for b in range(4):
                    pe.wait_ge(sq_ready, c.up(sq_ready))
                    stats([(ones, hg_sq[:, 2 * b:2 * b + 2, :])], 2 * T)
                project(s + 20, wait=mix_ready)
                for j in range(1, 4):
                    project(s + 20 + j)

            def head_stats(j):
                pe.wait_ge(sq_ready, c.up(sq_ready))
                stats([(con("blk64"), squares[j % 2][:, :, :])], 2 * T)

            def na(s):
                project(s, wait=xg_ready)
                token_stats()
                for j in range(1, 8):
                    project(s + j)
                    head_stats(j - 1)
                token_columns()
                for g in range(2):
                    project_tokens(s + 8 + 2 * g, 2, 2 * T, 4)
                    if g == 0:
                        head_stats(7)
                pe.wait_ge(norm_ready, c.up(norm_ready, 8))
                attention(NA_HEADS,
                          lambda h, tt: [(na_q[half64(h), h // 2, tt * P:(tt + 1) * P], na_k[half64(h), h // 2, :])],
                          lambda h, kt: na_v[:, kt, h * NA_DIM:(h + 1) * NA_DIM])
                pe.wait_ge(ot_ready, ot_base + NA_HEADS // 2)
                out_projection(s + 12)

            def mla(s):
                project(s, wait=xg_ready)
                token_stats()
                for j in range(1, 4):
                    project(s + j)
                project(s + 4, n_chunks=1)
                pe.wait_ge(sq_ready, c.up(sq_ready, 2))
                for at, n in ((MLA_Q // P, MLA_KV // P), (0, MLA_Q // P)):
                    stats([(ones, ml_sq[:, at + i, :]) for i in range(n)])
                pe.wait_ge(norm_ready, c.up(norm_ready))
                for j in range(2):
                    slab_in(s + 5 + j)
                    for u in range(2):
                        chunks(bank(), s + 5 + j, lambda k: operand(6 + k), k_chunks=2, first=8 * u).then_inc(mid_done, 1)
                        b = bank()
                        for tt in range(TT):
                            tok = slice(tt * P, (tt + 1) * P)
                            for k in range(2):
                                last = three(b[:, tt, :], (xh[:, 6 + k, tok], xl[:, 6 + k, tok]),
                                             tile_of(s + 5 + j, 8 * u + 4 + 2 * k, 2), k == 0, k == 1)
                        last.then_inc(mid_done if u == 0 else slab_done, 1)

                def rotate(sources):
                    pe.wait_ge(mix_ready, c.up(mix_ready))
                    b = bank()
                    for i, src in enumerate(sources):
                        last = nc.tensor.matmul(b[:, i, :], con("rot"), src, start=True, stop=True)
                    last.then_inc(rot_done, 1)

                def lengths(r, rope_sq):
                    b = stat_bank()
                    for i in range(2):
                        nc.tensor.matmul(b[:, i, :], con("blk64"), ml_sqn[:, 2 * r + i, :], start=True, stop=False)
                        last = nc.tensor.matmul(b[:, i, :], con("r2n", i * P, P), rope_sq, start=False, stop=True)
                    last.then_inc(stat_done, 1)
                    b = stat_bank()
                    nc.tensor.matmul(b[:, 0, :], con("blk32"), rope_sq, start=True, stop=False)
                    for i in range(2):
                        last = nc.tensor.matmul(b[:, 0, :], con("n2r", i * P, P), ml_sqn[:, 2 * r + i, :],
                                                start=False, stop=(i == 1))
                    last.then_inc(stat_done, 1)

                rotate([ml_kr[:, 0, :]])
                pe.wait_ge(norm_ready, c.up(norm_ready))
                for j in range(4):
                    project(s + 7 + j, k_chunks=6)
                    if j == 0:
                        pe.wait_ge(sq_ready, c.up(sq_ready, 2))
                    lengths(j, ml_sqr[:, 0, :])
                for j in range(2):
                    project(s + 11 + j, k_chunks=6)
                pe.wait_ge(sq_ready, c.up(sq_ready, 2))
                for r in range(4):
                    lengths(r, ml_sqr[:, r, :])
                    if r == 0:
                        for pair in range(2):
                            rotate([ml_qr[:, 2 * pair + i, :] for i in range(2)])
                pe.wait_ge(norm_ready, c.up(norm_ready))
                attention(MLA_HEADS,
                          lambda h, tt: [(ml_qn[half64(h), h // 2, tt * P:(tt + 1) * P], ml_kn[half64(h), h // 2, :]),
                                         (ml_qr[part32(h), h // 4, tt * P:(tt + 1) * P], ml_kr[part32(h), h // 4, :])],
                          lambda h, kt: ml_v[:, kt, h * 64:(h + 1) * 64])
                pe.wait_ge(ot_ready, ot_base + MLA_HEADS // 2)
                out_projection(s + 13)

            def branches(s):
                project(s, wait=xg_ready)
                token_stats()
                for j in range(1, 4):
                    project(s + j)
                    head_stats(j - 1)
                project(s + 4, n_chunks=1)
                head_stats(3)
                token_columns()
                project_tokens(s + 5, 2, 3 * P, 5)
                for j in range(5 + 12):
                    project(s + 7 + j)
                pe.wait_ge(mix_ready, c.up(mix_ready))
                stats([(ones, br_conv[:, i, :]) for i in range(2)])
                project(s + 24)
                pe.wait_ge(sq_ready, c.up(sq_ready))
                stats([(ones, br_sq[:, i, :]) for i in range(2)])
                for j in range(3):
                    project(s + 25 + j)
                pe.wait_ge(norm_ready, c.up(norm_ready, 5))
                pe.wait_ge(var_ready, n_stat[0])
                attention(SWA_HEADS + FOX_HEADS, br_scores, br_values)
                pe.wait_ge(ot_ready, ot_base + (SWA_HEADS + FOX_HEADS) // 2)
                for br in range(4):
                    if br >= 2:
                        pe.wait_ge(mix_ready, c.up(mix_ready))
                    slab_in(s + 28 + br)
                    for j in range(4):
                        last = chunks(bank(), s + 28 + br, lambda k: operand(2 * br + k), k_chunks=2, first=4 * j)
                        if j < 3:
                            last.then_inc(mid_done, 1)
                    last.then_inc(slab_done, 1)
                project(s + 32, wait=mix_ready)
                for j in range(1, 4):
                    project(s + 32 + j)

            def br_scores(h, tt):
                tok = slice(tt * P, (tt + 1) * P)
                if h < SWA_HEADS:
                    return [(br_q[half64(h), h // 2, tok], br_k[half64(h), h // 2, :])]
                g = h - SWA_HEADS
                return [(br_q[half64(g), 2 + g // 2, tok], br_k[half64(g), 2 + g // 2, :]),
                        (br_cum[0:FOX_HEADS, tok], con("select", g, 1, FOX_HEADS).to_broadcast([FOX_HEADS, T])),
                        (con("select", g, 1, FOX_HEADS).to_broadcast([FOX_HEADS, P]), br_ncum[0:FOX_HEADS, :])]

            def br_values(h, kt):
                if h < SWA_HEADS:
                    return br_v[:, kt, (h // 2) * 64:(h // 2) * 64 + 64]
                return br_v[:, kt, P + (h - SWA_HEADS) * 64:P + (h - SWA_HEADS) * 64 + 64]

            pe.wait_ge(inputs_loaded, 64)
            nc.tensor.matmul(acc[0][0:SWA_HEADS, :, :].rearrange("p a t -> p (a t)"), par("relb", 0, SWA_HEADS, BUCKETS),
                             start_const[0:BUCKETS, HOT:HOT + 2 * T], start=True, stop=True).then_inc(toe_row, 1)
            pe.wait_ge(zeros_ready, 1)
            ot_base = 0
            for layer, kind in enumerate(MIXERS):
                s1, sm, s2 = STAGES[layer]
                ffn(s1)
                {"hg": hg, "na": na, "mla": mla, "branches": branches}[kind](sm)
                ot_base += {"hg": 0, "na": 8, "mla": 8, "branches": 4}[kind]
                ffn(s2)

        @block.scalar
        def _(act):
            c = Counts()
            table = [None]
            n_stat = [0]

            def tables(name):
                if table[0] != name:
                    table[0] = name
                    act.preload_act_table_set(name)

            def root(width):
                tables("natural_log_exp_and_others")
                q = n_stat[0] % 2
                n_stat[0] += 1
                act.wait_ge(var_ready, c.up(var_ready))
                nc.scalar.activation(guess[:, q, 0:width], var[:, q, 0:width], ACT.Ln).then_inc(act_step, 1)
                act.wait_ge(act_step, c.up(act_step))
                nc.scalar.activation(guess[:, q, 0:width], guess[:, q, 0:width], ACT.Exp, scale=-0.5).then_inc(guess_ready, 1)

            def split(s, i=None, turn=0):
                at = s if i is None else i * TURN + s
                loads = 16 * (s // RAW + 1)
                act.wait_ge(slab_loaded[s % RAW], loads if i is None else i * (16 * TURN // RAW) + loads)
                if s >= HIGH:
                    act.wait_ge(slab_done, at + (1 - HIGH))
                nc.scalar.activation(high[:, s % HIGH, :], raw[:, s % RAW, :], ACT.Copy).then_inc(high_ready, 1)

            def ahead(s, n=1):
                for j in range(s + HIGH, s + n + HIGH):
                    if j < SLABS + SPARE:
                        split(j)

            def skip_stat():
                n_stat[0] += 1
                c.up(var_ready)

            def square(out, src):
                nc.scalar.activation(out, src, ACT.Square).then_inc(sq_ready, 1)

            def complete(gain, pairwise=False):
                pairs = c.now(x_ready)
                c.up(x_ready, 4)
                for j in range(4):
                    act.wait_ge(x_ready, pairs + j + 1 if pairwise else pairs + 4)
                    for k in (2 * j, 2 * j + 1):
                        nc.scalar.activation(xh[:, k, :], x[:, k, :], ACT.Identity, scale=par(gain, k)).then_inc(xh_ready, 1)
                square(x_squares, x[:, :, :])

            def sigmoid(out, src):
                tables("sigmoid_and_others")
                act.wait_ge(evac, c.up(evac))
                nc.scalar.activation(out, src, ACT.Sigmoid).then_inc(sig_ready, 1)

            def neighbourhood_bias(rows):
                for r in rows:
                    tt, rr = r // 2, r % 2
                    for key_row in range(4):
                        src = bass.AP(tensor=RPB.tensor, offset=(7 - r + key_row) * NA_RPB[1] + NA_WIN_C - GRID_W,
                                      ap=[[1, GRID_W], [NA_RPB[0] * NA_RPB[1], NA_HEADS], [1, GRID_W]])
                        act.dma_start(na_b[rr * GRID_W:(rr + 1) * GRID_W, :, tt, key_row, :], src).then_inc(bias_loaded, 16)

            def shifted_rows():
                act.wait_ge(toe_stored, 16)
                for tt in range(TT):
                    src = bass.AP(tensor=TOE_ROWS.tensor, offset=tt * P, ap=[[1, P], [2 * T, SWA_HEADS], [1, T]])
                    act.dma_start(toe[:, tt, :, :], src).then_inc(toe_loaded, 16)

            def ffn(s0, gain, bias_rows=(), toe_too=False):
                root(T)
                sigmoid(sg[:, :, :], gs[:, :, :])
                ahead(s0, 2)
                if toe_too:
                    shifted_rows()
                neighbourhood_bias(bias_rows[0:1])
                base = c.now(evac)
                with act.Fori(0, (FI - 1) // 2) as i:
                    for u in range(2):
                        act.wait_ge(evac, i * 4 + (base + 2 * u + 2))
                        nc.scalar.activation(sg[:, :, :], gs[:, :, :], ACT.Sigmoid).then_inc(sig_ready, 1)
                        for n in range(3):
                            split(s0 + 2 + 3 * u + n + HIGH, i)
                c.up(evac, 2 * FI - 1)
                neighbourhood_bias(bias_rows[1:2])
                if gain is not None:
                    complete(gain, pairwise=True)
                ahead(s0 + FFN_SLABS - 1)

            def attention(heads, scale, sink=None):
                tables("natural_log_exp_and_others")
                for i in range(heads + 3):
                    if 2 <= i < heads + 2:
                        act.wait_ge(t_done, c.up(t_done))
                        nc.scalar.activation(probsT[i % 2][:, :, :], acc[2 + i % 2][:, :, :], ACT.Copy).then_inc(pt_ready, 1)
                    if i < heads:
                        act.wait_ge(logits_ready, c.up(logits_ready))
                        st = small[:, i % 2, :]
                        src = acc[i % 2] if scale else logits[i % 2]
                        for tt in range(TT):
                            last = nc.scalar.activation(probs[i % 2][:, tt, :], src[:, tt, :], ACT.Exp, bias=st[:, tt:tt + 1],
                                                        scale=scale or 1.0, accum_out=st[:, 2 + tt:3 + tt])
                        if sink is not None and i < SWA_HEADS:
                            last = nc.scalar.activation(st[:, 4:6], st[:, 0:2], ACT.Exp, bias=sink(i))
                        last.then_inc(exp_done, 1)
                    if i >= 3:
                        act.wait_ge(pv_done, c.up(pv_done))
                        if i % 2 == 0:
                            pair = (i - 3) // 2
                            nc.scalar.activation(xh[:, pair, :], stat[pair % 2][:, 0, :], ACT.Copy).then_inc(ot_high, 1)

            def hg(s, gain):
                root(T)
                for j in range(8):
                    sigmoid(sg[:, :, :], gs[:, :, :])
                    ahead(s + j)
                c.up(evac, 4)
                skip_stat()
                c.up(evac, 4)
                ahead(s + 8, 6)

                def keys_of_level(n):
                    for g in range(2):
                        act.wait_ge(tree_ready, first + 2 * n + g + 1)
                        part = slice(g * HG_HEADS // 2, (g + 1) * HG_HEADS // 2)
                        out = hg_km[:, part, :].rearrange("p c (b two l) -> p (c b) two l", two=2, l=HALVES[n])
                        src = sides(hg_kg[:, part, :].rearrange("p c t -> p (c t)"), HALVES[n])
                        nc.scalar.activation(out, src, ACT.Copy).then_inc(keys_ready, 1)

                first = c.now(tree_ready)
                c.up(tree_ready, 2 * (len(HALVES) + 1))
                keys_of_level(1)
                ahead(s + 14, 2)
                keys_of_level(2)
                for j in range(4):
                    keys_of_level(3 + j)
                    sigmoid(sg[:, :, :], gs[:, :, :])
                    ahead(s + 16 + j)
                for b in range(4):
                    act.wait_ge(mix_done, c.up(mix_done))
                    square(hg_sq[:, 2 * b:2 * b + 2, :], acc[b][:, :, :])
                for b in range(4):
                    root(2 * T)
                c.up(evac, 4)
                ahead(s + 20, 3)
                complete(gain)
                ahead(s + 23)

            def head_square(j, src):
                act.wait_ge(evac, c.up(evac))
                square(squares[j % 2][:, :, :], src)

            def na(s, gain):
                root(T)
                for j in range(9):
                    if j < 8:
                        head_square(j, (na_q if j < 4 else na_k)[:, 2 * (j % 4):2 * (j % 4) + 2, :])
                        ahead(s + j)
                    if j == 8:
                        skip_stat()
                    if j >= 1:
                        root(2 * T)
                c.up(evac, 4)
                ahead(s + 8, 4)
                attention(NA_HEADS, None)
                c.up(evac, 4)
                ahead(s + 12, 3)
                complete(gain)
                ahead(s + 15)

            def mla(s, gain):
                root(T)
                ahead(s, 2)
                act.wait_ge(evac, c.up(evac, 3))
                square(ml_sq[:, 0:6, :], ml_cq)
                ahead(s + 2)
                act.wait_ge(evac, c.up(evac, 1))
                square(ml_sq[:, 6:8, :], ml_ckv)
                ahead(s + 3, 2)
                c.up(evac)
                root(T)
                root(T)
                ahead(s + 5, 2)
                act.wait_ge(evac, c.up(evac, 8))
                square(ml_sqn, ml_kn)
                square(ml_sqr[:, 0, :], ml_krr)
                c.up(evac)
                for j in range(4):
                    ahead(s + 7 + j)
                    root(2 * T)
                    root(T)
                act.wait_ge(stat_done, n_stat[0])
                act.wait_ge(evac, c.up(evac, 4))
                square(ml_sqn, ml_qn)
                ahead(s + 11, 2)
                act.wait_ge(evac, c.up(evac, 2))
                square(ml_sqr, ml_qr)
                c.up(evac, 2)
                for r in range(4):
                    root(2 * T)
                    root(T)
                attention(MLA_HEADS, (NOPE + ROPE) ** -0.5)
                c.up(evac, 4)
                ahead(s + 13, 3)
                complete(gain)
                ahead(s + 16)

            def branches(s, gain, l):
                act.wait_ge(toe_kept, 16)
                act.dma_start(toe, TOE).then_inc(toe_loaded, 16)
                root(T)
                for j in range(5):
                    if j < 4:
                        head_square(j, (br_q[:, 0:2, :], br_k[:, 0:2, :], br_q[:, 2:4, :], br_k[:, 2:4, :])[j])
                        ahead(s + j)
                    if j >= 1:
                        root(2 * T)
                ahead(s + 4, 3)
                act.wait_ge(aux_ready, c.up(aux_ready))
                nc.scalar.activation(br_l, br_cum, ACT.Exp, scale=-1.0).then_inc(act_step, 1)
                act.wait_ge(act_step, c.up(act_step))
                nc.scalar.activation(br_l, br_l, ACT.Ln, bias=con("ones", 0, 1, FOX_HEADS)).then_inc(log_ready, 1)
                c.up(evac, 1)
                skip_stat()
                c.up(evac, 2)
                sigmoid(sg[:, :, :], gs[:, :, :])
                ahead(s + 7, 5)
                c.up(evac, 4)
                for j in range(16):
                    sigmoid(br_g[:, 2 * j:2 * j + 2, :], (gs, hid)[j % 2][:, :, :])
                    ahead(s + 12 + j)
                    if j == 11:
                        skip_stat()
                        act.wait_ge(aux_ready, c.up(aux_ready))
                        square(br_sq, br_conv)
                    if j == 12:
                        root(T)
                act.wait_ge(aux_ready, c.up(aux_ready))
                nc.scalar.activation(sg[:, :, :], br_conv, ACT.Sigmoid).then_inc(sig_ready, 1)
                attention(SWA_HEADS + FOX_HEADS, None, lambda h: par(f"sink{l}", h))
                c.up(evac, 16 + 4)
                ahead(s + 28, 7)
                complete(gain)
                ahead(s + 35)


            for r in range(HIGH):
                split(r)
            act.wait_ge(inputs_loaded, 64)
            square(x_squares, x[:, :, :])
            act.wait_ge(toe_rows_done, 1)
            act.dma_start(TOE_ROWS, toe_rows).then_inc(toe_stored, 16)
            tables("natural_log_exp_and_others")
            act.wait_ge(lb_max, 1)
            nc.scalar.activation(lbt[:, 0:4 * HG_HEADS], lbt[:, 0:4 * HG_HEADS], ACT.Exp).then_inc(lb_exp, 1)
            for layer, kind in enumerate(MIXERS):
                s1, sm, s2 = STAGES[layer]
                ffn(s1, f"norm{layer}_1", (2, 3) if kind == "na" else (), layer == 0)
                if layer == 0:
                    act.wait_ge(toe_masked, TT)
                    act.dma_start(TOE, toe).then_inc(toe_kept, 16)
                gain = f"norm{layer}_2"
                if kind == "branches":
                    branches(sm, gain, layer - LAYERS_1)
                else:
                    {"hg": hg, "na": na, "mla": mla}[kind](sm, gain)
                ffn(s2, f"norm{layer + 1}_0" if layer + 1 < len(MIXERS) else None,
                    (0, 1) if MIXERS[layer + 1:layer + 2] == ["na"] else ())

        @block.vector
        def _(dve):
            c = Counts()
            n_prod = [0]
            n_stat = [0]
            v = nc.vector

            def link(ins):
                ins.then_inc(vec_step, 1)
                dve.wait_ge(vec_step, c.up(vec_step))

            def own(ins, signal):
                ins.then_inc(signal, 1)
                dve.wait_ge(signal, c.up(signal))

            def product(s=None):
                n = n_prod[0]
                n_prod[0] += 1
                if s is None:
                    dve.wait_ge(mid_done, c.up(mid_done))
                else:
                    dve.wait_ge(slab_done, s + 1)
                return prod[n % 2]

            def variance(width, n):
                q = n_stat[0] % 2
                n_stat[0] += 1
                dve.wait_ge(stat_done, c.up(stat_done))
                v.tensor_scalar(var[:, q, 0:width], stat[q][:, :, :].rearrange("p a t -> p (a t)")[:, 0:width],
                                1.0 / n, EPS, ALU.mult, ALU.add).then_inc(var_ready, 1)
                c.up(var_ready)
                return q

            def inverse_root(q, width, out=None, signal=None):
                dve.wait_ge(guess_ready, c.up(guess_ready))
                y, w, t = guess[:, q, 0:width], var[:, q, 0:width], newt[:, 0:width]
                out = y if out is None else out
                link(v.scalar_tensor_tensor(t, y, -0.5, y, ALU.mult, ALU.mult))
                link(v.tensor_tensor(t, t, w, ALU.mult))
                own(v.scalar_tensor_tensor(out, t, 1.5, y, ALU.add, ALU.mult), signal or vec_step)
                return out

            def next_norm(chunk, gain):
                link(v.tensor_scalar(xh[:, chunk, :], x[:, chunk, :], par(gain, chunk), None, ALU.mult))
                v.scalar_tensor_tensor(xl[:, chunk, :], x[:, chunk, :], par(gain, chunk), xh[:, chunk, :].bitcast(F32),
                                       ALU.mult, ALU.subtract).then_inc(xg_ready, 1)

            def split(src, at, n, signal):
                link(v.tensor_copy(xh[:, at:at + n, :], src))
                own(v.tensor_tensor(xl[:, at:at + n, :], src, xh[:, at:at + n, :].bitcast(F32), ALU.subtract), signal)

            def low_part(chunk, gain):
                dve.wait_ge(xh_ready, c.up(xh_ready))
                v.scalar_tensor_tensor(xl[:, chunk, :], x[:, chunk, :], par(gain, chunk), xh[:, chunk, :].bitcast(F32),
                                       ALU.mult, ALU.subtract).then_inc(xg_ready, 1)

            def token_norm():
                dve.wait_ge(sq_ready, c.up(sq_ready))
                v.tensor_reduce(sqsum, x_squares.rearrange("p c t -> p t c"), AX_X, ALU.add).then_inc(sum_ready, 1)
                q = variance(T, D)
                inverse_root(q, T, rstd[:, :], rstd_ready)

            def scaled(out, bank, factor=None):
                if factor is None:
                    own(v.tensor_tensor(out, bank, over(rstd[:, :], 2), ALU.mult), evac)
                else:
                    own(v.scalar_tensor_tensor(out, bank, factor, over(rstd[:, :], 2), ALU.mult, ALU.mult), evac)

            def columns():
                q = n_stat[0] % 2
                n_stat[0] += 1
                dve.wait_ge(stat_done, c.up(stat_done))
                own(v.tensor_copy(rstdT[:, :], stat[q][:, 0, 0:TT]), var_ready)

            def values(s, out, cols, at=0):
                for tt in range(TT):
                    b = product(s)
                    own(v.tensor_scalar(out[:, tt, at:at + cols], b[:, :, :].rearrange("p a t -> p (a t)")[:, 0:cols],
                                        rstdT[:, tt:tt + 1], None, ALU.mult), evac)

            def residual(s, gain):
                for j in range(4):
                    b = product(s + j)
                    pair = x[:, 2 * j:2 * j + 2, :]
                    own(v.tensor_tensor(pair, pair, b[:, :, :], ALU.add), evac)
                v.memset(small[:, 0, 0:1], 0.0).then_inc(x_ready, 4)
                c.up(x_ready, 4)
                for k in range(KC):
                    low_part(k, gain)

            def ffn(s0, gain):
                def gated():
                    v.tensor_tensor(sg[:, :, :], sg[:, :, :], gs[:, :, :], ALU.mult).then_inc(vec_step, 1)

                def scale_by_token():
                    v.tensor_tensor(sg[:, :, :], sg[:, :, :], over(rstd[:, :], 2), ALU.mult).then_inc(vec_step, 1)

                def split_hidden():
                    v.tensor_copy(hidh[:, :, :], hid[:, :, :]).then_inc(vec_step, 1)

                def split_rest():
                    v.tensor_tensor(hidl[:, :, :], hid[:, :, :], hidh[:, :, :].bitcast(F32), ALU.subtract).then_inc(hid_ready, 1)

                token_norm()
                scaled(gs[:, :, :], product(s0)[:, :, :])
                dve.wait_ge(sig_ready, c.up(sig_ready))
                gated()
                dve.wait_ge(vec_step, c.up(vec_step))
                scale_by_token()
                dve.wait_ge(vec_step, c.up(vec_step))
                own(v.tensor_tensor(hid[:, :, :], product(s0 + 1)[:, :, :], sg[:, :, :], ALU.mult), evac)
                split_hidden()
                dve.wait_ge(vec_step, c.up(vec_step))
                split_rest()
                e0, g0, t0 = c.now(evac), c.now(sig_ready), c.now(vec_step)
                with dve.Fori(0, (FI - 1) // 2) as i:
                    for u in range(2):
                        s = s0 + 2 + 3 * u
                        dve.wait_ge(slab_done, i * TURN + (s + 1))
                        v.tensor_tensor(gs[:, :, :], prod[0][:, :, :], over(rstd[:, :], 2), ALU.mult).then_inc(evac, 1)
                        dve.wait_ge(sig_ready, i * 2 + (g0 + u + 1))
                        gated()
                        dve.wait_ge(vec_step, i * 6 + (t0 + 3 * u + 1))
                        scale_by_token()
                        dve.wait_ge(vec_step, i * 6 + (t0 + 3 * u + 2))
                        dve.wait_ge(slab_done, i * TURN + (s + 3))
                        v.tensor_tensor(hid[:, :, :], prod[1][:, :, :], sg[:, :, :], ALU.mult).then_inc(evac, 1)
                        dve.wait_ge(evac, i * 4 + (e0 + 2 * u + 2))
                        split_hidden()
                        dve.wait_ge(vec_step, i * 6 + (t0 + 3 * u + 3))
                        split_rest()
                c.up(evac, 2 * (FI - 1))
                c.up(sig_ready, FI - 1)
                c.up(vec_step, 3 * (FI - 1))
                n_prod[0] += 2 * (FI - 1)
                dve.wait_ge(slab_done, s0 + FFN_SLABS)
                for j in range(4):
                    pair = x[:, 2 * j:2 * j + 2, :]
                    ins = v.scalar_tensor_tensor(pair, acc[j][:, :, :], 0.5, pair, ALU.mult, ALU.add)
                    if gain is None:
                        ins.then_inc(xg_ready, 1)
                    else:
                        own(ins, x_ready)
                        if j >= 1:
                            low_part(2 * j - 2, gain)
                            low_part(2 * j - 1, gain)
                if gain is not None:
                    low_part(KC - 2, gain)
                    low_part(KC - 1, gain)

            def attention(heads, scale, bias=None, sink=None, between=None):
                for i in range(heads + 1):
                    if i < heads:
                        st, mx = small[:, i % 2, :], small[:, 2 + i % 2, 0:2]
                        dve.wait_ge(s_done, c.up(s_done))
                        if bias is None:
                            link(v.tensor_reduce(mx, acc[i % 2][:, :, :], AX_X, ALU.max))
                            ins = v.tensor_scalar(st[:, 0:2], mx, -scale, None, ALU.mult)
                        else:
                            b = bias(i)
                            k = b.shape[-1]
                            link(v.scalar_tensor_tensor(logits[i % 2].rearrange("p a (r k) -> p (a r) k", k=k),
                                                        acc[i % 2][:, :, :].rearrange("p a (r k) -> p (a r) k", k=k),
                                                        scale, b, ALU.mult, ALU.add))
                            if sink is not None and i < SWA_HEADS:
                                link(v.tensor_reduce(mx, logits[i % 2], AX_X, ALU.max))
                                ins = v.tensor_scalar(st[:, 0:2], mx, sink(i), -1.0, ALU.max, ALU.mult)
                            else:
                                ins = v.tensor_reduce(st[:, 0:2], logits[i % 2], AX_X, ALU.max, negate=True)
                        ins.then_inc(logits_ready, 1)
                    if i >= 1:
                        h = i - 1
                        st = small[:, h % 2, :]
                        dve.wait_ge(exp_done, c.up(exp_done))
                        if sink is not None and h < SWA_HEADS:
                            link(v.tensor_tensor(st[:, 2:4], st[:, 2:4], st[:, 4:6], ALU.add))
                        link(v.reciprocal(st[:, 6:8], st[:, 2:4]))
                        for tt in range(TT):
                            last = v.tensor_scalar(probs[h % 2][:, tt, :], probs[h % 2][:, tt, :], st[:, 6 + tt:7 + tt],
                                                   None, ALU.mult)
                        last.then_inc(p_ready, 1)
                    if i >= 5 and i % 2:
                        low_out((i - 5) // 2)
                    if between:
                        between(i)
                low_out(heads // 2 - 2)
                low_out(heads // 2 - 1)

            def low_out(pair):
                dve.wait_ge(ot_high, c.up(ot_high))
                v.tensor_tensor(xl[:, pair, :], stat[pair % 2][:, 0, :], xh[:, pair, :].bitcast(F32), ALU.subtract).then_inc(ot_ready, 1)

            def head_norm(q, out, gain, width=2 * T):
                y = inverse_root(q, width)
                y = y.rearrange("p (a t) -> p a t", t=T) if width > T else y
                v.scalar_tensor_tensor(out, out, par(gain), y, ALU.mult, ALU.mult).then_inc(norm_ready, 1)
                c.up(norm_ready)

            def hg(s, which, gain):
                token_norm()
                for d in range(2):
                    for j in range(4):
                        scaled(gs[:, :, :], product(s + 4 * d + j)[:, :, :])
                        dve.wait_ge(sig_ready, c.up(sig_ready))
                        for i in range(2):
                            h = 2 * j + i
                            last = v.tensor_scalar(hg_f[d][:, h, :], sg[:, i, :], oml[:, which, h:h + 1], lbs[:, which, h:h + 1],
                                                   ALU.mult, ALU.add)
                        link(last)
                        link(v.tensor_scalar((hg_kg, hg_kx)[d][:, 2 * j:2 * j + 2, :], hg_f[d][:, 2 * j:2 * j + 2, :],
                                             -1.0, 1.0, ALU.mult, ALU.add))
                for j in range(4):
                    pair = slice(2 * j, 2 * j + 2)
                    scaled(hg_q[:, pair, :], product(s + 8 + j)[:, :, :], float(D // HG_HEADS) ** -0.5)
                    v.tensor_tensor(hg_ks[:, pair, :], hg_kg[:, pair, :], hg_kx[:, pair, :], ALU.add)
                    v.tensor_tensor(hg_qf[:, pair, :], hg_q[:, pair, :], hg_f[0][:, pair, :], ALU.mult)
                    last = v.tensor_tensor(hg_qy[:, pair, :], hg_q[:, pair, :], hg_f[1][:, pair, :], ALU.mult)
                    if j % 2:
                        own(last, tree_ready)
                columns()
                flat = [a.rearrange("p c t -> p (c t)") for a in (hg_qf, hg_qy, hg_kg, hg_kx)]
                total = [a.rearrange("p c t -> p (c t)") for a in hg_f]
                spare = region(8)
                for g in range(2):
                    dve.wait_ge(tree_done, c.up(tree_done))
                    for b in (2 * g, 2 * g + 1):
                        last = v.tensor_copy(hg_ad[:, 2 * b:2 * b + 2, :], acc[b][:, :, :])
                    own(last, tree_taken)
                for n, half in enumerate(HALVES):
                    if n in (0, 2):
                        values(s + 13 + 2 * (n // 2), hg_v, 2 * T, 2 * T * (n // 2))
                    elif n >= 3:
                        scaled(gs[:, :, :], product(s + 16 + n - 3)[:, :, :])
                    mask = levels[:, n, :].unsqueeze(1).to_broadcast([P, 4, P])
                    nb = KC * T // (2 * half)
                    pairs = [t[:, 0:2 * nb].rearrange("p (b two) -> p b two", two=2) for t in total]
                    if n % 2 == 0:
                        new = [spare[:, d * 1024:d * 1024 + nb] for d in range(2)]
                    else:
                        new = [hg_f[d].rearrange("p c t -> p (c t)")[:, 0:nb] for d in range(2)]
                    for g in range(2):
                        dve.wait_ge(tree_done, c.up(tree_done))
                        for b in (2 * g, 2 * g + 1):
                            last = v.copy_predicated(halves(hg_ad[:, 2 * b:2 * b + 2, :]), mask, halves(acc[b][:, :, :]))
                        own(last, tree_taken)
                        part = slice(g * nb // 2, (g + 1) * nb // 2)
                        for a, side, t in ((flat[0], 1, pairs[0]), (flat[1], 0, pairs[1]), (flat[2], 0, pairs[0]), (flat[3], 1, pairs[1])):
                            blocks = a.rearrange("p (b two l) -> p b two l", two=2, l=half)[:, part, side, :]
                            factor = t[:, part, 1 - side].unsqueeze(2).to_broadcast([P, nb // 2, half])
                            last = v.tensor_tensor(blocks, blocks, factor, ALU.mult)
                        own(last, tree_ready)
                        if half < HALVES[-1]:
                            for d in range(2):
                                last = v.tensor_tensor(new[d][:, part], pairs[d][:, part, 0], pairs[d][:, part, 1], ALU.mult)
                            link(last)
                    total = new
                    if n >= 3:
                        dve.wait_ge(sig_ready, c.up(sig_ready))
                        link(v.tensor_tensor(hg_sg[:, 2 * (n - 3):2 * (n - 3) + 2, :], gs[:, :, :], sg[:, :, :], ALU.mult))
                for g in range(2):
                    dve.wait_ge(tree_done, c.up(tree_done))
                    for b in (2 * g, 2 * g + 1):
                        last = v.tensor_copy(hg_ao[:, 2 * b:2 * b + 2, :], acc[b][:, :, :])
                    own(last, tree_taken)
                for b in range(4):
                    dve.wait_ge(sq_ready, c.up(sq_ready))
                    last = v.scalar_tensor_tensor(hg_o[:, 2 * b:2 * b + 2, :], acc[b][:, :, :], par(f"hg_g{HG_LAYERS[which]}"),
                                                  hg_sg[:, 2 * b:2 * b + 2, :], ALU.mult, ALU.mult)
                link(last)
                qs = {}
                for b in range(5):
                    if b < 4:
                        qs[b] = variance(2 * T, P)
                    if b >= 1:
                        a = b - 1
                        y = inverse_root(qs[a], 2 * T).rearrange("p (a t) -> p a t", a=2)
                        pair = slice(2 * a, 2 * a + 2)
                        link(v.tensor_tensor(hg_o[:, pair, :], hg_o[:, pair, :], y, ALU.mult))
                        link(v.tensor_copy(xh[:, pair, :], hg_o[:, pair, :]))
                        v.tensor_tensor(xl[:, pair, :], hg_o[:, pair, :], xh[:, pair, :].bitcast(F32), ALU.subtract).then_inc(mix_ready, 2)
                        c.up(mix_ready, 2)
                residual(s + 20, gain)

            def na(s, gain):
                token_norm()
                q = 0
                for j in range(9):
                    pair = (na_q if j < 4 else na_k)[:, 2 * (j % 4):2 * (j % 4) + 2, :]
                    if j < 8:
                        scaled(pair, product(s + j)[:, :, :])
                        if j == 0:
                            dve.wait_ge(bias_loaded, 16 * 16)
                        for h in (2 * j, 2 * j + 1):
                            b = na_b[:, h].rearrange("p a r k -> p (a r) k")
                            link(v.tensor_tensor(b, b, over(con("namask"), 4 * TT), ALU.add))
                    if j == 8:
                        columns()
                        values(s + 9, na_v, 2 * T, 0)
                    if j >= 1:
                        q = variance(2 * T, NA_DIM)
                        before = (na_q if j - 1 < 4 else na_k)[:, 2 * ((j - 1) % 4):2 * ((j - 1) % 4) + 2, :]
                        head_norm(q, before, "na_q" if j - 1 < 4 else "na_k")
                c.up(sq_ready, 8)
                values(s + 11, na_v, 2 * T, 2 * T)
                attention(NA_HEADS, NA_DIM ** -0.5, lambda h: backwards(na_b[:, h].rearrange("p a r k -> p (a r) k")))
                residual(s + 12, gain)

            def mla(s, gain):
                token_norm()
                for j in range(4):
                    scaled(act3(0)[:, 2 * j:2 * j + 2, :], product(s + j)[:, :, :])
                own(v.tensor_tensor(ml_krr, product(s + 4)[:, 0, :], rstd[:, :], ALU.mult), evac)
                own(v.tensor_scalar(ml_kr[:, 0, :], ml_krr, par("mla_kr"), None, ALU.mult), mix_ready)
                y = inverse_root(variance(T, MLA_KV), T)
                for k in range(MLA_KV // P):
                    last = v.scalar_tensor_tensor(ml_ckv[:, k, :], ml_ckv[:, k, :], par("mla_kva", k), y, ALU.mult, ALU.mult)
                link(last)
                split(ml_ckv, MLA_Q // P, MLA_KV // P, norm_ready)
                y = inverse_root(variance(T, MLA_Q), T)
                def latent(*ks):
                    for k in ks:
                        last = v.scalar_tensor_tensor(ml_cq[:, k, :], ml_cq[:, k, :], par("mla_qa", k), y, ALU.mult, ALU.mult)
                    link(last)

                for m in range(4):
                    own(v.tensor_copy(ml_kn[:, 2 * m:2 * m + 2, :], product()[:, :, :]), evac)
                    if m < 3:
                        latent(2 * m, 2 * m + 1)
                    else:
                        link(v.tensor_copy(xh[:, 0:MLA_Q // P, :], ml_cq))
                    own(v.tensor_copy(ml_v[:, :, m * T:(m + 1) * T], product(None if m % 2 == 0 else s + 5 + m // 2)[:, :, :]), evac)
                own(v.tensor_tensor(xl[:, 0:MLA_Q // P, :], ml_cq, xh[:, 0:MLA_Q // P, :].bitcast(F32), ALU.subtract), norm_ready)

                def rotation(src, dst, n):
                    dve.wait_ge(rot_done, c.up(rot_done))
                    b = prod[n_prod[0] % 2]
                    n_prod[0] += 1
                    own(v.tensor_tensor(gs[:, 0:n, :], b[:, 0:n, :], over(con("sin"), n), ALU.mult), evac)
                    link(v.tensor_tensor(sg[:, 0:n, :], src, over(con("cos"), n), ALU.mult))
                    link(v.tensor_tensor(dst, gs[:, 0:n, :], sg[:, 0:n, :], ALU.add))

                def lengths(keys, r):
                    qs = (variance(2 * T, NOPE + ROPE), variance(T, NOPE + ROPE))
                    y = inverse_root(qs[0], 2 * T)
                    out = (ml_kn if keys else ml_qn)[:, 2 * r:2 * r + 2, :]
                    link(v.scalar_tensor_tensor(out, out, par("mla_kn" if keys else "mla_qn"),
                                                y.rearrange("p (a t) -> p a t", a=2), ALU.mult, ALU.mult))
                    y = inverse_root(qs[1], T)
                    out = (ml_kr if keys else ml_qr)[:, r, :]
                    return v.tensor_tensor(out, ml_krot if keys else out, y, ALU.mult)

                rotation(ml_kr[:, 0:1, :], act3(4)[:, 5:6, :], 1)
                for j in range(4):
                    own(v.tensor_copy(ml_qn[:, 2 * j:2 * j + 2, :], product(s + 7 + j)[:, :, :]), evac)
                    link(lengths(True, j))
                for j in range(2):
                    own(v.tensor_copy(ml_qr[:, 2 * j:2 * j + 2, :], product(s + 11 + j)[:, :, :]), evac)
                dve.wait_ge(sq_ready, c.up(sq_ready, 6))
                for j in range(2):
                    v.tensor_scalar(ml_qr[:, 2 * j:2 * j + 2, :], ml_qr[:, 2 * j:2 * j + 2, :], par("mla_qr"), None, ALU.mult).then_inc(mix_ready, 1)
                dve.wait_ge(mix_ready, c.up(mix_ready, 2))
                for j in range(2):
                    rotation(ml_qr[:, 2 * j:2 * j + 2, :], ml_qr[:, 2 * j:2 * j + 2, :], 2)
                for r in range(4):
                    last = lengths(False, r)
                    own(last, norm_ready if r == 3 else vec_step)
                attention(MLA_HEADS, (NOPE + ROPE) ** -0.5)
                residual(s + 13, gain)

            def branches(s, l, gain):
                token_norm()
                pads = (br_u[:, :, 0:UPAD], br_t[:, :, 0:SPAD])
                for pad in pads:
                    v.memset(pad, 0.0).then_inc(vec_step, 1)
                    c.up(vec_step)
                pairs = [(br_q[:, 0:2, :], f"swq{l}"), (br_k[:, 0:2, :], f"swk{l}"), (br_q[:, 2:4, :], f"fxq{l}"), (br_k[:, 2:4, :], f"fxk{l}")]
                for j in range(5):
                    if j < 4:
                        scaled(pairs[j][0], product(s + j)[:, :, :])
                    else:
                        own(v.tensor_tensor(br_x, product(s + 4)[0:FOX_HEADS, 0, :], rstd[0:FOX_HEADS, :], ALU.mult), evac)
                    if j >= 1:
                        q = variance(2 * T, 64)
                        head_norm(q, *pairs[j - 1])
                c.up(sq_ready, 4)
                columns()
                values(s + 6, br_v, 3 * P)
                link(v.tensor_scalar(br_x, br_x, par(f"bf{l}", 0, 1, FOX_HEADS), None, ALU.add))
                link(v.tensor_scalar(br_ncum, br_x, -1.0, None, ALU.mult))
                own(v.tensor_tensor(br_cum, br_x, br_ncum, ALU.max), aux_ready)
                dve.wait_ge(log_ready, c.up(log_ready))
                link(v.scalar_tensor_tensor(br_x, br_x, 0.0, br_l, ALU.min, ALU.subtract))
                link(v.tensor_tensor_scan(br_l, con("ones", 0, 1, FOX_HEADS).to_broadcast([FOX_HEADS, T]), br_x, 0.0, ALU.mult, ALU.add))
                v.tensor_scalar(br_cum, br_l, 8.0, None, ALU.mult).then_inc(vec_step, 1)
                c.up(vec_step)
                own(v.tensor_scalar(br_ncum, br_l, -8.0, None, ALU.mult), norm_ready)
                scaled(gs[:, :, :], product(s + 7)[:, :, :])
                dve.wait_ge(sig_ready, c.up(sig_ready))
                link(v.tensor_tensor(sg[:, :, :], sg[:, :, :], over(rstd[:, :], 2), ALU.mult))
                own(v.tensor_tensor(br_u[:, :, UPAD:UPAD + T], product(s + 8)[:, :, :], sg[:, :, :], ALU.mult), evac)
                scaled(hid[:, :, :], product(s + 9)[:, :, :])
                link(v.tensor_tensor(hid[:, :, :], hid[:, :, :], over(rstd[:, :], 2), ALU.mult))
                own(v.tensor_tensor(br_t[:, :, SPAD:SPAD + T], product(s + 10)[:, :, :], hid[:, :, :], ALU.mult), evac)
                scaled(br_sb, product(s + 11)[:, :, :])

                sigmoids = c.now(sig_ready)
                c.up(sig_ready, 16)

                def gate(j):
                    if j >= 2:
                        dve.wait_ge(sig_ready, sigmoids + j - 1)
                    scaled((gs, hid)[j % 2][:, :, :], product(s + 12 + j)[:, :, :])

                def tap(out, src, w, k, first_bias=None):
                    for i in range(2):
                        shifted = src[:, i, k:k + T]
                        weight = w(i, k)
                        if k == 0:
                            last = v.tensor_scalar(out[:, i, :], shifted, weight, first_bias(i) if first_bias else 0.0,
                                                   ALU.mult, ALU.add)
                        else:
                            last = v.scalar_tensor_tensor(out[:, i, :], shifted, weight, out[:, i, :], ALU.mult, ALU.add)
                    link(last)

                for j in range(11):
                    gate(j)
                    for k in range(4 * j, min(4 * j + 4, CONV_K)):
                        tap(br_conv, br_u, lambda i, k: par(f"dw{l}", i * CONV_K + k), k, lambda i: par(f"dwb{l}", i))
                    if 8 <= j < 8 + SC_K:
                        tap(br_sc, br_t, lambda i, k: par(f"sc{l}", i * SC_K + k), j - 8)
                own(v.tensor_tensor(br_sc, br_sc, br_sb, ALU.mult), mix_ready)
                gate(11)
                q = n_stat[0] % 2
                n_stat[0] += 1
                dve.wait_ge(stat_done, c.up(stat_done))
                for i in range(2):
                    last = v.scalar_tensor_tensor(br_conv[:, i, :], stat[q][:, 0, :], -1.0 / (2 * P), br_conv[:, i, :], ALU.mult, ALU.add)
                    if i == 0:
                        link(last)
                own(last, var_ready)
                own(v.memset(small[:, 0, 0:1], 0.0), aux_ready)
                gate(12)
                q = variance(T, 2 * P)
                dve.wait_ge(sig_ready, sigmoids + 12)
                y = inverse_root(q, T)
                c.up(sq_ready)
                gate(13)
                link(v.tensor_tensor(br_conv, br_conv, over(y, 2), ALU.mult))
                for i in range(2):
                    last = v.tensor_scalar(br_conv[:, i, :], br_conv[:, i, :], par(f"lng{l}", i), par(f"lnb{l}", i), ALU.mult, ALU.add)
                own(last, aux_ready)
                gate(14)
                gate(15)

                def operands(i):
                    if i == 2:
                        split(br_sc, 4, 2, mix_ready)
                    if i == 3:
                        dve.wait_ge(sig_ready, c.up(sig_ready))
                        link(v.tensor_tensor(br_conv, br_conv, sg[:, :, :], ALU.mult))
                    if i == 4:
                        split(br_conv, 6, 2, mix_ready)

                dve.wait_ge(toe_loaded, 16 * (TT + 1 + l))
                attention(SWA_HEADS + FOX_HEADS, 64 ** -0.5,
                          lambda h: backwards(toe[:, :, h, :]) if h < SWA_HEADS else con("fxmask").rearrange("p (a t) -> p a t", a=TT),
                          lambda h: par(f"sink{l}", h), operands)
                for br in range(4):
                    for j in range(4):
                        b = product(None if j < 3 else s + 28 + br)
                        g = br_g[:, 8 * br + 2 * j:8 * br + 2 * j + 2, :]
                        pair = br_m[:, 2 * j:2 * j + 2, :]
                        if br == 0:
                            own(v.tensor_tensor(pair, b[:, :, :], g, ALU.mult), evac)
                        else:
                            own(v.tensor_tensor(gs[:, :, :], b[:, :, :], g, ALU.mult), evac)
                            link(v.tensor_tensor(pair, pair, gs[:, :, :], ALU.add))
                for k in range(KC):
                    split(br_m[:, k:k + 1, :], k, 1, mix_ready)
                residual(s + 32, gain)

            own(v.memset(zero16[:, :], 0.0), zeros_ready)
            dve.wait_ge(inputs_loaded, 64)
            dve.wait_ge(toe_row, 1)
            v.tensor_copy(toe_rows, acc[0][0:SWA_HEADS, :, :].rearrange("p a t -> p (a t)")).then_inc(toe_rows_done, 1)
            for k in range(KC):
                next_norm(k, "norm0_0")
            link(v.tensor_copy(levels.rearrange("p n t -> p (n t)"), start_const[:, LEVELS:N_START]))
            n = HG_HEADS
            logit = par("hg_lb", 0, 4 * n)
            top = lbt[:, 4 * n:5 * n]
            link(v.tensor_reduce(top, logit.rearrange("p (l h) -> p h l", l=LAYERS_1), AX_X, ALU.max))
            own(v.tensor_tensor(lbt[:, 0:4 * n].rearrange("p (l h) -> p l h", l=LAYERS_1), logit.rearrange("p (l h) -> p l h", l=LAYERS_1),
                                over(top, LAYERS_1), ALU.subtract), lb_max)
            dve.wait_ge(lb_exp, 1)
            rest, whole = lbt[:, 4 * n:5 * n], lbt[:, 5 * n:6 * n]
            link(v.tensor_tensor(rest, lbt[:, n:2 * n], lbt[:, 2 * n:3 * n], ALU.add))
            link(v.tensor_tensor(rest, rest, lbt[:, 3 * n:4 * n], ALU.add))
            link(v.tensor_tensor(whole, rest, lbt[:, 0:n], ALU.add))
            link(v.reciprocal(whole, whole))
            link(v.tensor_tensor(lbs[:, 1, :], rest, whole, ALU.mult))
            link(v.memset(lbs[:, 0, :], 0.0))
            link(v.tensor_scalar(oml[:, :, :], lbs[:, :, :], -1.0, 1.0, ALU.mult, ALU.add))

            for layer, kind in enumerate(MIXERS):
                s1, sm, s2 = STAGES[layer]
                ffn(s1, f"norm{layer}_1")
                gain = f"norm{layer}_2"
                if layer == 0:
                    dve.wait_ge(toe_kept, 16)
                if kind == "hg":
                    hg(sm, HG_LAYERS.index(layer), gain)
                elif kind == "na":
                    na(sm, gain)
                elif kind == "mla":
                    mla(sm, gain)
                else:
                    branches(sm, layer - LAYERS_1, gain)
                ffn(s2, f"norm{layer + 1}_0" if layer + 1 < len(MIXERS) else None)

        @block.gpsimd
        def _(pool):
            def split(s, i=None):
                at = s if i is None else i * TURN + s
                pool.wait_ge(high_ready, at + 1)
                if s >= LOW:
                    pool.wait_ge(slab_done, at + (1 - LOW))
                nc.gpsimd.tensor_tensor(low[:, s % LOW, :], raw[:, s % RAW, :], high[:, s % HIGH, :].bitcast(F32),
                                        ALU.subtract).then_inc(low_ready, 1)

            def split_many(first, turns):
                with pool.Fori(0, turns) as i:
                    for s in range(first, first + TURN):
                        split(s, i)

            early = 4
            for s in range(TURN):
                split(s)
            split_many(TURN, early)
            pool.wait_ge(inputs_loaded, 64)
            pool.wait_ge(toe_loaded, 16 * TT)
            for tt in range(TT):
                nc.gpsimd.tensor_tensor(toe[:, tt, :, :], toe[:, tt, :, :],
                                        over(start_const[:, SWMASK + tt * T:SWMASK + (tt + 1) * T], SWA_HEADS),
                                        ALU.add).then_inc(toe_masked, 1)
            at = TURN * (early + 1)
            turns = (SLABS - at) // TURN
            split_many(at, turns)
            for s in range(at + TURN * turns, SLABS):
                split(s)


def tiles(w, k_chunks, width=P):
    K, N = w.shape
    return w.reshape(k_chunks, P, N // width, width).transpose(2, 0, 1, 3)


def fill(stream, s, blocks):
    at = 0
    for b in blocks:
        stream[s, :, at:at + b.shape[1]] = b
        at += b.shape[1]


def features(stream, s, w, k_chunks=KC, per_slab=2):
    t = tiles(w, k_chunks)
    for j in range(0, t.shape[0], per_slab):
        fill(stream, s + j // per_slab, [t[n, k] for n in range(j, j + per_slab) for k in range(k_chunks)])


def token_major(stream, s, w, k_per_slab):
    rows = w.reshape(-1, P, w.shape[1])
    for j in range(0, len(rows), k_per_slab):
        fill(stream, s + j // k_per_slab, list(rows[j:j + k_per_slab]))


def ffn_slabs(stream, s, w_gate, w_up, w_down):
    n = 2 * P
    order = [("g", 0), ("u", 0)]
    for f in range(1, FI):
        order += [("g", f), ("d", f - 1), ("u", f)]
    order += [("d", FI - 1)]
    for i, (kind, f) in enumerate(order):
        if kind == "d":
            t = tiles(w_down[f * n:(f + 1) * n], 2)
            fill(stream, s + i, [t[c, k] for c in range(KC) for k in range(2)])
        else:
            features(stream, s + i, (w_gate if kind == "g" else w_up)[:, f * n:(f + 1) * n])


def constants():
    c = np.zeros((P, N_CONSTS), np.float32)
    start = np.zeros((P, N_START), np.float32)

    def put(name, a):
        at, w = CONSTS[name]
        c[:a.shape[0], at:at + a.shape[1]] = a

    i = np.arange(P)
    t = np.arange(T)
    put("ident", np.eye(P))
    put("ones", np.ones((P, P)))
    put("blk64", (i[:, None] // 64 == i[None] // 64) * 1.0)
    put("blk32", (i[:, None] // 32 == i[None] // 32) * 1.0)
    put("r2n", np.concatenate([(i[:, None] // 32 == 2 * a + i[None] // 64) * 1.0 for a in range(2)], 1))
    put("n2r", np.concatenate([(2 * a + i[:, None] // 64 == i[None] // 32) * 1.0 for a in range(2)], 1))
    half = ROPE // 2
    rot = np.zeros((P, P))
    for o in range(P):
        if o % ROPE < half:
            rot[o + half, o] = -1.0
        else:
            rot[o - half, o] = 1.0
    put("rot", rot)
    freq = np.float32(10000.0) ** (-np.arange(half, dtype=np.float32) / np.float32(half))
    ang = t.astype(np.float32)[None] * freq.astype(np.float32)[:, None]
    put("cos", np.tile(np.cos(ang.astype(np.float32)), (P // half, 1)))
    put("sin", np.tile(np.sin(ang.astype(np.float32)), (P // half, 1)))
    cols = np.arange(GRID_W)
    first = np.clip(cols - NA_WIN_C // 2, 0, GRID_W - NA_WIN_C)
    inside = (cols[None] >= first[:, None]) & (cols[None] < first[:, None] + NA_WIN_C)
    put("namask", np.tile(np.where(inside, 0.0, NEG), (2, 1))[:, ::-1])
    dist = t[:, None] - t[None]
    for name, ok in (("swmask", (dist >= 0) & (dist < P)), ("fxmask", dist >= 0)):
        m = np.where(ok, 0.0, NEG)
        m = m[:, ::-1] if name == "swmask" else m
        m = m.reshape(TT, P, T).transpose(1, 0, 2).reshape(P, TT * T)
        if name == "swmask":
            start[:, SWMASK:SWMASK + TT * T] = m
        else:
            put(name, m)
    exact = BUCKETS // 2
    d = np.arange(T)
    large = exact + (np.log(np.maximum(d, 1).astype(np.float32) / exact) / np.log(MAX_DISTANCE / exact)
                     * (BUCKETS - exact)).astype(np.int32)
    bucket = np.where(d < exact, d, np.minimum(large, BUCKETS - 1))
    hot = np.zeros((BUCKETS, 2 * T))
    for dd in range(P):
        hot[bucket[dd], T - 1 + dd] = 1.0
    start[:BUCKETS, HOT:HOT + 2 * T] = hot
    put("select", np.eye(FOX_HEADS))
    for n, h in enumerate(HALVES):
        start[:, LEVELS + n * P:LEVELS + (n + 1) * P] = ((i[:, None] // (2 * h) == i[None] // (2 * h))
                                                         & (i[:, None] // h % 2 != i[None] // h % 2))
    return c, start


def layout(z):
    stream = np.zeros((SLABS + SPARE, P, SLAB), np.float32)
    prm = np.zeros((P, N_PARAMS), np.float32)

    def put(name, a):
        at, w = PARAMS[name]
        prm[:a.shape[0], at:at + a.shape[1]] = a

    def by_chunk(a):
        return a.reshape(-1, P).T

    def twice(a):
        return np.concatenate([a, a])[:, None]

    for layer, (s1, sm, s2) in enumerate(STAGES):
        l2 = layer - LAYERS_1
        if l2 < 0:
            for i, name in enumerate(("ffn1_norm", "mix_norm", "ffn2_norm")):
                put(f"norm{layer}_{i}", by_chunk(z[name][layer]))
            for s, n in ((s1, "ffn1"), (s2, "ffn2")):
                gu = z[f"{n}_w_gu"][layer]
                ffn_slabs(stream, s, gu[:, :F], gu[:, F:], z[f"{n}_w_down"][layer])
        else:
            for i, name in enumerate(("ffn1_norm_2", "mix_norm_2", "ffn2_norm_2")):
                put(f"norm{layer}_{i}", by_chunk(z[name][l2]))
            for s, n in ((s1, "ffn1"), (s2, "ffn2")):
                ffn_slabs(stream, s, z[f"{n}_w_gate_2"][l2], z[f"{n}_w_up_2"][l2], z[f"{n}_w_down_2"][l2])
        kind = MIXERS[layer]
        if kind == "hg":
            a = HG_LAYERS.index(layer)
            q, zf, zb, i, g = np.split(z["hg_w_in"][a], 5, axis=1)
            for n, w in enumerate((zf, zb, q)):
                features(stream, sm + 4 * n, w)
            for n in range(2):
                token_major(stream, sm + 12 + 2 * n, i[:, n * 512:(n + 1) * 512], 4)
            features(stream, sm + 16, g)
            features(stream, sm + 20, z["hg_w_out"][a])
            put(f"hg_g{layer}", z["hg_g_norm"][a][:, None])
        elif kind == "na":
            q, k, v = np.split(z["na_w_in"][0], 3, axis=1)
            features(stream, sm, q)
            features(stream, sm + 4, k)
            for n in range(2):
                token_major(stream, sm + 8 + 2 * n, v[:, n * 512:(n + 1) * 512], 4)
            features(stream, sm + 12, z["na_w_out"][0])
        elif kind == "mla":
            w = z["mla_w_in"][0]
            features(stream, sm, w[:, :D])
            features(stream, sm + 4, np.tile(w[:, D:], (1, P // ROPE)), per_slab=1)
            uq = z["mla_w_uq"][0].reshape(MLA_Q, MLA_HEADS, NOPE + ROPE)
            features(stream, sm + 7, uq[:, :, :NOPE].reshape(MLA_Q, -1), MLA_Q // P)
            features(stream, sm + 11, uq[:, :, NOPE:].reshape(MLA_Q, -1), MLA_Q // P)
            ukv = z["mla_w_ukv"][0].reshape(MLA_KV, MLA_HEADS, NOPE + 64)
            kn, vv = tiles(ukv[:, :, :NOPE].reshape(MLA_KV, -1), 2), ukv[:, :, NOPE:].reshape(2, P, -1)
            for j in range(2):
                blocks = []
                for m in (2 * j, 2 * j + 1):
                    blocks += [kn[n, k] for n in (2 * m, 2 * m + 1) for k in range(2)]
                    blocks += [vv[k][:, m * T:(m + 1) * T] for k in range(2)]
                fill(stream, sm + 5 + j, blocks)
            features(stream, sm + 13, z["mla_w_out"][0])
        else:
            w = z["w_in_2"][l2]
            cuts = np.cumsum([256, 256, 256, 256, 256, 256, 128, 128, 256, 256, 256, 4])
            c_a, c_b, s_b, s_c, s_x, a_q, a_k, a_v, f_q, f_k, f_v, f_f, gates = np.split(w, cuts, axis=1)
            kk = a_k.reshape(D, 2, 1, 64)
            features(stream, sm, a_q)
            features(stream, sm + 1, np.concatenate([kk, kk], axis=2).reshape(D, 256))
            features(stream, sm + 2, f_q)
            features(stream, sm + 3, f_k)
            features(stream, sm + 4, np.concatenate([f_f, np.zeros((D, P - FOX_HEADS), np.float32)], axis=1), per_slab=1)
            token_major(stream, sm + 5, np.concatenate([a_v, f_v], axis=1), 5)
            for n, a in enumerate((c_b, c_a, s_c, s_x, s_b)):
                features(stream, sm + 7 + n, a)
            g = np.split(gates, 4, axis=1)
            for n, b in enumerate((2, 3, 1, 0)):
                features(stream, sm + 12 + 4 * n, g[b])
            for n, name in enumerate(("swa_w_o_2", "fox_w_o_2", "sc_w_out_2", "conf_w_out_2")):
                features(stream, sm + 28 + n, z[name][l2], 2, 8)
            features(stream, sm + 32, z["w_out_2"][l2])
            put(f"dw{l2}", z["conf_dw_2"][l2].reshape(CONV_K, 2, P).transpose(2, 1, 0).reshape(P, -1))
            put(f"sc{l2}", z["sc_conv_2"][l2].reshape(SC_K, 2, P).transpose(2, 1, 0).reshape(P, -1))
            for n, name in (("dwb", "conf_dw_b_2"), ("lng", "conf_ln_g_2"), ("lnb", "conf_ln_b_2")):
                put(f"{n}{l2}", by_chunk(z[name][l2]))
            for n, name in (("swq", "swa_q_norm_2"), ("swk", "swa_k_norm_2"), ("fxq", "fox_q_norm_2"), ("fxk", "fox_k_norm_2")):
                put(f"{n}{l2}", twice(z[name][l2]))
            put(f"bf{l2}", z["b_forget_2"][l2][:, None])
            put(f"sink{l2}", np.tile(z["swa_sink_2"][l2][None], (P, 1)))
    put("hg_lb", by_chunk(z["hg_lb_logits"]))
    put("na_q", twice(z["na_q_norm"][0]))
    put("na_k", twice(z["na_k_norm"][0]))
    put("mla_qa", by_chunk(z["mla_q_a_norm"][0]))
    put("mla_kva", by_chunk(z["mla_kv_a_norm"][0]))
    for n in "qk":
        g = z[f"mla_{n}_norm"][0]
        put(f"mla_{n}n", twice(g[:NOPE]))
        put(f"mla_{n}r", np.tile(g[NOPE:], 4)[:, None])
    put("relb", z["rel_bias_2"])
    return stream, prm


def kernel(**inputs):
    import concourse.bacc as bacc
    from concourse.bass_utils import run_bass_kernel_spmd

    z = {k: np.asarray(a) for k, a in inputs.items()}
    stream, prm = layout(z)
    consts, start = constants()
    arrays = {
        "stream": stream,
        "params": prm,
        "consts": consts,
        "start": start,
        "rpb": np.ascontiguousarray(z["na_rpb"][..., ::-1]).reshape(-1),
        "x_in": np.ascontiguousarray(z["x"][0].T.reshape(KC, P, T).transpose(1, 0, 2)),
    }
    nc = bacc.Bacc("TRN2", target_bir_lowering=False, num_devices=1)
    args = [nc.dram_tensor(k, a.shape, mybir.dt.from_np(a.dtype), kind="ExternalInput").ap() for k, a in arrays.items()]
    out = nc.dram_tensor("x_out", (P, KC, T), F32, kind="ExternalOutput").ap()
    by_distance = nc.dram_tensor("bias_by_distance", (SWA_HEADS, 2 * T), F32, kind="Internal").ap()
    shifted = nc.dram_tensor("bias_shifted", (P, TT, SWA_HEADS, T), F32, kind="Internal").ap()
    build(nc, *args, out, by_distance, shifted)
    r = run_bass_kernel_spmd(nc, [arrays], core_ids=[0])
    y = r.results[0]["x_out"]
    return np.ascontiguousarray(y.transpose(1, 0, 2).reshape(D, T).T)[None]
```
